# Optimizing a Trainium2 kernel written in Bass

```python
import math
import jax, jax.numpy as jnp
from jax import lax
import numpy as np
import jax
import jax.numpy as jnp

D_MODEL = 1024
BATCH = 1
SEQ = 256
DEPTH = 2

N_A_LAYERS = DEPTH // 2
N_B_LAYERS = DEPTH - N_A_LAYERS
N_DENSE = (DEPTH + 1) // 2
N_MOE = DEPTH // 2

HEAD_DIM = 64
N_HEADS = D_MODEL // HEAD_DIM
LORA_DECAY = 64
LORA_ICLR = 64
LORA_VRES = 32
LORA_GATE = 160
GN_EPS = 64e-5
LN_EPS = 1e-5

MOBA_BLOCK = 256
MOBA_TOPK = 3
QUERY_CHUNK = 64

D_FF = 2816
N_EXPERTS = 8
TOP_K_EXPERTS = 2
D_FF_EXPERT = 3584

DEEPNORM_ALPHA = (2.0 * DEPTH) ** 0.25
DEEPNORM_BETA = (8.0 * DEPTH) ** -0.25


def _heads(t):
    return t.reshape(t.shape[0], t.shape[1], N_HEADS, HEAD_DIM)

def layer_norm(x, g, b):
    xf = x.astype(jnp.float32)
    mu = jnp.mean(xf, axis=-1, keepdims=True)
    var = jnp.mean(jnp.square(xf - mu), axis=-1, keepdims=True)
    y = (xf - mu) * lax.rsqrt(var + LN_EPS)
    return (y * g + b).astype(x.dtype)

def deepnorm_residual(x, sub, g, b):
    return layer_norm(DEEPNORM_ALPHA * x + sub, g, b)

def wkv7_scan(r, decay, k, v, a, b):
    bsz, T, H, N = r.shape
    xs = tuple(jnp.moveaxis(t.astype(jnp.float32), 1, 0) for t in (r, decay, k, v, a, b))

    def step(S, inp):
        r_t, w_t, k_t, v_t, a_t, b_t = inp
        sa = jnp.einsum('bhvk,bhk->bhv', S, a_t)
        S = (S * w_t[:, :, None, :] + sa[..., None] * b_t[:, :, None, :]
             + v_t[..., None] * k_t[:, :, None, :])
        return S, jnp.einsum('bhvk,bhk->bhv', S, r_t)

    S0 = jnp.zeros((bsz, H, N, N), jnp.float32)
    _, y = lax.scan(step, S0, xs)
    return jnp.moveaxis(y, 0, 1)

def rwkv7_time_mix(x, v_first, mu, w_rkv, w_out, decay_w0, decay_w1, decay_w2,
                   iclr_a0, iclr_a1, iclr_a2, vres_v0, vres_v1, vres_v2,
                   gate_g1, gate_g2, k_k, k_a, r_k, gn_g, gn_b):
    bsz, T, D = x.shape
    x_prev = jnp.pad(x[:, :-1], ((0, 0), (1, 0), (0, 0)))
    xx = x_prev - x
    xm = x[None] + xx[None] * mu[:, None, None, :]
    rkv = jnp.einsum('cbtd,cde->cbte', xm[:3], w_rkv)
    r, k, v = rkv[0], rkv[1], rkv[2]
    xw, xa, xg = xm[3], xm[4], xm[5]
    w = -jax.nn.softplus(-(decay_w0 + jnp.tanh(xw @ decay_w1) @ decay_w2)) - 0.5
    if vres_v0 is None:
        v_first = v
    else:
        v = v + (v_first - v) * jax.nn.sigmoid(vres_v0 + (xm[2] @ vres_v1) @ vres_v2)
    a = jax.nn.sigmoid(iclr_a0 + (xa @ iclr_a1) @ iclr_a2)
    g = jax.nn.sigmoid(xg @ gate_g1) @ gate_g2
    kk = _heads((k * k_k).astype(jnp.float32))
    kk = kk * lax.rsqrt(jnp.maximum(jnp.sum(kk * kk, axis=-1, keepdims=True), 1e-24))
    k = k * (1 + (a - 1) * k_a)
    decay = jnp.exp(-jnp.exp(w.astype(jnp.float32)))
    a_h = _heads(a.astype(jnp.float32))
    y = wkv7_scan(_heads(r), _heads(decay), _heads(k), _heads(v), -kk, kk * a_h)
    mean = jnp.mean(y, axis=-1, keepdims=True)
    var = jnp.mean(jnp.square(y - mean), axis=-1, keepdims=True)
    y = ((y - mean) * lax.rsqrt(var + GN_EPS)).reshape(bsz, T, D) * gn_g + gn_b
    bonus = jnp.sum(_heads(r) * _heads(k) * r_k, axis=-1, keepdims=True) * _heads(v)
    y = y + bonus.reshape(bsz, T, D)
    out = (y * g) @ w_out
    return out.astype(x.dtype), v_first

def moba_shared_kv(h, w_k, w_v):
    bsz, T, D = h.shape
    nb = -(-T // MOBA_BLOCK)
    pad = nb * MOBA_BLOCK - T

    def blocks(t):
        t = _heads(t).transpose(0, 2, 1, 3)
        t = jnp.pad(t, ((0, 0), (0, 0), (0, pad), (0, 0)))
        return t.reshape(bsz, N_HEADS, nb, MOBA_BLOCK, HEAD_DIM)

    k_blocks = blocks(h @ w_k)
    v_blocks = blocks(h @ w_v)
    k_means = jnp.mean(k_blocks.astype(jnp.float32), axis=3)
    return k_blocks, v_blocks, k_means

def moba_attention(x, w_q, w_o, k_blocks, v_blocks, k_means):
    bsz, T, D = x.shape
    nb = k_blocks.shape[2]
    topk = min(MOBA_TOPK, nb)
    scale = HEAD_DIM ** -0.5
    q = _heads(x @ w_q).transpose(0, 2, 1, 3)
    n_chunks = T // QUERY_CHUNK
    q_chunks = q.reshape(bsz, N_HEADS, n_chunks, QUERY_CHUNK, HEAD_DIM).transpose(2, 0, 1, 3, 4)
    gather_blocks = jax.vmap(jax.vmap(lambda blk_arr, idx: blk_arr[idx]))

    def attend_chunk(args):
        c, q_c = args
        start = c * QUERY_CHUNK
        own = start // MOBA_BLOCK
        q_pos = start + jnp.arange(QUERY_CHUNK)
        gate = jnp.einsum('bhqd,bhnd->bhqn', q_c.astype(jnp.float32), k_means)
        gate = jnp.where(jnp.arange(nb) < own, gate, -jnp.inf)
        _, sel = lax.top_k(gate, topk)
        k_sel = gather_blocks(k_blocks, sel)
        v_sel = gather_blocks(v_blocks, sel)
        s_sel = jnp.einsum('bhqd,bhqsjd->bhqsj', q_c, k_sel).astype(jnp.float32) * scale
        slot_ok = jnp.arange(topk) < own
        s_sel = jnp.where(slot_ok[:, None], s_sel, -jnp.inf)
        s_sel = s_sel.reshape(bsz, N_HEADS, QUERY_CHUNK, topk * MOBA_BLOCK)
        k_own = lax.dynamic_index_in_dim(k_blocks, own, axis=2, keepdims=False)
        v_own = lax.dynamic_index_in_dim(v_blocks, own, axis=2, keepdims=False)
        s_own = jnp.einsum('bhqd,bhkd->bhqk', q_c, k_own).astype(jnp.float32) * scale
        k_pos = own * MOBA_BLOCK + jnp.arange(MOBA_BLOCK)
        s_own = jnp.where(k_pos[None, :] <= q_pos[:, None], s_own, -jnp.inf)
        p = jax.nn.softmax(jnp.concatenate([s_sel, s_own], axis=-1), axis=-1)
        p_sel = p[..., :topk * MOBA_BLOCK].reshape(bsz, N_HEADS, QUERY_CHUNK, topk, MOBA_BLOCK)
        p_own = p[..., topk * MOBA_BLOCK:]
        o = (jnp.einsum('bhqsj,bhqsjd->bhqd', p_sel.astype(v_sel.dtype), v_sel)
             + jnp.einsum('bhqk,bhkd->bhqd', p_own.astype(v_own.dtype), v_own))
        return o

    o = lax.map(attend_chunk, (jnp.arange(n_chunks), q_chunks))
    o = o.transpose(1, 0, 3, 2, 4).reshape(bsz, T, D)
    return (o @ w_o).astype(x.dtype)

def swiglu(x, w_gate, w_up, w_down):
    return (jax.nn.silu(x @ w_gate) * (x @ w_up)) @ w_down

def moe_swiglu(x, router, w_gate, w_up, w_down):
    logits = (x @ router).astype(jnp.float32)
    top_logits, top_idx = lax.top_k(logits, TOP_K_EXPERTS)
    top_w = jax.nn.softmax(top_logits, axis=-1)
    gates = jnp.sum(jax.nn.one_hot(top_idx, N_EXPERTS, dtype=jnp.float32) * top_w[..., None], axis=-2)
    gates = gates.astype(x.dtype)
    out = jnp.zeros_like(x)
    for e in range(N_EXPERTS):
        out = out + gates[..., e:e + 1] * swiglu(x, w_gate[e], w_up[e], w_down[e])
    return out

def first_inputs(seed: int = 0) -> dict:
    key = jax.random.key(seed)
    ks = iter(jax.random.split(key, 48))
    D, H, N = D_MODEL, N_HEADS, HEAD_DIM
    f32 = jnp.float32

    def nrm(shape, scale):
        return jax.random.normal(next(ks), shape, f32) * scale

    def unif(shape, lo, hi):
        return jax.random.uniform(next(ks), shape, f32, lo, hi)

    beta = DEEPNORM_BETA
    nA, nV = N_A_LAYERS, max(N_A_LAYERS - 1, 0)
    rkv_scale = jnp.array([1.0, 1.0, beta], f32)[:, None, None]
    return {
        'x': nrm((BATCH, SEQ, D), 1.0),
        'rwkv_mu': unif((nA, 6, D), 0.0, 1.0),
        'rwkv_w_rkv': nrm((nA, 3, D, D), D ** -0.5) * rkv_scale,
        'rwkv_w_out': nrm((nA, D, D), D ** -0.5 * beta),
        'rwkv_decay_w0': unif((nA, D), -6.0, -1.0),
        'rwkv_decay_w1': nrm((nA, D, LORA_DECAY), D ** -0.5),
        'rwkv_decay_w2': nrm((nA, LORA_DECAY, D), 0.1 * LORA_DECAY ** -0.5),
        'rwkv_iclr_a0': nrm((nA, D), 0.1),
        'rwkv_iclr_a1': nrm((nA, D, LORA_ICLR), D ** -0.5),
        'rwkv_iclr_a2': nrm((nA, LORA_ICLR, D), 0.1 * LORA_ICLR ** -0.5),
        'rwkv_vres_v0': 1.0 + nrm((nV, D), 0.1),
        'rwkv_vres_v1': nrm((nV, D, LORA_VRES), D ** -0.5),
        'rwkv_vres_v2': nrm((nV, LORA_VRES, D), 0.1 * LORA_VRES ** -0.5),
        'rwkv_gate_g1': nrm((nA, D, LORA_GATE), D ** -0.5),
        'rwkv_gate_g2': nrm((nA, LORA_GATE, D), LORA_GATE ** -0.5),
        'rwkv_k_k': 0.85 + nrm((nA, D), 0.05),
        'rwkv_k_a': 1.0 + nrm((nA, D), 0.05),
        'rwkv_r_k': nrm((nA, H, N), 0.1),
        'rwkv_gn_g': 1.0 + nrm((nA, D), 0.05),
        'rwkv_gn_b': nrm((nA, D), 0.01),
        'moba_w_k': nrm((D, D), D ** -0.5),
        'moba_w_v': nrm((D, D), D ** -0.5 * beta),
        'moba_w_q': nrm((N_B_LAYERS, D, D), D ** -0.5),
        'moba_w_o': nrm((N_B_LAYERS, D, D), D ** -0.5 * beta),
        'ffn_w_gate': nrm((N_DENSE, D, D_FF), D ** -0.5),
        'ffn_w_up': nrm((N_DENSE, D, D_FF), D ** -0.5),
        'ffn_w_down': nrm((N_DENSE, D_FF, D), D_FF ** -0.5 * beta),
        'moe_router': nrm((N_MOE, D, N_EXPERTS), D ** -0.5),
        'moe_w_gate': nrm((N_MOE, N_EXPERTS, D, D_FF_EXPERT), D ** -0.5),
        'moe_w_up': nrm((N_MOE, N_EXPERTS, D, D_FF_EXPERT), D ** -0.5),
        'moe_w_down': nrm((N_MOE, N_EXPERTS, D_FF_EXPERT, D), D_FF_EXPERT ** -0.5 * beta),
        'ln_g': 1.0 + nrm((DEPTH, 2, D), 0.05),
        'ln_b': nrm((DEPTH, 2, D), 0.01),
    }

def first_block(x, rwkv_mu, rwkv_w_rkv, rwkv_w_out, rwkv_decay_w0, rwkv_decay_w1, rwkv_decay_w2,
              rwkv_iclr_a0, rwkv_iclr_a1, rwkv_iclr_a2, rwkv_vres_v0, rwkv_vres_v1, rwkv_vres_v2,
              rwkv_gate_g1, rwkv_gate_g2, rwkv_k_k, rwkv_k_a, rwkv_r_k, rwkv_gn_g, rwkv_gn_b,
              moba_w_k, moba_w_v, moba_w_q, moba_w_o,
              ffn_w_gate, ffn_w_up, ffn_w_down,
              moe_router, moe_w_gate, moe_w_up, moe_w_down,
              ln_g, ln_b):
    h = x
    v_first = None
    kv = None
    for layer in range(DEPTH):
        if layer < N_A_LAYERS:
            i = layer
            if i == 0:
                v0, v1, v2 = None, None, None
            else:
                v0, v1, v2 = rwkv_vres_v0[i - 1], rwkv_vres_v1[i - 1], rwkv_vres_v2[i - 1]
            mix, v_first = rwkv7_time_mix(
                h, v_first, rwkv_mu[i], rwkv_w_rkv[i], rwkv_w_out[i],
                rwkv_decay_w0[i], rwkv_decay_w1[i], rwkv_decay_w2[i],
                rwkv_iclr_a0[i], rwkv_iclr_a1[i], rwkv_iclr_a2[i], v0, v1, v2,
                rwkv_gate_g1[i], rwkv_gate_g2[i], rwkv_k_k[i], rwkv_k_a[i], rwkv_r_k[i],
                rwkv_gn_g[i], rwkv_gn_b[i])
        else:
            j = layer - N_A_LAYERS
            k_blocks, v_blocks, k_means = kv
            mix = moba_attention(h, moba_w_q[j], moba_w_o[j], k_blocks, v_blocks, k_means)
        h = deepnorm_residual(h, mix, ln_g[layer, 0], ln_b[layer, 0])
        if layer % 2 == 0:
            e = layer // 2
            ffn = swiglu(h, ffn_w_gate[e], ffn_w_up[e], ffn_w_down[e])
        else:
            e = layer // 2
            ffn = moe_swiglu(h, moe_router[e], moe_w_gate[e], moe_w_up[e], moe_w_down[e])
        h = deepnorm_residual(h, ffn, ln_g[layer, 1], ln_b[layer, 1])
        if layer == N_A_LAYERS - 1:
            kv = moba_shared_kv(h, moba_w_k, moba_w_v)
    return h


GRID_W = 64
CTX_LEN = 256
EPS = 1e-6
NEG_INF = -1e30

NA_HEADS = 8
NA_HEAD_DIM = 64
NA_WIN_ROWS = 8
NA_WIN_COLS = 16
NA_WIDTH = NA_HEADS * NA_HEAD_DIM

ML_HEADS = 4
ML_HEAD_DIM = 128
ML_WIDTH = ML_HEADS * ML_HEAD_DIM
ML_CHUNK = 128
ML_CONV = 3
ML_GATES = 4 * ML_HEADS

EVEN_IN = 3 * NA_WIDTH + 4 * ML_WIDTH + ML_GATES
EVEN_SPLITS = (NA_WIDTH, 2 * NA_WIDTH, 3 * NA_WIDTH,
               3 * NA_WIDTH + 2 * ML_WIDTH, 3 * NA_WIDTH + 3 * ML_WIDTH,
               3 * NA_WIDTH + 4 * ML_WIDTH)
EVEN_OUT = NA_WIDTH + ML_WIDTH

MLA_HEADS = 16
MLA_NOPE = 64
MLA_ROPE = 32
MLA_V = 64
MLA_QK_DIM = MLA_NOPE + MLA_ROPE
MLA_Q_RANK = 256
MLA_KV_RANK = 128
ATTN_BLOCK = 128
ROPE_BASE = 10000.0

FFN_HIDDEN = 2816
FFN_CONV = 3


def rms_norm(x, g):
    xf = x.astype(jnp.float32)
    y = xf * lax.rsqrt(jnp.mean(xf * xf, axis=-1, keepdims=True) + EPS)
    return (y * g.astype(jnp.float32)).astype(x.dtype)

def modulate(h, shift, scale):
    return h * (1 + scale) + shift

def dwconv_centred(x, w, b):
    k = w.shape[0]
    p = k // 2
    t = x.shape[1]
    xp = jnp.pad(x, ((0, 0), (p, p), (0, 0)))
    y = b + xp[:, 0:t] * w[0]
    for j in range(1, k):
        y = y + xp[:, j:j + t] * w[j]
    return y

def _rotate(x, pos):
    d = x.shape[-1]
    half = d // 2
    inv = ROPE_BASE ** (-jnp.arange(half, dtype=jnp.float32) / half)
    ang = pos.astype(jnp.float32)[:, None] * inv
    ang = ang.reshape((ang.shape[0],) + (1,) * (x.ndim - 3) + (half,))
    cos = jnp.cos(ang).astype(x.dtype)
    sin = jnp.sin(ang).astype(x.dtype)
    x1, x2 = x[..., :half], x[..., half:]
    return jnp.concatenate([x1 * cos - x2 * sin, x1 * sin + x2 * cos], axis=-1)

def rope_2d(x, row, col):
    a = x.shape[-1] // 2
    return jnp.concatenate([_rotate(x[..., :a], row), _rotate(x[..., a:], col)], axis=-1)

def dense_attention(q, k, v):
    s = jnp.einsum('bqhd,bkhd->bhqk', q, k).astype(jnp.float32) * (q.shape[-1] ** -0.5)
    p = jax.nn.softmax(s, axis=-1).astype(v.dtype)
    o = jnp.einsum('bhqk,bkhd->bqhd', p, v)
    return o.reshape(o.shape[0], o.shape[1], -1)

def blocked_attention(q, k, v):
    b, t, h, d = q.shape
    nb = t // ATTN_BLOCK
    qb = jnp.moveaxis(q.reshape(b, nb, ATTN_BLOCK, h, d), 1, 0)
    scale = d ** -0.5

    def one_block(qi):
        s = jnp.einsum('bqhd,bkhd->bhqk', qi, k).astype(jnp.float32) * scale
        p = jax.nn.softmax(s, axis=-1).astype(v.dtype)
        return jnp.einsum('bhqk,bkhd->bqhd', p, v)

    o = lax.map(one_block, qb)
    return jnp.moveaxis(o, 0, 1).reshape(b, t, -1)

def neighbourhood_attention(q, k, v, k_c, v_c, rpb):
    b, t, h, d = q.shape
    rows = t // GRID_W
    kh = min(NA_WIN_ROWS, rows)
    kw = NA_WIN_COLS
    scale = d ** -0.5
    qg = q.reshape(b, rows, GRID_W, h, d)
    kg = k.reshape(b, rows, GRID_W, h, d)
    vg = v.reshape(b, rows, GRID_W, h, d)
    col = jnp.arange(GRID_W)
    cs = jnp.clip(col - kw // 2, 0, GRID_W - kw)
    in_win = (col[None, :] >= cs[:, None]) & (col[None, :] < cs[:, None] + kw)
    dc_idx = jnp.clip(col[None, :] - col[:, None], -(kw - 1), kw - 1) + (NA_WIN_COLS - 1)
    rpb_cols = rpb.astype(jnp.float32)[:, :, dc_idx]

    def row_block(args):
        r, q_row = args
        rs = jnp.clip(r - kh // 2, 0, rows - kh)
        k_band = lax.dynamic_slice_in_dim(kg, rs, kh, axis=1).reshape(b, kh * GRID_W, h, d)
        v_band = lax.dynamic_slice_in_dim(vg, rs, kh, axis=1).reshape(b, kh * GRID_W, h, d)
        dr_idx = rs + jnp.arange(kh) - r + (NA_WIN_ROWS - 1)
        bias = jnp.take(rpb_cols, dr_idx, axis=1)
        bias = jnp.where(in_win[None, None], bias, NEG_INF)
        bias = bias.transpose(0, 2, 1, 3).reshape(h, GRID_W, kh * GRID_W)
        s_lat = jnp.einsum('bqhd,bkhd->bhqk', q_row, k_band).astype(jnp.float32) * scale + bias
        s_ctx = jnp.einsum('bqhd,bkhd->bhqk', q_row, k_c).astype(jnp.float32) * scale
        p = jax.nn.softmax(jnp.concatenate([s_lat, s_ctx], axis=-1), axis=-1).astype(v.dtype)
        nl = kh * GRID_W
        return (jnp.einsum('bhqk,bkhd->bqhd', p[..., :nl], v_band)
                + jnp.einsum('bhqk,bkhd->bqhd', p[..., nl:], v_c))

    o = lax.map(row_block, (jnp.arange(rows), jnp.moveaxis(qg, 1, 0)))
    return jnp.moveaxis(o, 0, 1).reshape(b, t, h * d)

def mlstm_chunked(q, k, v, i_pre, logf, state):
    b, h, t, d = q.shape
    nc = t // ML_CHUNK

    def to_chunks(a):
        return jnp.moveaxis(a.reshape(a.shape[:2] + (nc, ML_CHUNK) + a.shape[3:]), 2, 0)

    xs = tuple(to_chunks(a) for a in (q, k, v, i_pre, logf))
    lower = jnp.tril(jnp.ones((ML_CHUNK, ML_CHUNK), dtype=bool))

    def step(carry, chunk):
        c_st, n_st, m_st = carry
        qc, kc, vc, ic, fc = chunk
        bcum = jnp.cumsum(fc, axis=-1)
        d_in = jnp.where(lower, bcum[..., :, None] - bcum[..., None, :] + ic[..., None, :], -jnp.inf)
        m_inter = bcum + m_st[..., None]
        m_t = jnp.maximum(m_inter, jnp.max(d_in, axis=-1))
        w = jnp.exp(d_in - m_t[..., None])
        a = jnp.exp(m_inter - m_t)
        qk = jnp.einsum('bhtd,bhsd->bhts', qc, kc) * w
        num = (a[..., None] * jnp.einsum('bhvd,bhtd->bhtv', c_st, qc)
               + jnp.einsum('bhts,bhsv->bhtv', qk, vc))
        den = a * jnp.einsum('bhd,bhtd->bht', n_st, qc) + jnp.sum(qk, axis=-1)
        h_out = num / jnp.maximum(jnp.abs(den), jnp.exp(-m_t))[..., None]
        b_last = bcum[..., -1]
        g = b_last[..., None] - bcum + ic
        m_new = jnp.maximum(b_last + m_st, jnp.max(g, axis=-1))
        decay = jnp.exp(b_last + m_st - m_new)
        wk = jnp.exp(g - m_new[..., None])
        c_new = decay[..., None, None] * c_st + jnp.einsum('bhs,bhsv,bhsd->bhvd', wk, vc, kc)
        n_new = decay[..., None] * n_st + jnp.einsum('bhs,bhsd->bhd', wk, kc)
        return (c_new, n_new, m_new), h_out

    state, hs = lax.scan(step, state, xs)
    return jnp.moveaxis(hs, 0, 2).reshape(b, h, t, d), state

def _ml_heads(a):
    b, t, _ = a.shape
    return a.reshape(b, t, ML_HEADS, ML_HEAD_DIM).transpose(0, 2, 1, 3).astype(jnp.float32)

def _rev(a):
    return jnp.flip(a, axis=2)

def _mlstm_inputs(qk, v, g, conv_w, conv_b):
    qk = jax.nn.silu(dwconv_centred(qk, conv_w, conv_b))
    q, k = jnp.split(qk, 2, axis=-1)
    q = _ml_heads(q) * (ML_HEAD_DIM ** -0.5)
    g = g.astype(jnp.float32).transpose(0, 2, 1)
    i_f, f_f, i_b, f_b = jnp.split(g, 4, axis=1)
    return (_ml_heads(q.transpose(0, 2, 1, 3).reshape(q.shape[0], q.shape[2], ML_WIDTH)),
            _ml_heads(k), _ml_heads(v),
            i_f, jax.nn.log_sigmoid(f_f), i_b, jax.nn.log_sigmoid(f_b))

def _mlstm_output(h, o_pre, g):
    b, nh, t, d = h.shape
    o = jax.nn.sigmoid(o_pre.astype(jnp.float32)).reshape(b, t, nh, d).transpose(0, 2, 1, 3)
    h = o * h
    mu = jnp.mean(h, axis=-1, keepdims=True)
    var = jnp.mean(jnp.square(h - mu), axis=-1, keepdims=True)
    h = (h - mu) * lax.rsqrt(var + EPS)
    h = h.transpose(0, 2, 1, 3).reshape(b, t, nh * d) * g.astype(jnp.float32)
    return h.astype(o_pre.dtype)

def _zero_state(b):
    return (jnp.zeros((b, ML_HEADS, ML_HEAD_DIM, ML_HEAD_DIM), jnp.float32),
            jnp.zeros((b, ML_HEADS, ML_HEAD_DIM), jnp.float32),
            jnp.zeros((b, ML_HEADS), jnp.float32))

def even_mixer(hx, hc, w_in, gate_b, conv_w, conv_b, rpb, ml_norm_g, w_out, ctx_out):
    naq_x, nak_x, nav_x, mlqk_x, mlv_x, mlo_x, mlg_x = jnp.split(hx @ w_in, list(EVEN_SPLITS), axis=-1)
    naq_c, nak_c, nav_c, mlqk_c, mlv_c, mlo_c, mlg_c = jnp.split(hc @ w_in, list(EVEN_SPLITS), axis=-1)

    def heads(a):
        return a.reshape(a.shape[0], a.shape[1], NA_HEADS, NA_HEAD_DIM)

    na_x = neighbourhood_attention(heads(naq_x), heads(nak_x), heads(nav_x),
                                   heads(nak_c), heads(nav_c), rpb)

    q_x, k_x, v_x, if_x, lf_x, ib_x, lb_x = _mlstm_inputs(mlqk_x, mlv_x, mlg_x + gate_b, conv_w, conv_b)
    q_c, k_c, v_c, if_c, lf_c, ib_c, lb_c = _mlstm_inputs(mlqk_c, mlv_c, mlg_c + gate_b, conv_w, conv_b)
    zero = _zero_state(hx.shape[0])
    h_cf, st_f = mlstm_chunked(q_c, k_c, v_c, if_c, lf_c, zero)
    h_xf, _ = mlstm_chunked(q_x, k_x, v_x, if_x, lf_x, st_f)
    h_cb, st_b = mlstm_chunked(_rev(q_c), _rev(k_c), _rev(v_c), _rev(ib_c), _rev(lb_c), zero)
    h_xb, _ = mlstm_chunked(_rev(q_x), _rev(k_x), _rev(v_x), _rev(ib_x), _rev(lb_x), st_b)
    ml_x = _mlstm_output(h_xf + _rev(h_xb), mlo_x, ml_norm_g)
    y_x = jnp.concatenate([na_x, ml_x], axis=-1) @ w_out
    if not ctx_out:
        return y_x, None
    na_c = dense_attention(heads(naq_c), heads(nak_c), heads(nav_c))
    ml_c = _mlstm_output(h_cf + _rev(h_cb), mlo_c, ml_norm_g)
    y_c = jnp.concatenate([na_c, ml_c], axis=-1) @ w_out
    return y_x, y_c

def _mla_q(h, w_dq, q_norm_g, w_uq, row, col):
    b, t, _ = h.shape
    q = (rms_norm(h @ w_dq, q_norm_g) @ w_uq).reshape(b, t, MLA_HEADS, MLA_QK_DIM)
    if row is None:
        return q
    return jnp.concatenate([q[..., :MLA_NOPE], rope_2d(q[..., MLA_NOPE:], row, col)], axis=-1)

def _mla_kv(h, w_dkv, kv_norm_g, w_ukv, row, col):
    b, t, _ = h.shape
    ckv = h @ w_dkv
    c_kv, k_pe = ckv[..., :MLA_KV_RANK], ckv[..., MLA_KV_RANK:]
    if row is not None:
        k_pe = rope_2d(k_pe, row, col)
    kv = (rms_norm(c_kv, kv_norm_g) @ w_ukv).reshape(b, t, MLA_HEADS, MLA_NOPE + MLA_V)
    k = jnp.concatenate([kv[..., :MLA_NOPE],
                         jnp.broadcast_to(k_pe[:, :, None, :], (b, t, MLA_HEADS, MLA_ROPE))], axis=-1)
    return k, kv[..., MLA_NOPE:]

def odd_mixer(hx, hc, w_dq, q_norm_g, w_uq, w_dkv, kv_norm_g, w_ukv, w_o, row, col, ctx_out):
    q_x = _mla_q(hx, w_dq, q_norm_g, w_uq, row, col)
    k_x, v_x = _mla_kv(hx, w_dkv, kv_norm_g, w_ukv, row, col)
    k_c, v_c = _mla_kv(hc, w_dkv, kv_norm_g, w_ukv, None, None)
    y_x = blocked_attention(q_x, jnp.concatenate([k_x, k_c], axis=1),
                            jnp.concatenate([v_x, v_c], axis=1)) @ w_o
    if not ctx_out:
        return y_x, None
    q_c = _mla_q(hc, w_dq, q_norm_g, w_uq, None, None)
    return y_x, dense_attention(q_c, k_c, v_c) @ w_o

def conv_ffn(h, w_up, conv_w, conv_b, w_down):
    u = dwconv_centred(h @ w_up, conv_w, conv_b)
    a, g = jnp.split(u, 2, axis=-1)
    return (a * jax.nn.silu(g)) @ w_down

def second_inputs(seed: int = 0) -> dict:
    key = jax.random.key(seed)
    ks = jax.random.split(key, 32)
    n_even = (DEPTH + 1) // 2
    n_odd = DEPTH // 2
    f32 = jnp.float32

    def nrm(k, shape, scale):
        return jax.random.normal(k, shape, f32) * scale

    gk = jax.random.split(ks[15], 4)
    forget_b = jnp.linspace(3.0, 6.0, ML_HEADS, dtype=f32)
    gate_b = jnp.concatenate([
        nrm(gk[0], (n_even, ML_HEADS), 0.1),
        forget_b + nrm(gk[1], (n_even, ML_HEADS), 0.1),
        nrm(gk[2], (n_even, ML_HEADS), 0.1),
        forget_b + nrm(gk[3], (n_even, ML_HEADS), 0.1)], axis=-1)
    return {
        "x": nrm(ks[0], (BATCH, SEQ, D_MODEL), 1.0),
        "c": nrm(ks[1], (BATCH, D_MODEL), 1.0),
        "ctx": nrm(ks[2], (BATCH, CTX_LEN, D_MODEL), 1.0),
        "c_ctx": nrm(ks[3], (D_MODEL,), 1.0),
        "ada_w": nrm(ks[4], (DEPTH, D_MODEL, 6 * D_MODEL), D_MODEL ** -0.5),
        "ada_b": nrm(ks[5], (DEPTH, 6 * D_MODEL), 0.02),
        "norm_g": 1.0 + nrm(ks[6], (DEPTH, 4, D_MODEL), 0.05),
        "ffn_w_up": nrm(ks[7], (DEPTH, D_MODEL, 2 * FFN_HIDDEN), D_MODEL ** -0.5),
        "ffn_conv_w": nrm(ks[8], (DEPTH, FFN_CONV, 2 * FFN_HIDDEN), FFN_CONV ** -0.5),
        "ffn_conv_b": nrm(ks[9], (DEPTH, 2 * FFN_HIDDEN), 0.02),
        "ffn_w_down": nrm(ks[10], (DEPTH, FFN_HIDDEN, D_MODEL), FFN_HIDDEN ** -0.5),
        "ev_w_in": nrm(ks[11], (n_even, D_MODEL, EVEN_IN), D_MODEL ** -0.5),
        "ev_gate_b": gate_b,
        "ev_conv_w": nrm(ks[12], (n_even, ML_CONV, 2 * ML_WIDTH), ML_CONV ** -0.5),
        "ev_conv_b": nrm(ks[13], (n_even, 2 * ML_WIDTH), 0.02),
        "ev_rpb": nrm(ks[14], (n_even, NA_HEADS, 2 * NA_WIN_ROWS - 1, 2 * NA_WIN_COLS - 1), 0.1),
        "ev_ml_norm_g": 1.0 + nrm(ks[16], (n_even, ML_WIDTH), 0.05),
        "ev_w_out": nrm(ks[17], (n_even, EVEN_OUT, D_MODEL), EVEN_OUT ** -0.5),
        "od_w_dq": nrm(ks[18], (n_odd, D_MODEL, MLA_Q_RANK), D_MODEL ** -0.5),
        "od_q_norm_g": 1.0 + nrm(ks[19], (n_odd, MLA_Q_RANK), 0.05),
        "od_w_uq": nrm(ks[20], (n_odd, MLA_Q_RANK, MLA_HEADS * MLA_QK_DIM), MLA_Q_RANK ** -0.5),
        "od_w_dkv": nrm(ks[21], (n_odd, D_MODEL, MLA_KV_RANK + MLA_ROPE), D_MODEL ** -0.5),
        "od_kv_norm_g": 1.0 + nrm(ks[22], (n_odd, MLA_KV_RANK), 0.05),
        "od_w_ukv": nrm(ks[23], (n_odd, MLA_KV_RANK, MLA_HEADS * (MLA_NOPE + MLA_V)), MLA_KV_RANK ** -0.5),
        "od_w_o": nrm(ks[24], (n_odd, MLA_HEADS * MLA_V, D_MODEL), (MLA_HEADS * MLA_V) ** -0.5),
    }

def second_block(x, c, ctx, c_ctx, ada_w, ada_b, norm_g, ffn_w_up, ffn_conv_w, ffn_conv_b, ffn_w_down,
              ev_w_in, ev_gate_b, ev_conv_w, ev_conv_b, ev_rpb, ev_ml_norm_g, ev_w_out,
              od_w_dq, od_q_norm_g, od_w_uq, od_w_dkv, od_kv_norm_g, od_w_ukv, od_w_o):
    t = x.shape[1]
    pos = jnp.arange(t)
    row = pos // GRID_W
    col = pos % GRID_W
    silu_c = jax.nn.silu(c)
    silu_cc = jax.nn.silu(c_ctx)
    xc = ctx
    for l in range(DEPTH):
        ctx_out = l < DEPTH - 1
        mod_x = (silu_c @ ada_w[l] + ada_b[l])[:, None, :]
        mod_c = silu_cc @ ada_w[l] + ada_b[l]
        sh1, sc1, g1, sh2, sc2, g2 = jnp.split(mod_x, 6, axis=-1)
        csh1, csc1, cg1, csh2, csc2, cg2 = jnp.split(mod_c, 6, axis=-1)
        hx = modulate(rms_norm(x, norm_g[l, 0]), sh1, sc1)
        hc = modulate(rms_norm(xc, norm_g[l, 0]), csh1, csc1)
        if l % 2 == 0:
            e = l // 2
            yx, yc = even_mixer(hx, hc, ev_w_in[e], ev_gate_b[e], ev_conv_w[e], ev_conv_b[e],
                                ev_rpb[e], ev_ml_norm_g[e], ev_w_out[e], ctx_out)
        else:
            o = l // 2
            yx, yc = odd_mixer(hx, hc, od_w_dq[o], od_q_norm_g[o], od_w_uq[o], od_w_dkv[o],
                               od_kv_norm_g[o], od_w_ukv[o], od_w_o[o], row, col, ctx_out)
        x = x + g1 * rms_norm(yx, norm_g[l, 1])
        hx = modulate(rms_norm(x, norm_g[l, 2]), sh2, sc2)
        x = x + g2 * rms_norm(conv_ffn(hx, ffn_w_up[l], ffn_conv_w[l], ffn_conv_b[l], ffn_w_down[l]),
                              norm_g[l, 3])
        if ctx_out:
            xc = xc + cg1 * rms_norm(yc, norm_g[l, 1])
            hc = modulate(rms_norm(xc, norm_g[l, 2]), csh2, csc2)
            xc = xc + cg2 * rms_norm(conv_ffn(hc, ffn_w_up[l], ffn_conv_w[l], ffn_conv_b[l], ffn_w_down[l]),
                                     norm_g[l, 3])
    return x


def setup_inputs(seed=0):
    out = dict(first_inputs(seed))
    for name, value in second_inputs(seed + 1).items():
        if name != "x":
            out[name + "_2"] = value
    return out


def reference(
    x, rwkv_mu, rwkv_w_rkv, rwkv_w_out, rwkv_decay_w0, rwkv_decay_w1, rwkv_decay_w2,
    rwkv_iclr_a0, rwkv_iclr_a1, rwkv_iclr_a2, rwkv_vres_v0, rwkv_vres_v1, rwkv_vres_v2,
    rwkv_gate_g1, rwkv_gate_g2, rwkv_k_k, rwkv_k_a, rwkv_r_k, rwkv_gn_g, rwkv_gn_b, moba_w_k,
    moba_w_v, moba_w_q, moba_w_o, ffn_w_gate, ffn_w_up, ffn_w_down, moe_router, moe_w_gate,
    moe_w_up, moe_w_down, ln_g, ln_b, c_2, ctx_2, c_ctx_2, ada_w_2, ada_b_2, norm_g_2,
    ffn_w_up_2, ffn_conv_w_2, ffn_conv_b_2, ffn_w_down_2, ev_w_in_2, ev_gate_b_2, ev_conv_w_2,
    ev_conv_b_2, ev_rpb_2, ev_ml_norm_g_2, ev_w_out_2, od_w_dq_2, od_q_norm_g_2, od_w_uq_2,
    od_w_dkv_2, od_kv_norm_g_2, od_w_ukv_2, od_w_o_2,
):
    x = first_block(
        x, rwkv_mu, rwkv_w_rkv, rwkv_w_out, rwkv_decay_w0, rwkv_decay_w1, rwkv_decay_w2,
        rwkv_iclr_a0, rwkv_iclr_a1, rwkv_iclr_a2, rwkv_vres_v0, rwkv_vres_v1, rwkv_vres_v2,
        rwkv_gate_g1, rwkv_gate_g2, rwkv_k_k, rwkv_k_a, rwkv_r_k, rwkv_gn_g, rwkv_gn_b,
        moba_w_k, moba_w_v, moba_w_q, moba_w_o, ffn_w_gate, ffn_w_up, ffn_w_down, moe_router,
        moe_w_gate, moe_w_up, moe_w_down, ln_g, ln_b,
    )
    return second_block(
        x, c_2, ctx_2, c_ctx_2, ada_w_2, ada_b_2, norm_g_2, ffn_w_up_2, ffn_conv_w_2,
        ffn_conv_b_2, ffn_w_down_2, ev_w_in_2, ev_gate_b_2, ev_conv_w_2, ev_conv_b_2, ev_rpb_2,
        ev_ml_norm_g_2, ev_w_out_2, od_w_dq_2, od_q_norm_g_2, od_w_uq_2, od_w_dkv_2,
        od_kv_norm_g_2, od_w_ukv_2, od_w_o_2,
    )


_drawn_inputs = setup_inputs


def setup_inputs(seed=0):
    import zlib

    import numpy as np

    out = dict(_drawn_inputs(seed))
    spreads = {}
    factors = {'rwkv_decay_w1': 8.0,
     'rwkv_decay_w2': 8.0,
     'rwkv_iclr_a0': 5.005,
     'rwkv_iclr_a1': 4.636,
     'rwkv_iclr_a2': 4.84,
     'rwkv_k_k': 4.723,
     'rwkv_k_a': 4.995,
     'rwkv_gn_g': 4.918,
     'rwkv_gn_b': 8.0,
     'ffn_conv_b_2': 4.297,
     'ev_conv_b_2': 8.0,
     'ev_rpb_2': 8.0,
     'od_q_norm_g_2': 8.0,
     'od_kv_norm_g_2': 3.126}
    for name, (base, spread) in spreads.items():
        noise = np.random.default_rng([zlib.crc32(name.encode()), seed]).standard_normal(out[name].shape)
        drawn = base * np.exp(spread * noise) if base else spread * noise
        out[name] = jnp.asarray(drawn.astype(out[name].dtype))
    for name, factor in factors.items():
        out[name] = (out[name] * factor).astype(out[name].dtype)
    return out
```

```python
import math
from contextlib import ExitStack

import concourse.bass as bass
from concourse import mybir

F32 = mybir.dt.float32
U32 = mybir.dt.uint32
ALU = mybir.AluOpType
ACT = mybir.ActivationFunctionType
AX = mybir.AxisListType.X

P = 128
D = 1024
KT = D // P
T = 256
TT = T // P
CH = 2048
R = 7
FF = 2816
FE = 3584
NE = 8
ALPHA = 4.0 ** 0.25
NEG = -1e30


class Sig:

    def __init__(self, handle):
        self.h, self.n, self.base = handle, 0, 0

    def up(self, by=1):
        self.n += by
        return self.h, by

    def at(self, k):
        return self.h, self.base + k

    def now(self):
        return self.h, self.n


class Kern:

    def __init__(self, nc, ctx, ins, out):
        self.nc, self.ctx, self.i, self.out = nc, ctx, ins, out
        sem = lambda n: ctx.enter_context(nc.semaphore(n))
        sb = lambda n, s, dt=F32: ctx.enter_context(nc.sbuf_tensor(n, s, dt))
        self.ring = sb("weight_ring", [P, R, CH])
        self.landed = [sem(f"weights_landed{s}") for s in range(R)]
        self.used = Sig(sem("weights_used"))
        self.dve, self.act, self.pool = Sig(sem("dve_chain")), Sig(sem("act_chain")), Sig(sem("pool_chain"))
        self.free_sigs = [Sig(sem(f"signal{n}")) for n in range(14)]
        self.load = Sig(sem("small_loads"))
        self.ps = [ctx.enter_context(nc.psum_tensor(f"bank{b}", [P, 512], F32)) for b in range(8)]
        self.plan, self.taken, self.issued = [], 0, 0
        self.ident = sb("ident", [P, P])
        self.ones = sb("ones", [P, P])
        self.junk = sb("junk", [P, 1])
        self.nphase, self.uniq = 0, 0

    def sig(self, n):
        out = self.free_sigs[:n]
        for s in out:
            s.base = s.n
        return out

    def begin(self):
        self.nphase += 1
        for s in (self.used, self.dve, self.act, self.pool, self.load):
            s.base = s.n
        self.used.base = self.taken
        return self.nc.Block(f"phase{self.nphase}", no_gpsimd_drain=True)

    def chunk(self, pe):
        n = self.taken
        self.taken += 1
        pe.wait_ge(self.landed[n % R], 16 * (n // R + 1))
        return self.ring[:, n % R, :]

    def stream(self, sp):
        while self.issued < min(self.taken + R, len(self.plan)):
            n = self.issued
            if n >= R:
                sp.wait_ge(self.used.h, n - R + 1)
            sp.dma_start(self.ring[:, n % R, :], self.plan[n]).then_inc(self.landed[n % R], 16)
            self.issued += 1

    def v(self, eng, ins, sig=None):
        s = sig or self.dve
        ins.then_inc(*s.up())
        eng.wait_ge(*s.now())

    def a(self, eng, ins, sig=None):
        s = sig or self.act
        ins.then_inc(*s.up())
        eng.wait_ge(*s.now())

    def g(self, eng, ins, sig=None):
        s = sig or self.pool
        ins.then_inc(*s.up())
        eng.wait_ge(*s.now())


def scratch(K, st, *shapes):
    K.uniq += 1
    return [st.enter_context(K.nc.sbuf_tensor(f"s{K.uniq}_{n}", list(s), F32)) for n, s in enumerate(shapes)]


def load(K, eng, dst, src):
    eng.dma_start(dst, src).then_inc(*K.load.up(16))


def bc(ap, shape):
    return ap.broadcast_to(list(shape))


def constants(K):
    nc = K.nc
    with K.begin() as block:
        @block.gpsimd
        def _(pool):
            K.g(pool, nc.gpsimd.memset(K.ident[:, :], 0.0))
            K.g(pool, nc.gpsimd.memset(K.ones[:, :], 1.0))
            K.g(pool, nc.gpsimd.affine_select(out=K.ident[:, :], in_=K.ident[:, :], compare_op=ALU.not_equal,
                                              fill=1.0, base=0, pattern=[[-1, P]], channel_multiplier=1))

        @block.sync
        def _(sp):
            K.stream(sp)


def load_phase(K, pairs):
    with K.begin() as block:
        @block.scalar
        def _(act):
            for dst, src in pairs:
                load(K, act, dst, src)
            act.wait_ge(*K.load.now())


def linear_cols(K, jobs):
    nc = K.nc
    evac, = K.sig(1)
    with K.begin() as block:
        @block.tensor
        def _(pe):
            n = 0
            for x, chunks, _ in jobs:
                tok = x.shape[2]
                nb = tok // 256
                for c in range(chunks):
                    w = K.chunk(pe).rearrange("p (k n) -> p k n", k=KT)
                    if n >= 3:
                        pe.wait_ge(*evac.at(n - 2))
                    for h in range(2):
                        for k in range(KT):
                            o = K.ps[n % 3 * 2 + (h if nb == 2 else 0)][:, (0 if nb == 2 else h * tok):][:, 0:tok]
                            last = nc.tensor.matmul(o, w[:, k, h * P:(h + 1) * P], x[:, k, :],
                                                    start=(k == 0), stop=(k == KT - 1))
                    last.then_inc(*K.used.up())
                    n += 1

        @block.scalar
        def _(act):
            n = 0
            for x, chunks, fn in jobs:
                tok = x.shape[2]
                nb = tok // 256
                for c in range(chunks):
                    act.wait_ge(*K.used.at(n + 1))
                    for h in range(2):
                        o = K.ps[n % 3 * 2 + (h if nb == 2 else 0)][:, (0 if nb == 2 else h * tok):][:, 0:tok]
                        last = fn(act, c, h, o)
                    K.a(act, last, evac)
                    n += 1

        @block.sync
        def _(sp):
            K.stream(sp)


def mm_rows(K, pe, x, kts, first=True, final=True, banks=(0, 1, 2, 3), tts=TT):
    nc = K.nc
    for i in range(0, len(kts), 2):
        w = K.chunk(pe).rearrange("p (k n) -> p k n", k=2)
        for q in range(2):
            for tt in range(tts):
                for h in range(2):
                    last = nc.tensor.matmul(K.ps[banks[tt * 2 + h]][:, :], x[:, kts[i + q], tt * P:(tt + 1) * P],
                                            w[:, q, h * 512:(h + 1) * 512],
                                            start=(first and i == 0 and q == 0),
                                            stop=(final and i + q == len(kts) - 1))
        last.then_inc(*K.used.up())


def linear_rows(K, x, kts, evac, tts=TT, after=None, sqrts=None, root_bufs=()):
    nc = K.nc
    with K.begin() as block:
        @block.tensor
        def _(pe):
            mm_rows(K, pe, x, kts, banks=tuple(range(8)), tts=tts)

        @block.vector
        def _(dve):
            dve.wait_ge(*K.used.at(len(kts) // 2))
            for tt in range(tts):
                for h in range(2):
                    K.v(dve, evac(dve, tt, h, K.ps[tt * 2 + h][:, :]))
            if after:
                after(dve)

        @block.scalar
        def _(act):
            if sqrts:
                roots(K, act, *sqrts, root_bufs)

        @block.sync
        def _(sp):
            K.stream(sp)


def to_cols(K, rows, cols, tiles, tts=TT, evac=None, width=P):
    nc = K.nc
    done, read = K.sig(2)
    jobs = [(tt, j) for tt in range(tts) for j in range(tiles)]
    with K.begin() as block:
        @block.tensor
        def _(pe):
            for n, (tt, j) in enumerate(jobs):
                if n % 4 == 0 and n >= 32:
                    pe.wait_ge(*read.at(n // 4 - 7))
                last = nc.tensor.transpose(K.ps[n // 4 % 8][0:width, n % 4 * P:n % 4 * P + P],
                                           rows(tt, j), K.ident[:, :])
                if n % 4 == 3 or n == len(jobs) - 1:
                    last.then_inc(*done.up())

        @block.scalar
        def _(act):
            for n, (tt, j) in enumerate(jobs):
                if n % 4 == 0:
                    act.wait_ge(*done.at(n // 4 + 1))
                src = K.ps[n // 4 % 8][0:width, n % 4 * P:n % 4 * P + P]
                last = evac(j, tt, src) if evac else nc.scalar.activation(cols(j, tt), src, ACT.Copy)
                if n % 4 == 3 or n == len(jobs) - 1:
                    last.then_inc(*read.up())
            act.wait_ge(*read.now())

        @block.sync
        def _(sp):
            K.stream(sp)


def roots(K, act, ask, given, bufs):
    for n, buf in enumerate(bufs):
        act.wait_ge(*ask.at(n + 1))
        K.nc.scalar.activation(buf, buf, ACT.Sqrt).then_inc(*given.up())


def rsqrt(K, dve, ins, buf, sqrts):
    ask, given = sqrts
    K.v(dve, ins, ask)
    dve.wait_ge(*given.at(ask.n - ask.base))
    K.v(dve, K.nc.vector.reciprocal(buf, buf))


def layer_norm(K, dve, z, out, small, g, b, width, groups, eps, sqrts):
    nc = K.nc
    st, mv, rs = small
    for n in range(groups):
        for q in range(0, width, 512):
            K.v(dve, nc.vector.bn_stats(st[:, (q // 512) * 6:(q // 512) * 6 + 6], z[:, n, q:q + min(512, width)]))
        K.v(dve, nc.vector.bn_aggr(mv[:, n, :], st[:, 0:6 * max(1, width // 512)]))
    rsqrt(K, dve, nc.vector.tensor_scalar(rs[:, 0:groups], mv[:, 0:groups, 1], eps, None, ALU.add),
          rs[:, 0:groups], sqrts)
    for n in range(groups):
        K.v(dve, nc.vector.tensor_scalar(out[:, n, :], z[:, n, :], mv[:, n, 0:1], rs[:, n:n + 1],
                                         ALU.subtract, ALU.mult))
    flat = out.rearrange("p n w -> p (n w)")
    K.v(dve, nc.vector.tensor_tensor(flat, flat, g, ALU.mult))
    if b is not None:
        K.v(dve, nc.vector.tensor_tensor(flat, flat, b, ALU.add))


def gated_hidden(K, st, x, hid, chunks, conv=None):
    nc = K.nc
    tok = x.shape[2]
    seqs = tok // T
    nb = tok // 256
    side = scratch(K, st, [P, 2, 2, 2, tok])[0]
    centre, tapped, gated, free = K.sig(4)

    def bank(c, s, h):
        return K.ps[c % 2 * 4 + s * 2 + (h if nb == 2 else 0)][:, (0 if nb == 2 else h * tok):][:, 0:tok]

    with K.begin() as block:
        @block.tensor
        def _(pe):
            for c in range(chunks):
                if c >= 2:
                    pe.wait_ge(*free.at(c - 1))
                for s in range(2):
                    w = K.chunk(pe).rearrange("p (k n) -> p k n", k=KT)
                    for h in range(2):
                        for k in range(KT):
                            last = nc.tensor.matmul(bank(c, s, h), w[:, k, h * P:(h + 1) * P], x[:, k, :],
                                                    start=(k == 0), stop=(k == KT - 1))
                    last.then_inc(*K.used.up())

        @block.scalar
        def _(act):
            def silu(c):
                act.wait_ge(*tapped.at(c + 1))
                for h in range(2):
                    last = nc.scalar.activation(side[:, c % 2, 0, h, :], side[:, c % 2, 0, h, :], ACT.Silu)
                last.then_inc(*gated.up())

            for c in range(chunks):
                if conv is None:
                    act.wait_ge(*K.used.at(2 * c + 1))
                    if c >= 2:
                        act.wait_ge(*free.at(c - 1))
                    for h in range(2):
                        last = nc.scalar.activation(side[:, c % 2, 0, h, :], bank(c, 0, h), ACT.Silu)
                    last.then_inc(*gated.up())
                    continue
                act.wait_ge(*K.used.at(2 * c + 2))
                if c >= 2:
                    act.wait_ge(*free.at(c - 1))
                for s in range(2):
                    for h in range(2):
                        j = (chunks * 2 if s == 0 else 0) + 2 * c + h
                        last = nc.scalar.activation(side[:, c % 2, s, h, :], bank(c, s, h), ACT.Identity,
                                                    bias=conv[1][:, j:j + 1], scale=conv[0][:, j, 1:2])
                last.then_inc(*centre.up())
                if c >= 1:
                    silu(c - 1)
            if conv is not None:
                silu(chunks - 1)

        @block.vector
        def _(dve):
            def product(c):
                dve.wait_ge(*gated.at(c + 1))
                for h in range(2):
                    up = side[:, c % 2, 1, h, :] if conv else bank(c, 1, h)
                    last = nc.vector.tensor_tensor(hid[:, 2 * c + h, :], side[:, c % 2, 0, h, :], up, ALU.mult)
                last.then_inc(*free.up())

            for c in range(chunks):
                if conv is None:
                    dve.wait_ge(*K.used.at(2 * c + 2))
                    product(c)
                    continue
                dve.wait_ge(*centre.at(c + 1))
                for tap, (dst, src) in enumerate(((slice(1, T), slice(0, T - 1)), (slice(0, T - 1), slice(1, T)))):
                    for s in range(2):
                        for h in range(2):
                            j = (chunks * 2 if s == 0 else 0) + 2 * c + h
                            o = side[:, c % 2, s, h, :].rearrange("p (q t) -> p q t", q=seqs)[:, :, dst]
                            i = bank(c, s, h).rearrange("p (q t) -> p q t", q=seqs)[:, :, src]
                            last = nc.vector.scalar_tensor_tensor(o, i, conv[0][:, j, 2 * tap:2 * tap + 1], o,
                                                                  ALU.mult, ALU.add)
                    K.v(dve, last, tapped if tap else None)
                if c >= 1:
                    product(c - 1)
            if conv is not None:
                product(chunks - 1)
            dve.wait_ge(*free.now())

        @block.sync
        def _(sp):
            K.stream(sp)


def rwkv(K, h1):
    nc, i = K.nc, K.i
    with ExitStack() as st:
        S = lambda *s: scratch(K, st, *s)
        units, = S([P, 14, CH])
        unit = lambda n, pat="p (j t) -> p j t", **kw: units[:, n, :].rearrange(pat, **kw)
        vr, gr = (unit(n, j=TT) for n in (0, 1))
        rT, kT, aT, dec = (unit(n, j=KT) for n in (2, 3, 4, 5))
        cols, = S([P, 5, KT])
        w0, a0, k_k, k_a, r_k = (cols[:, n, :] for n in range(5))
        with ExitStack() as st1:
            S1 = lambda *s: scratch(K, st1, *s)
            mixes = [unit(n, j=KT) for n in range(6, 12)]
            xT = unit(12, j=KT)
            mu, w2s, a2s, g1s, g2a, g2b = S1([P, 6, KT], [64, D], [64, D], [P, KT, 160], [P, D], [32, D])
            w1s = units[:, 13, 0:512].rearrange("p (k n) -> p k n", k=KT)
            a1s = units[:, 13, 512:1024].rearrange("p (k n) -> p k n", k=KT)
            hw, ha = units[0:64, 13, 1024:1280], units[0:64, 13, 1280:1536]
            hg, hg2 = units[:, 13, 1536:1792], units[0:32, 13, 1792:2048]
            load_phase(K, [(xT[:, :, :], i["x_cols"]), (mu[:, :, :], i["mu_cols"]), (cols[:, :, :], i["rwkv_cols"]),
                           (w1s[:, :, :], i["decay_w1"]), (w2s[:, :], i["decay_w2"]),
                           (a1s[:, :, :], i["iclr_a1"]), (a2s[:, :], i["iclr_a2"]), (g1s[:, :, :], i["gate_g1"]),
                           (g2a[:, :], i["gate_g2"][0:P, :]), (g2b[:, :], i["gate_g2"][P:160, :])])
            xx = mixes[5]

            with K.begin() as block:
                @block.vector
                def _(dve):
                    nc.vector.tensor_tensor(xx[:, :, 1:T], xT[:, :, 0:T - 1], xT[:, :, 1:T], ALU.subtract)
                    K.v(dve, nc.vector.tensor_scalar(xx[:, :, 0:1], xT[:, :, 0:1], -1.0, None, ALU.mult))
                    for m in range(6):
                        for k in range(KT):
                            last = nc.vector.scalar_tensor_tensor(mixes[m][:, k, :], xx[:, k, :], mu[:, m, k:k + 1],
                                                                  xT[:, k, :], ALU.mult, ALU.add)
                    K.v(dve, last)

                @block.sync
                def _(sp):
                    K.stream(sp)

            def keep(dst):
                return lambda act, c, h, o: nc.scalar.activation(dst[:, 2 * c + h, :], o, ACT.Copy)

            linear_cols(K, [(mixes[0], 4, keep(rT)), (mixes[1], 4, keep(kT))])
            linear_rows(K, mixes[2], range(KT), lambda dve, tt, h, o: nc.vector.tensor_copy(
                vr[:, tt, h * 512:(h + 1) * 512], o))

            low, mid, hi, seen = K.sig(4)
            with K.begin() as block:
                @block.tensor
                def _(pe):
                    for b, (x, w, n0, n1) in enumerate(((mixes[3], w1s, 0, 64), (mixes[4], a1s, 0, 64),
                                                        (mixes[5], g1s, 0, P), (mixes[5], g1s, P, 160))):
                        for k in range(KT):
                            last = nc.tensor.matmul(K.ps[b][0:n1 - n0, 0:T], w[:, k, n0:n1], x[:, k, :],
                                                    start=(k == 0), stop=(k == KT - 1))
                        last.then_inc(*low.up())
                    pe.wait_ge(*mid.at(4))
                    for n in range(2 * KT):
                        w, x = (w2s, hw) if n < KT else (a2s, ha)
                        if n % 2 == 0 and n >= 8:
                            pe.wait_ge(*seen.at(n // 2 - 3))
                        last = nc.tensor.matmul(K.ps[4 + n // 2 % 4][:, n % 2 * T:n % 2 * T + T],
                                                w[:, n % KT * P:n % KT * P + P], x[:, :], start=True, stop=True)
                        if n % 2:
                            last.then_inc(*hi.up())
                    for tt in range(TT):
                        for h in range(2):
                            o = K.ps[2 * tt + h][:, :]
                            nc.tensor.matmul(o, hg[:, tt * P:(tt + 1) * P], g2a[:, h * 512:(h + 1) * 512],
                                             start=True, stop=False)
                            last = nc.tensor.matmul(o, hg2[:, tt * P:(tt + 1) * P], g2b[:, h * 512:(h + 1) * 512],
                                                    start=False, stop=True)
                    last.then_inc(*low.up())

                @block.scalar
                def _(act):
                    for b, (o, f) in enumerate(((hw, ACT.Tanh), (ha, ACT.Copy), (hg, ACT.Sigmoid),
                                                (hg2, ACT.Sigmoid))):
                        act.wait_ge(*low.at(b + 1))
                        nc.scalar.activation(o[:, :], K.ps[b][0:o.shape[0], 0:T], f).then_inc(*mid.up())
                    for n in range(2 * KT):
                        if n % 2 == 0:
                            act.wait_ge(*hi.at(n // 2 + 1))
                        dst, bias = (dec, w0) if n < KT else (aT, a0)
                        j = n % KT
                        last = nc.scalar.activation(dst[:, j, :], K.ps[4 + n // 2 % 4][:, n % 2 * T:n % 2 * T + T],
                                                    ACT.Sigmoid, bias=bias[:, j:j + 1])
                        if n % 2:
                            last.then_inc(*seen.up())
                    act.wait_ge(*seen.now())

                @block.vector
                def _(dve):
                    dve.wait_ge(*low.at(5))
                    for tt in range(TT):
                        for h in range(2):
                            last = nc.vector.tensor_copy(gr[:, tt, h * 512:(h + 1) * 512], K.ps[2 * tt + h][:, :])
                    K.v(dve, last)

                @block.sync
                def _(sp):
                    K.stream(sp)

        yr = h1
        with ExitStack() as st2:
            S2 = lambda *s: scratch(K, st2, *s)
            At, Rt, G, E, Bt, Kt = (unit(n, j=KT) for n in range(6, 12))
            AR = units[:, 12:14, :].rearrange("p u (j c a t) -> p (u j) c a t", j=KT // 2, c=TT, a=2)
            bones, hsel, bonus = S2([P, P], [P, 2], [P, TT, 16])
            level, dstate = S2([P, 7, P], [P, KT])
            tri, = S2([P, 4, P])
            Brow, Krow, Sbd = S2([P, D], [P, D], [P, KT, P])
            load_phase(K, [(bones[:, :], i["head_block"]), (hsel[:, :], i["head_pick"]), (level[:, :, :], i["levels"]),
                           (tri[:, :, :], i["tri"])])

            sq, nm, gs, ex, rk, ask, given = K.sig(7)
            b3 = lambda c: bc(c.unsqueeze(2), [P, KT, T])
            with K.begin() as block:
                @block.vector
                def _(dve):
                    V = nc.vector
                    K.v(dve, V.tensor_tensor(At[:, :, :], kT[:, :, :], b3(k_k), ALU.mult))
                    K.v(dve, V.tensor_tensor(E[:, :, :], At[:, :, :], At[:, :, :], ALU.mult), sq)
                    K.v(dve, V.tensor_scalar(dec[:, :, :], dec[:, :, :], -math.exp(-0.5), None, ALU.mult))
                    for j in range(KT):
                        for c in range(TT):
                            t = slice(c * P, c * P + P)
                            last = V.tensor_tensor_scan(G[:, j, t], K.ones[:, :], dec[:, j, t], 0.0, ALU.mult, ALU.add)
                    K.v(dve, last)
                    G4 = G[:, :, :].rearrange("p j (c t) -> p (j c) t", c=TT)
                    K.v(dve, V.tensor_copy(Sbd[:, 0, 0:2 * KT], G4[:, :, P - 1]))
                    K.v(dve, V.scalar_tensor_tensor(G4, bc(Sbd[:, 0, 0:2 * KT].unsqueeze(2), [P, 2 * KT, P]), -0.5, G4,
                                                    ALU.mult, ALU.add), gs)
                    dve.wait_ge(*nm.at(1))
                    K.v(dve, V.tensor_scalar(E[:, :, :], aT[:, :, :], -1.0, None, ALU.add))
                    K.v(dve, V.tensor_tensor(E[:, :, :], E[:, :, :], b3(k_a), ALU.mult))
                    K.v(dve, V.tensor_scalar(E[:, :, :], E[:, :, :], 1.0, None, ALU.add))
                    K.v(dve, V.tensor_tensor(kT[:, :, :], kT[:, :, :], E[:, :, :], ALU.mult))
                    K.v(dve, V.tensor_tensor(E[:, :, :], rT[:, :, :], kT[:, :, :], ALU.mult))
                    K.v(dve, V.tensor_tensor(E[:, :, :], E[:, :, :], b3(r_k), ALU.mult), rk)
                    for b in range(4):
                        rsqrt(K, dve, V.tensor_scalar(K.ps[b][:, :], K.ps[b][:, :], 1e-24, None, ALU.max),
                              K.ps[b][:, :], (ask, given))
                        pair = At[:, 2 * b:2 * b + 2, :].rearrange("p j t -> p (j t)")
                        K.v(dve, V.tensor_tensor(pair, pair, K.ps[b][:, :], ALU.mult))
                    K.v(dve, V.tensor_tensor(Bt[:, :, :], At[:, :, :], aT[:, :, :], ALU.mult))
                    dve.wait_ge(*nm.at(2))
                    K.v(dve, V.tensor_copy(bonus[:, :, :], K.ps[4][:, 0:32].rearrange("p (t h) -> p t h", t=TT)))
                    A4, R4 = (AR[:, :, :, n, :].rearrange("p j c t -> p (j c) t") for n in range(2))
                    flat = lambda x: x[:, :, :].rearrange("p j (c t) -> p (j c) t", c=TT)
                    dve.wait_ge(*ex.at(3))
                    K.v(dve, V.tensor_tensor(dstate[:, :], dstate[:, :], Sbd[:, 1, 0:KT], ALU.mult))
                    K.v(dve, V.tensor_tensor(R4, flat(rT), flat(Rt), ALU.mult))
                    K.v(dve, V.scalar_tensor_tensor(A4, flat(At), -1.0, flat(dec), ALU.mult, ALU.mult))
                    K.v(dve, V.tensor_tensor(Bt[:, :, :], Bt[:, :, :], Kt[:, :, :], ALU.mult))
                    K.v(dve, V.tensor_tensor(Kt[:, :, :], kT[:, :, :], Kt[:, :, :], ALU.mult))

                @block.tensor
                def _(pe):
                    pe.wait_ge(*sq.at(1))
                    for j in range(KT):
                        last = nc.tensor.matmul(K.ps[j // 2][:, j % 2 * T:j % 2 * T + T], bones[:, :], E[:, j, :],
                                                start=True, stop=True)
                    last.then_inc(*nm.up())
                    pe.wait_ge(*rk.at(1))
                    for tt in range(TT):
                        for j in range(KT):
                            last = nc.tensor.matmul(K.ps[4][:, tt * 16 + 2 * j:tt * 16 + 2 * j + 2],
                                                    E[:, j, tt * P:(tt + 1) * P], hsel[:, :], start=True, stop=True)
                    last.then_inc(*nm.up())

                @block.scalar
                def _(act):
                    act.wait_ge(*gs.at(1))
                    K.a(act, nc.scalar.activation(Rt[:, :, :], G[:, :, :], ACT.Exp), ex)
                    K.a(act, nc.scalar.activation(Kt[:, :, :], G[:, :, :], ACT.Exp, scale=-1.0), ex)
                    gend = G[:, :, :].rearrange("p j (c t) -> p j c t", c=TT)[:, :, :, P - 1]
                    K.a(act, nc.scalar.activation(dstate[:, :], gend[:, :, 0], ACT.Exp))
                    K.a(act, nc.scalar.activation(Sbd[:, 1, 0:KT], gend[:, :, 1], ACT.Exp))
                    act.wait_ge(*K.pool.at(1))
                    K.a(act, nc.scalar.activation(dec[:, :, :], dec[:, :, :], ACT.Exp), ex)
                    roots(K, act, ask, given, [K.ps[b][:, :] for b in range(4)])

                @block.gpsimd
                def _(pool):
                    pool.wait_ge(*gs.at(1))
                    K.g(pool, nc.gpsimd.tensor_tensor(dec[:, :, :], G[:, :, :], dec[:, :, :], ALU.subtract))

                @block.sync
                def _(sp):
                    K.stream(sp)

            to_cols(K, lambda tt, j: Bt[:, j, 0:P], lambda j, tt: Brow[:, j * P:(j + 1) * P], KT, tts=1)
            to_cols(K, lambda tt, j: Kt[:, j, 0:P], lambda j, tt: Krow[:, j * P:(j + 1) * P], KT, tts=1)
            gram = units[:, 2:6, :].rearrange("p u (h a t) -> p (u h) a t", h=4, a=4)
            Dm, DT, Wm, Lo = (unit(n, "p (h t) -> p h t", h=16) for n in (6, 7, 8, 9))
            X, SA = units[:, 9, 0:D], units[:, 8, 0:D]
            for c in range(TT):
                wkv_chunk(K, c, AR, Bt, Kt, vr, gram, Dm, DT, Wm, Lo, X, SA, tri, level, Brow, Krow, Sbd,
                          dstate, bones, yr)

            gg, gb = units[:, 10, 0:D], units[:, 10, D:2 * D]
            tmp = units[:, 11, 0:D].rearrange("p (n w) -> p n w", n=16)
            st_, mv, rs = S2([P, 12], [P, 16, 2], [P, 16])
            load_phase(K, [(gg[:, :], i["gn_g"].partition_broadcast(P)), (gb[:, :], i["gn_b"].partition_broadcast(P))])
            ask, given = K.sig(2)
            with K.begin() as block:
                @block.scalar
                def _(act):
                    roots(K, act, ask, given, [rs[:, :]] * TT)

                @block.vector
                def _(dve):
                    for tt in range(TT):
                        y = yr[:, tt, :].rearrange("p (n w) -> p n w", n=16)
                        layer_norm(K, dve, y, y, (st_, mv, rs), gg[:, :], gb[:, :], 64, 16, 64e-5, (ask, given))
                        v3 = vr[:, tt, :].rearrange("p (n w) -> p n w", n=16)
                        K.v(dve, nc.vector.tensor_tensor(tmp[:, :, :], v3, bc(bonus[:, tt, :].unsqueeze(2), [P, 16, 64]),
                                                         ALU.mult))
                        K.v(dve, nc.vector.tensor_tensor(y, y, tmp[:, :, :], ALU.add))
                        K.v(dve, nc.vector.tensor_tensor(yr[:, tt, :], yr[:, tt, :], gr[:, tt, :], ALU.mult))

                @block.sync
                def _(sp):
                    K.stream(sp)

        yT, xr = unit(2, j=KT), unit(3, j=TT)
        to_cols(K, lambda tt, j: yr[:, tt, j * P:(j + 1) * P], lambda j, tt: yT[:, j, tt * P:(tt + 1) * P], KT)
        load_phase(K, [(xr, i["x_rows"])])
        project_residual_norm(K, st, yT, KT, xr, h1, 0)


def project_residual_norm(K, st, hT, kts, x, out, n):
    nc, i = K.nc, K.i
    g, b, st_, mv, rs = scratch(K, st, [P, D], [P, D], [P, 12], [P, 1, 2], [P, 1])
    load_phase(K, [(g[:, :], i["ln_g"][n].partition_broadcast(P)), (b[:, :], i["ln_b"][n].partition_broadcast(P))])

    sqrts = K.sig(2)

    def evac(dve, tt, h, o):
        s = slice(h * 512, h * 512 + 512)
        return nc.vector.scalar_tensor_tensor(out[:, tt, s], x[:, tt, s], ALPHA, o, ALU.mult, ALU.add)

    def after(dve):
        for tt in range(TT):
            z = out[:, tt, :].unsqueeze(1)
            layer_norm(K, dve, z, z, (st_, mv, rs), g[:, :], b[:, :], D, 1, 1e-5, sqrts)

    linear_rows(K, hT, range(kts), evac, after=after, sqrts=sqrts, root_bufs=[rs[:, :]] * TT)


def wkv_chunk(K, c, AR, Bt, Kt, vr, gram, Dm, DT, Wm, Lo, X, SA, tri, level, Brow, Krow, Sbd, dstate, bones, yr):
    nc = K.nc
    V = nc.vector
    tok = slice(c * P, c * P + P)
    made, kept = K.sig(2)
    with K.begin() as block:
        @block.tensor
        def _(pe):
            for h in range(16):
                j, r = h // 2, slice(64 * (h % 2), 64 * (h % 2) + 64)
                if h >= 8:
                    pe.wait_ge(*kept.at(h - 7))
                rhs = AR[r, j, c, :, :].rearrange("p a t -> p (a t)")
                nc.tensor.matmul(K.ps[h % 8][:, 0:256], Bt[r, j, tok], rhs, start=True, stop=True)
                nc.tensor.matmul(K.ps[h % 8][:, 256:512], Kt[r, j, tok], rhs, start=True,
                                 stop=True).then_inc(*made.up())

        @block.vector
        def _(dve):
            K.v(dve, V.memset(gram[:, :, :, :], 0.0))
            for m in (Dm, DT):
                K.v(dve, V.tensor_copy(m[:, :, :], bc(K.ident[:, :].unsqueeze(1), [P, 16, P])))
            for h in range(16):
                dve.wait_ge(*made.at(h + 1))
                V.copy_predicated(gram[:, h, :, :].rearrange("p a t -> p (a t)"),
                                  tri[:, :, :].bitcast(U32).rearrange("p a t -> p (a t)"),
                                  K.ps[h % 8][:, :]).then_inc(*kept.up())
            dve.wait_ge(*kept.now())

        @block.sync
        def _(sp):
            K.stream(sp)

    lo, w, wc, dd, dn = K.sig(5)
    with K.begin() as block:
        @block.vector
        def _(dve):
            for l in range(7):
                for q in range(4):
                    if l:
                        dve.wait_ge(*w.at(4 * l))
                    K.v(dve, V.tensor_tensor(Lo[:, 4 * q:4 * q + 4, :], gram[:, 4 * q:4 * q + 4, 0, :],
                                             bc(level[:, l, :].unsqueeze(1), [P, 4, P]), ALU.mult), lo)
                for q in range(4):
                    dve.wait_ge(*dd.at(4 * l + q + 1))
                    o = q % 2 * 2
                    for m, b in ((Dm, 4 + o), (DT, 5 + o)):
                        f = m[:, 4 * q:4 * q + 4, :].rearrange("p a t -> p (a t)")
                        last = V.tensor_tensor(f, f, K.ps[b][:, :], ALU.add)
                    K.v(dve, last, dn)

        @block.tensor
        def _(pe):
            for l in range(7):
                for q in range(4):
                    pe.wait_ge(*lo.at(4 * l + q + 1))
                    if l:
                        pe.wait_ge(*dn.at(4 * (l - 1) + q + 1))
                        pe.wait_ge(*wc.at(4 * (l - 1) + q + 1))
                    for n in range(4):
                        h = 4 * q + n
                        last = nc.tensor.matmul(K.ps[q][:, n * P:(n + 1) * P], Lo[:, h, :], Dm[:, h, :],
                                                start=True, stop=True)
                    last.then_inc(*w.up())
                for q in range(4):
                    pe.wait_ge(*wc.at(4 * l + q + 1))
                    if 4 * l + q >= 2:
                        pe.wait_ge(*dn.at(4 * l + q - 1))
                    for n in range(4):
                        h = 4 * q + n
                        nc.tensor.matmul(K.ps[4 + q % 2 * 2][:, n * P:(n + 1) * P], DT[:, h, :], Wm[:, h, :],
                                         start=True, stop=True)
                        last = nc.tensor.matmul(K.ps[5 + q % 2 * 2][:, n * P:(n + 1) * P], Wm[:, h, :], DT[:, h, :],
                                                start=True, stop=True)
                    last.then_inc(*dd.up())

        @block.scalar
        def _(act):
            for l in range(7):
                for q in range(4):
                    act.wait_ge(*w.at(4 * l + q + 1))
                    if l:
                        act.wait_ge(*dd.at(4 * (l - 1) + q + 1))
                    nc.scalar.activation(Wm[:, 4 * q:4 * q + 4, :].rearrange("p a t -> p (a t)"), K.ps[q][:, :],
                                         ACT.Copy).then_inc(*wc.up())
            act.wait_ge(*wc.now())

        @block.sync
        def _(sp):
            K.stream(sp)

    vt = lambda h: vr[:, c, h * 64:(h + 1) * 64]
    p1, p2 = K.sig(2)
    with K.begin() as block:
        @block.tensor
        def _(pe):
            def accumulate(bank0, parts, state):
                for b in range(2):
                    first = True
                    for h in range(8 * b, 8 * b + 8):
                        o = K.ps[bank0 + b][:, h % 8 * 64:h % 8 * 64 + 64]
                        for lhsT, rhs in parts(h):
                            last = nc.tensor.matmul(o, lhsT, rhs, start=first, stop=(b == 1 and not state and h == 15),
                                                    skip_group_check=True)
                            first = False
                    if state is not None:
                        for j in range(4 * b, 4 * b + 4):
                            last = nc.tensor.matmul(K.ps[bank0 + b][:, j % 4 * P:j % 4 * P + P], AR[:, j, c, state, :],
                                                    Sbd[:, j, :], start=False, stop=True, skip_group_check=True)
                last.then_inc(*p1.up())

            accumulate(0, lambda h: [(gram[:, h, 2, :], vt(h))], 0 if c else None)
            pe.wait_ge(*p2.at(1))
            accumulate(2, lambda h: [(DT[:, h, :], X[:, h * 64:(h + 1) * 64])], None)
            pe.wait_ge(*p2.at(2))
            accumulate(4, lambda h: [(gram[:, h, 1, :], SA[:, h * 64:(h + 1) * 64]), (gram[:, h, 3, :], vt(h))],
                       1 if c else None)
            if c == 0:
                for b in range(2):
                    for j in range(4 * b, 4 * b + 4):
                        o = K.ps[6 + b][:, j % 4 * P:j % 4 * P + P]
                        nc.tensor.matmul(o, Brow[:, j * P:(j + 1) * P], SA[:, j * P:(j + 1) * P],
                                         start=True, stop=False)
                        last = nc.tensor.matmul(o, Krow[:, j * P:(j + 1) * P], vr[:, c, j * P:(j + 1) * P],
                                                start=False, stop=True)
                last.then_inc(*p1.up())

        @block.vector
        def _(dve):
            for n, dst in enumerate((X[:, :], SA[:, :], yr[:, c, :])):
                dve.wait_ge(*p1.at(n + 1))
                for b in range(2):
                    last = V.tensor_copy(dst[:, b * 512:(b + 1) * 512], K.ps[2 * n + b][:, :])
                K.v(dve, last, p2)
            if c == 0:
                dve.wait_ge(*p1.at(4))
                for j in range(KT):
                    K.v(dve, V.scalar_tensor_tensor(Sbd[:, j, :], K.ps[6 + j // 4][:, j % 4 * P:j % 4 * P + P],
                                                    dstate[:, j:j + 1], bones[:, :], ALU.mult, ALU.mult))

        @block.sync
        def _(sp):
            K.stream(sp)


def attention(K, st, units, scale, outs):
    nc = K.nc
    V = nc.vector
    S, Pm, PT = scratch(K, st, *[[P, 2, 512]] * 3)
    mx, sm = scratch(K, st, [P, 2], [P, 2])
    scored, ready, expd, normed, turned, copied, applied, oread = K.sig(8)
    N = len(units)
    with K.begin() as block:
        @block.tensor
        def _(pe):
            def turn(u):
                pe.wait_ge(*normed.at(u + 1))
                if u >= 2:
                    pe.wait_ge(*copied.at(u - 1))
                nk = units[u][1].shape[1]
                for b in range(nk // P):
                    last = nc.tensor.transpose(K.ps[2 + u % 2][:, b * P:(b + 1) * P], Pm[:, u % 2, b * P:(b + 1) * P],
                                               K.ident[:, :])
                last.then_inc(*turned.up())

            def apply(u):
                pe.wait_ge(*copied.at(u + 1))
                g = u // 4
                if u % 4 == 0 and g >= 2:
                    pe.wait_ge(*oread.at(g - 1))
                vs = units[u][2]
                r, c = 64 * (u % 4 // 2), P * (u % 2)
                for b, v in enumerate(vs):
                    last = nc.tensor.matmul(K.ps[4 + g % 2][r:r + 64, c:c + P], v, PT[:, u % 2, b * P:(b + 1) * P],
                                            start=(b == 0), stop=(b == len(vs) - 1))
                last.then_inc(*applied.up())

            for u in range(N + 2):
                if u < N:
                    q, k = units[u][:2]
                    if u >= 2:
                        pe.wait_ge(*expd.at(u - 1))
                    nc.tensor.matmul(K.ps[u % 2][:, 0:k.shape[1]], q, k, start=True, stop=True)\
                        .then_inc(*scored.up())
                if 1 <= u <= N:
                    turn(u - 1)
                if u >= 2:
                    apply(u - 2)

        @block.vector
        def _(dve):
            def norm(u):
                nk = units[u][1].shape[1]
                dve.wait_ge(*expd.at(u + 1))
                K.v(dve, V.reciprocal(sm[:, u % 2:u % 2 + 1], sm[:, u % 2:u % 2 + 1]))
                V.tensor_scalar(Pm[:, u % 2, 0:nk], Pm[:, u % 2, 0:nk], sm[:, u % 2:u % 2 + 1], None,
                                ALU.mult).then_inc(*normed.up())

            for u in range(N + 3):
                if u < N:
                    nk, bias = units[u][1].shape[1], units[u][3]
                    s = K.ps[u % 2][:, 0:nk]
                    dve.wait_ge(*scored.at(u + 1))
                    if u >= 2:
                        dve.wait_ge(*expd.at(u - 1))
                    if bias is not None:
                        nb = bias.shape[1]
                        K.v(dve, V.scalar_tensor_tensor(S[:, u % 2, 0:nb], K.ps[u % 2][:, 0:nb], scale, bias,
                                                        ALU.mult, ALU.add))
                        if nb < nk:
                            K.v(dve, V.tensor_scalar(S[:, u % 2, nb:nk], K.ps[u % 2][:, nb:nk], scale, None, ALU.mult))
                        s = S[:, u % 2, 0:nk]
                    K.v(dve, V.reduce_max(mx[:, u % 2:u % 2 + 1], s, AX))
                    K.v(dve, V.tensor_scalar(mx[:, u % 2:u % 2 + 1], mx[:, u % 2:u % 2 + 1],
                                             -scale if bias is None else -1.0, None, ALU.mult), ready)
                if 1 <= u <= N:
                    norm(u - 1)
                if u >= 3 and (u - 3) % 4 == 3:
                    g = (u - 3) // 4
                    dve.wait_ge(*applied.at(4 * g + 4))
                    V.tensor_copy(outs[g], K.ps[4 + g % 2][:, 0:256]).then_inc(*oread.up())
            dve.wait_ge(*oread.now())

        @block.scalar
        def _(act):
            def copy(u):
                nk = units[u][1].shape[1]
                act.wait_ge(*turned.at(u + 1))
                if u >= 2:
                    act.wait_ge(*applied.at(u - 1))
                nc.scalar.activation(PT[:, u % 2, 0:nk], K.ps[2 + u % 2][:, 0:nk], ACT.Copy).then_inc(*copied.up())

            for u in range(N + 1):
                if u < N:
                    nk, bias = units[u][1].shape[1], units[u][3]
                    act.wait_ge(*ready.at(u + 1))
                    if u >= 2:
                        act.wait_ge(*turned.at(u - 1))
                    s, f = (K.ps[u % 2][:, 0:nk], scale) if bias is None else (S[:, u % 2, 0:nk], 1.0)
                    K.a(act, nc.scalar.activation(Pm[:, u % 2, 0:nk], s, ACT.Exp, bias=mx[:, u % 2:u % 2 + 1],
                                                  scale=f, accum_out=sm[:, u % 2:u % 2 + 1]), expd)
                if u >= 1:
                    copy(u - 1)

        @block.sync
        def _(sp):
            K.stream(sp)


def causal_attention(K, h2, h3):
    i = K.i
    with ExitStack() as st:
        hT, qT, kT, oT = scratch(K, st, *[[P, KT, T]] * 4)
        vr, mask = scratch(K, st, [P, TT, D], [P, TT, T])
        load_phase(K, [(mask[:, :, :], i["causal"])])
        to_cols(K, lambda tt, j: h2[:, tt, j * P:(j + 1) * P], lambda j, tt: hT[:, j, tt * P:(tt + 1) * P], KT)
        keep = lambda dst: lambda act, c, h, o: K.nc.scalar.activation(dst[:, 2 * c + h, :], o, ACT.Copy)
        linear_cols(K, [(hT[:, :, :], 4, keep(qT)), (hT[:, :, :], 4, keep(kT))])
        linear_rows(K, hT, range(KT), lambda dve, tt, h, o: K.nc.vector.tensor_copy(
            vr[:, tt, h * 512:(h + 1) * 512], o))
        units = []
        for h in range(16):
            r, j = slice(64 * (h % 2), 64 * (h % 2) + 64), h // 2
            for qt in range(TT):
                nk = (qt + 1) * P
                units.append((qT[r, j, qt * P:(qt + 1) * P], kT[r, j, 0:nk],
                              [vr[:, b, h * 64:(h + 1) * 64] for b in range(qt + 1)], mask[:, qt, 0:nk]))
        with ExitStack() as st2:
            attention(K, st2, units, 0.125, [oT[:, j, :] for j in range(KT)])
        project_residual_norm(K, st, oT, KT, h2, h3, 2)


def moe(K, h3, h4):
    nc, i = K.nc, K.i
    V = nc.vector
    HALF, STEPS = 2 * NE, FE // 2 // 256
    PER = 3 * STEPS
    with ExitStack() as st:
        hT, acc = scratch(K, st, [P, KT, T], [P, TT, D])
        hid, sg = scratch(K, st, [P, 2, 2, T], [P, 2, 2, T])
        rt, lg, cmp_, eq, rank, gates, e8, m8, nm, low = scratch(
            K, st, [P, KT, NE], [P, TT, NE], [P, TT, NE, NE], [P, TT, NE, NE], [P, TT, NE], [P, TT, HALF],
            [P, TT, NE], [P, TT, NE], [P, TT], [P, NE, NE])
        g, b, st_, mv, rs = scratch(K, st, [P, D], [P, D], [P, 12], [P, 1, 2], [P, 1])
        load_phase(K, [(rt[:, :, :], i["moe_router"]), (low[:, :, :], i["earlier"]),
                       (g[:, :], i["ln_g"][3].partition_broadcast(P)), (b[:, :], i["ln_b"][3].partition_broadcast(P))])
        to_cols(K, lambda tt, j: h3[:, tt, j * P:(j + 1) * P], lambda j, tt: hT[:, j, tt * P:(tt + 1) * P], KT)

        done, req, got = K.sig(3)
        with K.begin() as block:
            @block.tensor
            def _(pe):
                for tt in range(TT):
                    for k in range(KT):
                        last = nc.tensor.matmul(K.ps[0][:, tt * NE:(tt + 1) * NE], hT[:, k, tt * P:(tt + 1) * P],
                                                rt[:, k, :], start=(k == 0), stop=(k == KT - 1))
                last.then_inc(*done.up())

            @block.vector
            def _(dve):
                dve.wait_ge(*done.at(1))
                K.v(dve, V.tensor_copy(lg[:, :, :], K.ps[0][:, 0:TT * NE].rearrange("p (t e) -> p t e", t=TT)))
                for tt in range(TT):
                    K.v(dve, V.max(m8[:, tt, :], lg[:, tt, :]))
                    K.v(dve, V.tensor_scalar(e8[:, tt, :], lg[:, tt, :], m8[:, tt, 0:1], None, ALU.subtract))
                    me = bc(lg[:, tt, :].unsqueeze(2), [P, NE, NE])
                    other = bc(lg[:, tt, :].unsqueeze(1), [P, NE, NE])
                    K.v(dve, V.tensor_tensor(cmp_[:, tt, :, :], other, me, ALU.is_gt))
                    K.v(dve, V.tensor_tensor(eq[:, tt, :, :], other, me, ALU.is_equal))
                    K.v(dve, V.tensor_tensor(eq[:, tt, :, :], eq[:, tt, :, :], low[:, :, :], ALU.mult))
                    K.v(dve, V.tensor_tensor(cmp_[:, tt, :, :], cmp_[:, tt, :, :], eq[:, tt, :, :], ALU.add))
                    K.v(dve, V.reduce_sum(rank[:, tt, :], cmp_[:, tt, :, :], AX))
                    K.v(dve, V.tensor_scalar(rank[:, tt, :], rank[:, tt, :], 1.5, None, ALU.is_lt))
                K.v(dve, V.memset(nm[:, :], 0.0), req)
                dve.wait_ge(*got.at(1))
                K.v(dve, V.tensor_tensor(e8[:, :, :], e8[:, :, :], rank[:, :, :], ALU.mult))
                K.v(dve, V.reduce_sum(nm[:, :], e8[:, :, :], AX))
                K.v(dve, V.reciprocal(nm[:, :], nm[:, :]))
                for q in range(2):
                    K.v(dve, V.tensor_tensor(gates[:, :, :].rearrange("p t (e q) -> p t e q", q=2)[:, :, :, q],
                                             e8[:, :, :], bc(nm[:, :].unsqueeze(2), [P, TT, NE]), ALU.mult))
                K.v(dve, V.tensor_scalar(acc[:, :, :], h3[:, :, :], ALPHA, None, ALU.mult))

            @block.scalar
            def _(act):
                act.wait_ge(*req.at(1))
                K.a(act, nc.scalar.activation(e8[:, :, :], e8[:, :, :], ACT.Exp), got)

            @block.sync
            def _(sp):
                K.stream(sp)

        assert K.issued == K.taken + R and PER % R == 0
        first = K.taken
        wave = PER // R
        gated, hready, dread, ask, given = K.sig(5)
        with K.begin() as block:
            u0, g0, h0, d0 = K.used.n, gated.n, hready.n, dread.n
            assert min(u0, g0, h0, d0) > 0

            @block.tensor
            def _(pe):
                with pe.Fori(0, HALF) as m:
                    at = [0]

                    def chunk():
                        n = at[0]
                        at[0] += 1
                        pe.wait_ge(K.landed[(first + n) % R], m * (16 * wave) + 16 * ((first + n) // R + 1))
                        return K.ring[:, (first + n) % R, :]

                    def down(c):
                        w = chunk().rearrange("p (k n) -> p k n", k=2)
                        pe.wait_ge(hready.h, m * STEPS + (h0 + c + 1))
                        if c == 0:
                            pe.wait_ge(dread.h, m + d0)
                        for q in range(2):
                            for tt in range(TT):
                                for h in range(2):
                                    last = nc.tensor.matmul(K.ps[tt * 2 + h][:, :],
                                                            hid[:, c % 2, q, tt * P:(tt + 1) * P],
                                                            w[:, q, h * 512:(h + 1) * 512],
                                                            start=(c == 0 and q == 0), stop=(c == STEPS - 1 and q == 1))
                        last.then_inc(K.used.h, 1)

                    for c in range(STEPS):
                        pe.wait_ge(hready.h, m * STEPS + (h0 + max(c - 1, 0)))
                        for s in range(2):
                            w = chunk().rearrange("p (k n) -> p k n", k=KT)
                            for h in range(2):
                                for k in range(KT):
                                    last = nc.tensor.matmul(K.ps[4 + c % 2 * 2 + s][:, h * T:(h + 1) * T],
                                                            w[:, k, h * P:(h + 1) * P], hT[:, k, :],
                                                            start=(k == 0), stop=(k == KT - 1))
                            last.then_inc(K.used.h, 1)
                        if c >= 1:
                            down(c - 1)
                    down(STEPS - 1)

            gate_at = [1 if c == 0 else 3 * c for c in range(STEPS)]
            up_at = [n + 1 for n in gate_at]
            down_at = [3 * c + 5 for c in range(STEPS)]
            down_at[-1] = PER

            @block.scalar
            def _(act):
                with act.Fori(0, HALF) as m:
                    for c in range(STEPS):
                        act.wait_ge(K.used.h, m * PER + (u0 + gate_at[c]))
                        act.wait_ge(hready.h, m * STEPS + (h0 + max(c - 1, 0)))
                        nc.scalar.activation(sg[:, c % 2, :, :].rearrange("p h t -> p (h t)"),
                                             K.ps[4 + c % 2 * 2][:, :], ACT.Silu).then_inc(gated.h, 1)

            @block.vector
            def _(dve):
                with dve.Fori(0, HALF) as m:
                    for c in range(STEPS):
                        dve.wait_ge(K.used.h, m * PER + (u0 + up_at[c]))
                        dve.wait_ge(gated.h, m * STEPS + (g0 + c + 1))
                        if c >= 2:
                            dve.wait_ge(K.used.h, m * PER + (u0 + down_at[c - 2]))
                        V.tensor_tensor(hid[:, c % 2, :, :].rearrange("p h t -> p (h t)"),
                                        sg[:, c % 2, :, :].rearrange("p h t -> p (h t)"),
                                        K.ps[5 + c % 2 * 2][:, :], ALU.mult).then_inc(hready.h, 1)
                    dve.wait_ge(K.used.h, m * PER + (u0 + PER))
                    for tt in range(TT):
                        for h in range(2):
                            a = acc[:, tt, h * 512:(h + 1) * 512]
                            last = V.scalar_tensor_tensor(a, K.ps[tt * 2 + h][:, :], gates[:, tt, bass.ds(m, 1)], a,
                                                          ALU.mult, ALU.add)
                    last.then_inc(dread.h, 1)
                    dve.wait_ge(dread.h, m + (d0 + 1))

            @block.sync
            def _(sp):
                def fill(m, n):
                    sp.wait_ge(K.used.h, m * PER + (first + n + 1))
                    sp.dma_start(K.ring[:, (first + n) % R, :], i["moe_w"][m * PER + (n + R)] if isinstance(m, int) else
                                 i["moe_w"][bass.ds(m * PER + (n + R), 1)].rearrange("o p c -> p (o c)"))\
                        .then_inc(K.landed[(first + n) % R], 16)

                with sp.Fori(0, HALF - 1) as m:
                    for n in range(PER):
                        fill(m, n)
                for n in range(PER - R):
                    fill(HALF - 1, n)
                K.taken += HALF * PER
                K.issued = K.taken
                K.stream(sp)
            K.used.n += HALF * PER
            gated.n += HALF * STEPS
            hready.n += HALF * STEPS
            dread.n += HALF

        sqrts = K.sig(2)
        with K.begin() as block:
            @block.vector
            def _(dve):
                for tt in range(TT):
                    layer_norm(K, dve, acc[:, tt, :].unsqueeze(1), h4[:, tt, :].unsqueeze(1), (st_, mv, rs),
                               g[:, :], b[:, :], D, 1, 1e-5, sqrts)

            @block.scalar
            def _(act):
                roots(K, act, *sqrts, [rs[:, :]] * TT)


FC = 2816
T2 = 2 * T
EPS = 1e-6


def adaln(K, coef, grow):
    nc, i = K.nc, K.i
    V = nc.vector
    with ExitStack() as st:
        cT, rep, ab, ng = scratch(K, st, [P, KT, 2], [P, KT, 2, P], [P, 2, 4, KT], [P, 2, 4, KT])
        grb, gng = scratch(K, st, [P, 4, D], [P, 4, D])
        load_phase(K, [(cT[:, :, :], i["c_cols"]), (ab[:, :, :, :], i["ada_b_cols"]), (ng[:, :, :, :], i["norm_g_cols"])]
                   + [(grb[:, n, :], i["ada_b_gates"][n].partition_broadcast(P)) for n in range(4)]
                   + [(gng[:, n, :], i["norm_g_gates"][n].partition_broadcast(P)) for n in range(4)])
        hot, sil, gread = K.sig(3)
        with K.begin() as block:
            @block.scalar
            def _(act):
                K.a(act, nc.scalar.activation(cT[:, :, :], cT[:, :, :], ACT.Silu), sil)

            @block.tensor
            def _(pe):
                pe.wait_ge(*hot.at(1))
                for l in range(2):
                    for p in range(6):
                        if p in (2, 5) and (l or p == 5):
                            pe.wait_ge(*gread.at(2 * l + (p == 5)))
                        for c in range(4):
                            w = K.chunk(pe).rearrange("p (k n) -> p k n", k=KT)
                            if p in (2, 5):
                                for who in range(2 - l):
                                    for k in range(KT):
                                        last = nc.tensor.matmul(
                                            K.ps[1 + who * 2 + c // 2][:, c % 2 * 256:c % 2 * 256 + 256],
                                            rep[:, k, who, :], w[:, k, :], start=(k == 0), stop=(k == KT - 1))
                            else:
                                for h in range(2):
                                    n = (p if p < 2 else p - 1) * KT + 2 * c + h
                                    for k in range(KT):
                                        last = nc.tensor.matmul(K.ps[5 * l][:, 2 * n:2 * n + 2],
                                                                w[:, k, h * P:(h + 1) * P], cT[:, k, :],
                                                                start=(k == 0), stop=(k == KT - 1))
                            last.then_inc(*K.used.up())

            @block.vector
            def _(dve):
                dve.wait_ge(*sil.at(1))
                K.v(dve, V.tensor_copy(rep[:, :, :, :], bc(cT[:, :, :].unsqueeze(3), [P, KT, 2, P])), hot)
                row = 0
                for l in range(2):
                    for g in range(2):
                        dve.wait_ge(*K.used.at(24 * l + 12 * (g + 1)))
                        for who in range(2 - l):
                            for b in range(2):
                                s = slice(b * 512, b * 512 + 512)
                                K.v(dve, V.tensor_tensor(grow[:, row, s], K.ps[1 + who * 2 + b][:, :],
                                                         grb[:, 2 * l + g, s], ALU.add))
                            if who == 1 - l:
                                K.v(dve, V.memset(K.junk[:, 0:1], 0.0), gread)
                            K.v(dve, V.tensor_tensor(grow[:, row, :], grow[:, row, :], gng[:, 2 * l + g, :], ALU.mult))
                            row += 1
                    m = K.ps[5 * l][:, 0:64].rearrange("p (q j w) -> p q j w", q=4, w=2)
                    for n in range(2):
                        for who in range(2):
                            K.v(dve, V.tensor_tensor(coef[:, l, n, who, 1, :], m[:, 2 * n, :, who], ab[:, l, 2 * n, :],
                                                     ALU.add))
                            s = coef[:, l, n, who, 0, :]
                            K.v(dve, V.tensor_tensor(s, m[:, 2 * n + 1, :, who], ab[:, l, 2 * n + 1, :], ALU.add))
                            K.v(dve, V.scalar_tensor_tensor(s, s, 1.0, ng[:, l, 2 * n, :], ALU.add, ALU.mult))

            @block.sync
            def _(sp):
                K.stream(sp)


def rms_phase(K, st, srcs, finish):
    nc = K.nc
    width = srcs[0].shape[1]
    junk, ss = scratch(K, st, [P, width], [P, len(srcs)])
    sqd, ask, given = K.sig(3)
    with K.begin() as block:
        @block.scalar
        def _(act):
            for n, src in enumerate(srcs):
                K.a(act, nc.scalar.activation(junk[:, :], src, ACT.Square, accum_out=ss[:, n:n + 1]), sqd)
            roots(K, act, ask, given, [ss[:, n:n + 1] for n in range(len(srcs))])

        @block.vector
        def _(dve):
            for n in range(len(srcs)):
                dve.wait_ge(*sqd.at(n + 1))
                r = ss[:, n:n + 1]
                rsqrt(K, dve, nc.vector.tensor_scalar(r, r, 1.0 / width, EPS, ALU.mult, ALU.add), r, (ask, given))
                finish(dve, n, r)

        @block.sync
        def _(sp):
            K.stream(sp)


def norm_to_cols(K, x, xn, hT, tts, coef):
    V, nc = K.nc.vector, K.nc
    with ExitStack() as st:
        rms_phase(K, st, [x[:, tt, :] for tt in range(tts)], lambda dve, n, r: K.v(dve, V.tensor_scalar(
            xn[:, n, :], x[:, n, :], r, None, ALU.mult)))
    to_cols(K, lambda tt, j: xn[:, tt, j * P:(j + 1) * P], None, KT, tts=tts,
            evac=lambda j, tt, src: nc.scalar.activation(
                hT[:, j, tt * P:(tt + 1) * P], src, ACT.Identity, bias=coef[:, tt // TT, 1, j:j + 1],
                scale=coef[:, tt // TT, 0, j:j + 1]))


def gated_residual(K, x, y, tts, gates):
    V = K.nc.vector
    with ExitStack() as st:
        def fin(dve, n, r):
            K.v(dve, V.scalar_tensor_tensor(y[:, n, :], y[:, n, :], r, gates[n // TT], ALU.mult, ALU.mult))
            K.v(dve, V.tensor_tensor(x[:, n, :], x[:, n, :], y[:, n, :], ALU.add))

        rms_phase(K, st, [y[:, tt, :] for tt in range(tts)], fin)


def keep_rows(K, y):
    return lambda dve, tt, h, o: K.nc.vector.tensor_copy(y[:, tt, h * 512:(h + 1) * 512], o)


def conv_ffn(K, x, l, tts, coef, gates):
    i = K.i
    with ExitStack() as st:
        hT, hid, cw, cb = scratch(K, st, [P, KT, tts * P], [P, FC // P, tts * P], [P, 2 * FC // P, 3], [P, 2 * FC // P])
        load_phase(K, [(cw[:, :, :], i["ffn_conv_w"][l]), (cb[:, :], i["ffn_conv_b"][l])])
        xn = hid[:, 0:KT, :].rearrange("p j t -> p (j t)").rearrange("p (t d) -> p t d", d=D)
        norm_to_cols(K, x, xn, hT, tts, coef)
        with ExitStack() as st2:
            gated_hidden(K, st2, hT[:, :, :], hid, FC // 256, conv=(cw, cb))
        y = hT[:, :, :].rearrange("p j t -> p (j t)").rearrange("p (t d) -> p t d", d=D)
        linear_rows(K, hid, range(FC // P), keep_rows(K, y), tts=tts)
        gated_residual(K, x, y, tts, gates)


def linear_rows512(K, x, outs):
    nc = K.nc
    read, = K.sig(1)
    with K.begin() as block:
        @block.tensor
        def _(pe):
            for m in range(len(outs)):
                if m >= 2:
                    pe.wait_ge(*read.at(m - 1))
                for c in range(2):
                    w = K.chunk(pe).rearrange("p (k n) -> p k n", k=4)
                    for k in range(4):
                        for tt in range(4):
                            last = nc.tensor.matmul(K.ps[m % 2 * 4 + tt][:, :],
                                                    x[:, 4 * c + k, tt * P:(tt + 1) * P], w[:, k, :],
                                                    start=(c == 0 and k == 0), stop=(c == 1 and k == 3))
                    last.then_inc(*K.used.up())

        @block.vector
        def _(dve):
            for m, o in enumerate(outs):
                dve.wait_ge(*K.used.at(2 * m + 2))
                for tt in range(4):
                    last = nc.vector.tensor_copy(o[:, tt, :], K.ps[m % 2 * 4 + tt][:, :])
                K.v(dve, last, read)

        @block.sync
        def _(sp):
            K.stream(sp)


def even_layer(K, x4, coef, grow):
    nc, i = K.nc, K.i
    V = nc.vector
    with ExitStack() as st:
        units, = scratch(K, st, [P, 11, CH])
        two = lambda n, pat="p u (j t) -> p (u j) t", **kw: units[:, n:n + 2, :].rearrange(pat, **(kw or {"t": T2}))
        one = lambda n, **kw: units[:, n, :].rearrange("p (j t) -> p j t", **(kw or {"t": T2}))
        yT, hT = two(0), two(2)
        naq, nak, nav = one(4), one(5), one(6)
        raw, mlv, mlo = two(7), one(9), one(10)
        cw, cb, gw, gb = scratch(K, st, [P, KT, 3], [P, KT], [P, KT, 16], [P, 16])
        load_phase(K, [(cw[:, :, :], i["ev_conv_w"]), (cb[:, :], i["ev_conv_b"]), (gw[:, :, :], i["ev_w_gates"]),
                       (gb[:, :], i["ev_gate_b"].partition_broadcast(P))])
        norm_to_cols(K, x4, two(4, "p u (a d) -> p (u a) d", d=D), hT, 4, coef[:, 0, 0])
        keep = lambda dst: lambda act, c, h, o: nc.scalar.activation(dst[:, 2 * c + h, :], o, ACT.Copy)
        linear_cols(K, [(hT, 2, keep(naq)), (hT, 2, keep(nak)), (hT, 4, keep(raw))])
        linear_rows512(K, hT, [nav, mlv, mlo])
        G8, lf, tmp, bb, tot, u8 = scratch(K, st, [P, 4, 2, 2, 4], *[[P, 4, 2, 4]] * 5)
        tri, mask, window = scratch(K, st, [P, 2, P], [P, 2, P], [P, 64])
        load_phase(K, [(window[:, :], i["window"]), (tri[:, :, :], i["ml_tri"]), (mask[:, :, :], i["ml_mask"])])
        SEQ = ((2, 3, 0, 1), (3, 2, 1, 0))
        pg, ve, ae, pb = K.sig(4)
        with K.begin() as block:
            @block.tensor
            def _(pe):
                for tt in range(4):
                    for k in range(KT):
                        last = nc.tensor.matmul(K.ps[0][:, tt * 16:(tt + 1) * 16], hT[:, k, tt * P:(tt + 1) * P],
                                                gw[:, k, :], start=(k == 0), stop=(k == KT - 1))
                last.then_inc(*pg.up())
                pe.wait_ge(*ve.at(3))
                for d in range(2):
                    nc.tensor.matmul(K.ps[1][:, d * 16:(d + 1) * 16], tri[:, d, :], lf[:, :, d, :], start=True, stop=True)
                nc.tensor.matmul(K.ps[1][:, 32:64], K.ones[:, :], lf[:, :, :, :].rearrange("p s d h -> p (s d h)"),
                                 start=True, stop=True).then_inc(*pb.up())

            @block.vector
            def _(dve):
                dve.wait_ge(*pg.at(1))
                for d in range(2):
                    for s in range(4):
                        c = SEQ[d][s] * 16 + 8 * d
                        K.v(dve, V.tensor_tensor(G8[:, s, d, :, :].rearrange("p a h -> p (a h)"), K.ps[0][:, c:c + 8],
                                                 gb[:, 8 * d:8 * d + 8], ALU.add))
                f = G8[:, :, :, 1, :]
                K.v(dve, V.tensor_scalar(tmp[:, :, :, :], f, -1.0, None, ALU.mult))
                K.v(dve, V.tensor_tensor(tmp[:, :, :, :], tmp[:, :, :, :], f, ALU.min), ve)
                dve.wait_ge(*ae.at(1))
                K.v(dve, V.tensor_scalar(tmp[:, :, :, :], tmp[:, :, :, :], 1.0, None, ALU.add), ve)
                dve.wait_ge(*ae.at(2))
                K.v(dve, V.tensor_scalar(lf[:, :, :, :], f, 0.0, None, ALU.min))
                K.v(dve, V.tensor_tensor(lf[:, :, :, :], lf[:, :, :, :], tmp[:, :, :, :], ALU.subtract), ve)
                dve.wait_ge(*pb.at(1))
                for d in range(2):
                    K.v(dve, V.tensor_copy(bb[:, :, d, :], K.ps[1][:, d * 16:(d + 1) * 16].rearrange(
                        "p (s h) -> p s h", s=4)))
                K.v(dve, V.tensor_copy(tot[:, :, :, :].rearrange("p s d h -> p (s d h)"), K.ps[1][:, 32:64]))
                K.v(dve, V.tensor_tensor(u8[:, :, :, :], G8[:, :, :, 0, :], bb[:, :, :, :], ALU.subtract))

            @block.scalar
            def _(act):
                act.wait_ge(*ve.at(1))
                K.a(act, nc.scalar.activation(tmp[:, :, :, :], tmp[:, :, :, :], ACT.Exp), ae)
                act.wait_ge(*ve.at(2))
                K.a(act, nc.scalar.activation(tmp[:, :, :, :], tmp[:, :, :, :], ACT.Ln), ae)

            @block.sync
            def _(sp):
                K.stream(sp)

        neighbourhood(K, naq, nak, nav, units[:, 2:4, :].rearrange("p u (a k) -> p (u a) k", k=T), window[:, :],
                      yT)

        cqk = two(2)
        cv, = K.sig(1)
        with K.begin() as block:
            @block.vector
            def _(dve):
                for j in range(KT):
                    K.v(dve, V.tensor_scalar(cqk[:, j, :], raw[:, j, :], cw[:, j, 1:2], cb[:, j:j + 1], ALU.mult, ALU.add))
                    for tap, dst, src in ((0, slice(1, T), slice(0, T - 1)), (2, slice(0, T - 1), slice(1, T))):
                        o = cqk[:, j, :].rearrange("p (q t) -> p q t", q=2)[:, :, dst]
                        r = raw[:, j, :].rearrange("p (q t) -> p q t", q=2)[:, :, src]
                        K.v(dve, V.scalar_tensor_tensor(o, r, cw[:, j, tap:tap + 1], o, ALU.mult, ALU.add),
                            cv if tap else None)

            @block.scalar
            def _(act):
                for j in range(KT):
                    act.wait_ge(*cv.at(j + 1))
                    K.a(act, nc.scalar.activation(cqk[:, j, :], cqk[:, j, :], ACT.Silu))
                K.a(act, nc.scalar.activation(cqk[:, 0:4, :], cqk[:, 0:4, :], ACT.Copy, scale=P ** -0.5))
                K.a(act, nc.scalar.activation(mlo[:, :, :], mlo[:, :, :], ACT.Sigmoid))

            @block.sync
            def _(sp):
                K.stream(sp)
        krow, hf, hb = one(4), one(5), one(6)
        to_cols(K, lambda tt, j: cqk[:, 4 + j, tt * P:(tt + 1) * P], lambda j, tt: krow[:, tt, j * P:(j + 1) * P], 4, tts=4)
        mlstm(K, cqk, krow, mlv, (hf, hb), one(7, t=P), one(8, t=P), bb, tot, u8, mask, SEQ)

        mg, st_, mv, rs = scratch(K, st, [P, 512], [P, 12], [P, 4, 2], [P, 4])
        load_phase(K, [(mg[:, :], i["ev_ml_norm_g"].partition_broadcast(P))])
        sqrts = K.sig(2)
        with K.begin() as block:
            @block.vector
            def _(dve):
                K.v(dve, V.tensor_tensor(hf, hf, hb, ALU.add))
                K.v(dve, V.tensor_tensor(hf, hf, mlo, ALU.mult))
                for tt in range(4):
                    z = hf[:, tt, :].rearrange("p (n w) -> p n w", n=4)
                    layer_norm(K, dve, z, z, (st_, mv, rs), mg[:, :], None, P, 4, EPS, sqrts)

            @block.scalar
            def _(act):
                roots(K, act, *sqrts, [rs[:, :]] * 4)

            @block.sync
            def _(sp):
                K.stream(sp)
        to_cols(K, lambda tt, j: hf[:, tt, j * P:(j + 1) * P], lambda j, tt: yT[:, 4 + j, tt * P:(tt + 1) * P], 4, tts=4)
        y = two(2, "p u (a d) -> p (u a) d", d=D)
        linear_rows(K, yT, range(KT), keep_rows(K, y), tts=4)
        gated_residual(K, x4, y, 4, [grow[:, 0, :], grow[:, 1, :]])


def neighbourhood(K, q, k, v, bias, window, yT):
    nc, i = K.nc, K.i
    b5 = bias.rearrange("p (h q) (r c) -> p h q r c", q=TT, c=64)
    with K.begin() as block:
        @block.scalar
        def _(act):
            for qr in range(4):
                for h in range(8):
                    act.dma_start(b5[64 * (qr % 2):64 * (qr % 2) + 64, h, qr // 2, :, :],
                                  i["rpb"][h, 7 - qr:11 - qr, :, :].rearrange("r q k -> q r k"))\
                        .then_inc(*K.load.up(16))
            act.wait_ge(*K.load.now())

        @block.vector
        def _(dve):
            dve.wait_ge(*K.load.now())
            K.v(dve, nc.vector.tensor_tensor(bias.rearrange("p u (r c) -> p (u r) c", c=64),
                                             bias.rearrange("p u (r c) -> p (u r) c", c=64),
                                             bc(window.unsqueeze(1), [P, 64, 64]), ALU.add))

        @block.sync
        def _(sp):
            K.stream(sp)
    units, outs = [], []
    for j in range(4):
        for ctx in range(2):
            for h in (2 * j, 2 * j + 1):
                r = slice(64 * (h % 2), 64 * (h % 2) + 64)
                for qt in range(TT):
                    c = (2 * ctx + qt) * P
                    keys = range(2 * ctx, 4)
                    units.append((q[r, j, c:c + P], k[r, j, keys[0] * P:T2], [v[:, b, h * 64:(h + 1) * 64] for b in keys],
                                  None if ctx else bias[:, 2 * h + qt, :]))
            outs.append(yT[:, j, ctx * T:(ctx + 1) * T])
    with ExitStack() as st:
        attention(K, st, units, 0.125, outs)


def mlstm(K, cqk, krow, vrow, hout, ua, ub, bb, tot, u8, mask, SEQ):
    nc = K.nc
    V = nc.vector
    diag, W = ua[:, 0:8, :], ua[:, 8:16, :]
    qkw, qkT = ub[:, 0:8, :], ub[:, 8:16, :]
    with ExitStack() as st:
        Ct, Kw, args, sm = scratch(K, st, [P, 8, P], [P, 8, P], [P, 4, 8], [P, 8, 8])
        n_st, m_st, umax, mu, top, den, neg, rden = (sm[:, n, :] for n in range(8))
        sU, pU, sW, aW, pQ, vQ, pT, aT, pN, vK, pS, vS = K.sig(12)
        b3 = lambda a, n=8: bc(a.unsqueeze(2), [P, n, P])
        bank = lambda b: K.ps[b][:, :].rearrange("p (h s) -> p h s", h=4)
        with K.begin() as block:
            @block.tensor
            def _(pe):
                for k in range(4):
                    pe.wait_ge(*sU.at(k + 1))
                    for d in range(2):
                        last = nc.tensor.matmul(K.ps[d][:, :], K.ones[:, :],
                                                diag[:, 4 * d:4 * d + 4, :].rearrange("p h s -> p (h s)"),
                                                start=True, stop=True)
                    last.then_inc(*pU.up())
                    if k:
                        pe.wait_ge(*vS.at(k))
                    unit = [(u, u // 4, u % 4, slice(SEQ[u // 4][k] * P, SEQ[u // 4][k] * P + P), SEQ[u // 4][k])
                            for u in range(8)]
                    for u, d, h, t, _ in unit:
                        last = nc.tensor.matmul(K.ps[2 + d][:, h * P:(h + 1) * P], cqk[:, h, t], cqk[:, 4 + h, t],
                                                start=True, stop=True)
                    last.then_inc(*pQ.up())
                    pe.wait_ge(*vQ.at(k + 1))
                    for u, d, h, t, _ in unit:
                        last = nc.tensor.transpose(K.ps[d][:, h * P:(h + 1) * P], qkw[:, u, :], K.ident[:, :])
                    last.then_inc(*pT.up())
                    pe.wait_ge(*aT.at(k + 1))
                    for u, d, h, t, tt in unit:
                        nc.tensor.matmul(K.ps[4 + d][:, h * P:(h + 1) * P], qkT[:, u, :], vrow[:, tt, h * P:(h + 1) * P],
                                         start=True, stop=True)
                        nc.tensor.matmul(K.ps[6 + d][:, h * P:(h + 1) * P], cqk[:, h, t], Ct[:, u, :],
                                         start=True, stop=True)
                        last = nc.tensor.matmul(K.ps[2][:, u:u + 1], cqk[:, h, t], n_st[:, u:u + 1],
                                                start=True, stop=True)
                    last.then_inc(*pN.up())
                    pe.wait_ge(*vK.at(k + 1))
                    for u, d, h, t, tt in unit:
                        nc.tensor.matmul(K.ps[d][:, h * P:(h + 1) * P], Kw[:, u, :], vrow[:, tt, h * P:(h + 1) * P],
                                         start=True, stop=True)
                        last = nc.tensor.matmul(K.ps[3][:, u:u + 1], Kw[:, u, :], K.ones[:, 0:1], start=True, stop=True)
                    last.then_inc(*pS.up())

            @block.vector
            def _(dve):
                K.v(dve, V.memset(Ct[:, :, :], 0.0))
                K.v(dve, V.memset(sm[:, :, :], 0.0))
                for k in range(4):
                    flat = lambda a: a[:, k, :, :].rearrange("p d h -> p (d h)")
                    b8, t8, w8 = flat(bb), flat(tot), flat(u8)
                    K.v(dve, V.tensor_tensor(diag, bc(K.ident[:, :].unsqueeze(1), [P, 8, P]), b3(w8), ALU.mult), sU)
                    dve.wait_ge(*pU.at(k + 1))
                    for d in range(2):
                        K.v(dve, V.reduce_max(umax[:, 4 * d:4 * d + 4], bank(d), AX))
                        K.v(dve, V.tensor_tensor(W[:, 4 * d:4 * d + 4, :], bank(d),
                                                 bc(mask[:, d, :].unsqueeze(1), [P, 4, P]), ALU.add))
                    K.v(dve, V.reduce_max(mu, W, AX))
                    K.v(dve, V.tensor_tensor(mu, mu, m_st, ALU.max))
                    K.v(dve, V.tensor_tensor(top, umax, m_st, ALU.max))
                    K.v(dve, V.tensor_tensor(W, W, b3(mu), ALU.subtract))
                    K.v(dve, V.tensor_tensor(args[:, 0, :], m_st, mu, ALU.subtract))
                    K.v(dve, V.scalar_tensor_tensor(args[:, 1, :], b8, -1.0, mu, ALU.mult, ALU.subtract))
                    K.v(dve, V.tensor_tensor(args[:, 2, :], m_st, top, ALU.subtract))
                    K.v(dve, V.tensor_tensor(args[:, 3, :], w8, top, ALU.subtract), sW)
                    dve.wait_ge(*aW.at(k + 1))
                    dve.wait_ge(*pQ.at(k + 1))
                    for d in range(2):
                        last = V.tensor_tensor(qkw[:, 4 * d:4 * d + 4, :], bank(2 + d), W[:, 4 * d:4 * d + 4, :], ALU.mult)
                    K.v(dve, last, vQ)
                    for d in range(2):
                        last = V.tensor_tensor(Kw[:, 4 * d:4 * d + 4, :],
                                               krow[:, SEQ[d][k], :].rearrange("p (h e) -> p h e", h=4),
                                               b3(args[:, 3, 4 * d:4 * d + 4], 4), ALU.mult)
                    K.v(dve, last, vK)
                    K.v(dve, V.reduce_sum(den, qkw, AX))
                    dve.wait_ge(*pN.at(k + 1))
                    K.v(dve, V.tensor_tensor(neg, K.ps[2][:, 0:8], args[:, 0, :], ALU.mult))
                    K.v(dve, V.tensor_tensor(den, den, neg, ALU.add))
                    K.v(dve, V.tensor_scalar(neg, den, -1.0, None, ALU.mult))
                    K.v(dve, V.tensor_tensor(den, den, neg, ALU.max))
                    K.v(dve, V.tensor_tensor(den, den, args[:, 1, :], ALU.max))
                    K.v(dve, V.reciprocal(rden, den))
                    for d in range(2):
                        o = hout[d][:, SEQ[d][k], :].rearrange("p (h e) -> p h e", h=4)
                        s = slice(4 * d, 4 * d + 4)
                        K.v(dve, V.tensor_tensor(o, bank(6 + d), b3(args[:, 0, s], 4), ALU.mult))
                        K.v(dve, V.tensor_tensor(o, o, bank(4 + d), ALU.add))
                        K.v(dve, V.tensor_tensor(o, o, b3(rden[:, s], 4), ALU.mult))
                    K.v(dve, V.tensor_tensor(Ct[:, :, :], Ct[:, :, :], b3(args[:, 2, :]), ALU.mult))
                    K.v(dve, V.tensor_tensor(n_st, n_st, args[:, 2, :], ALU.mult))
                    K.v(dve, V.tensor_tensor(m_st, t8, top, ALU.add))
                    dve.wait_ge(*pS.at(k + 1))
                    for d in range(2):
                        K.v(dve, V.tensor_tensor(Ct[:, 4 * d:4 * d + 4, :], Ct[:, 4 * d:4 * d + 4, :], bank(d), ALU.add))
                    K.v(dve, V.tensor_tensor(n_st, n_st, K.ps[3][:, 0:8], ALU.add), vS)

            @block.scalar
            def _(act):
                for k in range(4):
                    act.wait_ge(*sW.at(k + 1))
                    K.a(act, nc.scalar.activation(W, W, ACT.Exp))
                    K.a(act, nc.scalar.activation(args[:, :, :], args[:, :, :], ACT.Exp), aW)
                    act.wait_ge(*pT.at(k + 1))
                    if k:
                        act.wait_ge(*pN.at(k))
                    for d in range(2):
                        last = nc.scalar.activation(qkT[:, 4 * d:4 * d + 4, :], bank(d), ACT.Copy)
                    K.a(act, last, aT)

            @block.sync
            def _(sp):
                K.stream(sp)


def odd_layer(K, x4, coef, grow):
    nc, i = K.nc, K.i
    V = nc.vector
    H, QK = 16, 96
    with ExitStack() as st:
        kT, qT, vr = scratch(K, st, [P, H, T2], [P, H, T], [P, 4, D])
        cqT, ckvT, oT, g = scratch(K, st, [P, 2, T], [P, T2], [P, KT, T], [P, 3])
        xn = kT[:, 0:8, :].rearrange("p j t -> p (j t)").rearrange("p (t d) -> p t d", d=D)
        hT = kT[:, 8:16, :]
        with ExitStack() as st1:
            wkv, wq = scratch(K, st1, [P, KT, 160], [P, KT, T])
            ckv, cq, rope, t4 = scratch(K, st1, [P, 4, 160], [P, TT, T], [P, TT, 2, 2, 8], [P, 4, 2, 8])
            load_phase(K, [(wkv[:, :, :], i["od_w_dkv"]), (wq[:, :, :], i["od_w_dq"]), (g[:, :], i["od_norm_g"]),
                           (rope[:, :, :, :, :], i["rope"])])
            norm_to_cols(K, x4, xn, hT, 4, coef[:, 1, 0])
            low, = K.sig(1)
            with K.begin() as block:
                @block.tensor
                def _(pe):
                    for tt in range(4):
                        for w, b, n in ((wkv, tt, 160), (wq, 4 + tt, T))[:2 if tt < TT else 1]:
                            for k in range(KT):
                                last = nc.tensor.matmul(K.ps[b][:, 0:n], hT[:, k, tt * P:(tt + 1) * P], w[:, k, :],
                                                        start=(k == 0), stop=(k == KT - 1))
                    last.then_inc(*low.up())

                @block.vector
                def _(dve):
                    dve.wait_ge(*low.at(1))
                    for tt in range(4):
                        K.v(dve, V.tensor_copy(ckv[:, tt, :], K.ps[tt][:, 0:160]))
                        if tt < TT:
                            K.v(dve, V.tensor_copy(cq[:, tt, :], K.ps[4 + tt][:, 0:T]))
                            rotate(K, dve, ckv[:, tt, 128:160].unsqueeze(1), rope[:, tt], t4)

                @block.sync
                def _(sp):
                    K.stream(sp)
            for t, n, w in ((ckv, 4, P), (cq, TT, T)):
                with ExitStack() as s2:
                    rms_phase(K, s2, [t[:, tt, 0:w] for tt in range(n)], lambda dve, m, r, t=t, w=w: K.v(
                        dve, V.tensor_scalar(t[:, m, 0:w], t[:, m, 0:w], r, None, ALU.mult)))
            to_cols(K, lambda tt, j: ckv[:, tt, 0:P], None, 1, tts=4, evac=lambda j, tt, src: nc.scalar.activation(
                ckvT[:, tt * P:(tt + 1) * P], src, ACT.Copy, scale=g[:, 2:3]))
            to_cols(K, lambda tt, j: cq[:, tt, j * P:(j + 1) * P], None, 2, evac=lambda j, tt, src: nc.scalar.activation(
                cqT[:, j, tt * P:(tt + 1) * P], src, ACT.Copy, scale=g[:, j:j + 1]))
            to_cols(K, lambda tt, j: ckv[:, tt, P:160], None, 1, tts=4, width=32,
                    evac=lambda j, tt, src: nc.scalar.activation(
                        kT[64:96, :, tt * P:(tt + 1) * P], bc(src.unsqueeze(1), [32, H, P]), ACT.Copy))
        with ExitStack() as st1:
            wuk, wuv, wuq, qr = scratch(K, st1, [P, D], [P, D], [P, 2, H * QK], [P, TT, H * QK])
            rope, t4 = scratch(K, st1, [P, TT, 2, 2, 8], [P, 4, H * 8])
            load_phase(K, [(wuk[:, :], i["od_w_uk"]), (wuv[:, :], i["od_w_uv"]), (wuq[:, :, :], i["od_w_uq"]),
                           (rope[:, :, :, :, :], i["rope"])])
            kd, kr, vd, qd = K.sig(4)
            with K.begin() as block:
                @block.tensor
                def _(pe):
                    for h in range(H):
                        if h >= 2:
                            pe.wait_ge(*kr.at(h - 1))
                        nc.tensor.matmul(K.ps[h % 2][0:64, :], wuk[:, h * 64:(h + 1) * 64], ckvT[:, :],
                                         start=True, stop=True).then_inc(*kd.up())
                    for tt in range(4):
                        for b in range(2):
                            n = 2 * tt + b
                            if n >= 3:
                                pe.wait_ge(*vd.at(n - 2))
                            nc.tensor.matmul(K.ps[2 + n % 3][:, :], ckvT[:, tt * P:(tt + 1) * P],
                                             wuv[:, b * 512:(b + 1) * 512], start=True, stop=True).then_inc(*qd.up())
                    for tt in range(TT):
                        for b in range(3):
                            n = 3 * tt + b
                            if n >= 3:
                                pe.wait_ge(*vd.at(8 + n - 2))
                            for k in range(2):
                                last = nc.tensor.matmul(K.ps[5 + b][:, :], cqT[:, k, tt * P:(tt + 1) * P],
                                                        wuq[:, k, b * 512:(b + 1) * 512], start=(k == 0), stop=(k == 1))
                            last.then_inc(*qd.up())

                @block.scalar
                def _(act):
                    for h in range(H):
                        act.wait_ge(*kd.at(h + 1))
                        nc.scalar.activation(kT[0:64, h, :], K.ps[h % 2][0:64, :], ACT.Copy).then_inc(*kr.up())
                    act.wait_ge(*kr.now())

                @block.vector
                def _(dve):
                    for n in range(14):
                        dve.wait_ge(*qd.at(n + 1))
                        dst, src = ((vr[:, n // 2, n % 2 * 512:n % 2 * 512 + 512], 2 + n % 3) if n < 8 else
                                    (qr[:, (n - 8) // 3, (n - 8) % 3 * 512:(n - 8) % 3 * 512 + 512], 5 + (n - 8) % 3))
                        K.v(dve, V.tensor_copy(dst, K.ps[src][:, :]), vd)
                    for tt in range(TT):
                        rotate(K, dve, qr[:, tt, :].rearrange("p (h e) -> p h e", h=H)[:, :, 64:96], rope[:, tt],
                               t4[:, :, :])

                @block.sync
                def _(sp):
                    K.stream(sp)
            to_cols(K, lambda tt, j: qr[:, tt, j * QK:(j + 1) * QK], lambda j, tt: qT[0:QK, j, tt * P:(tt + 1) * P], H,
                    width=QK)
        units = [(qT[0:QK, h, qt * P:(qt + 1) * P], kT[0:QK, h, :], [vr[:, b, h * 64:(h + 1) * 64] for b in range(4)], None)
                 for h in range(H) for qt in range(TT)]
        with ExitStack() as st1:
            attention(K, st1, units, QK ** -0.5, [oT[:, j, :] for j in range(KT)])
        y = qT[:, 0:8, :].rearrange("p j t -> p (j t)").rearrange("p (t d) -> p t d", d=D)
        linear_rows(K, oT, range(KT), keep_rows(K, y))
        gated_residual(K, x4, y, TT, [grow[:, 4, :]])


def rotate(K, dve, x, table, tmp):
    V = K.nc.vector
    n = x.shape[1]
    for ax in range(2):
        lo, hi = x[:, :, 16 * ax:16 * ax + 8], x[:, :, 16 * ax + 8:16 * ax + 16]
        cos, sin = (bc(table[:, f, ax, :].unsqueeze(1), [P, n, 8]) for f in range(2))
        t = [tmp[:, m].rearrange("p a b -> p (a b)")[:, 0:8 * n] if len(tmp.shape) == 4 else tmp[:, m, 0:8 * n]
             for m in range(4)]
        t = [a.rearrange("p (n e) -> p n e", n=n) for a in t]
        for m, (a, b) in enumerate(((lo, cos), (hi, sin), (lo, sin), (hi, cos))):
            K.v(dve, V.tensor_tensor(t[m], a, b, ALU.mult))
        K.v(dve, V.tensor_tensor(lo, t[0], t[1], ALU.subtract))
        K.v(dve, V.tensor_tensor(hi, t[2], t[3], ALU.add))


def second_stack(K, x4):
    coef, grow = scratch(K, K.ctx, [P, 2, 2, 2, 2, KT], [P, 6, D])
    load_phase(K, [(x4[:, TT:2 * TT, :], K.i["ctx_rows"])])
    adaln(K, coef, grow)
    even_layer(K, x4, coef, grow)
    conv_ffn(K, x4, 0, 4, coef[:, 0, 1], [grow[:, 2, :], grow[:, 3, :]])
    odd_layer(K, x4, coef, grow)
    conv_ffn(K, x4, 1, TT, coef[:, 1, 1], [grow[:, 5, :]])


def store_rows(K, rows):
    with K.begin() as block:
        @block.sync
        def _(sp):
            sp.dma_start(K.out.rearrange("o (t p) d -> p (o t) d", p=P), rows[:, 0:TT, :]).then_inc(*K.load.up(16))
            sp.wait_ge(*K.load.now())


def build(nc, i, out):
    with ExitStack() as ctx:
        K = Kern(nc, ctx, i, out)
        plan = K.plan
        chunks = lambda name, *r: plan.extend(i[name][n] for n in range(*(r or (i[name].shape[0],))))
        chunks("w_rkv_cols")
        chunks("w_rkv_rows")
        chunks("rwkv_w_out")
        chunks("ffn_w_in")
        chunks("ffn_w_down")
        chunks("moba_qk")
        chunks("moba_v")
        chunks("moba_o")
        chunks("moe_w")
        chunks("ada_w")
        chunks("ev_cols")
        chunks("ev_rows")
        chunks("ev_w_out")
        chunks("ffn_up", 0, 22)
        chunks("ffn_down", 0, 11)
        chunks("od_w_o")
        chunks("ffn_up", 22, 44)
        chunks("ffn_down", 11, 22)
        x4 = ctx.enter_context(nc.sbuf_tensor("x4", [P, 2 * TT, D], F32))
        ha, hb = x4[:, 0:TT, :], x4[:, TT:2 * TT, :]
        constants(K)
        rwkv(K, hb)
        with ExitStack() as st:
            hT, hid = scratch(K, st, [P, KT, T], [P, FF // P, T])
            to_cols(K, lambda tt, j: hb[:, tt, j * P:(j + 1) * P], lambda j, tt: hT[:, j, tt * P:(tt + 1) * P], KT)
            gated_hidden(K, st, hT[:, :, :], hid, FF // 256)
            project_residual_norm(K, st, hid, FF // P, hb, ha, 1)
        causal_attention(K, ha, hb)
        moe(K, hb, ha)
        second_stack(K, x4)
        store_rows(K, x4)


def by_cols(np, w):
    k, n = w.shape
    return np.ascontiguousarray(w.reshape(k // P, P, n // 256, 256).transpose(2, 1, 0, 3)).reshape(n // 256, P, -1)


def by_rows(np, w):
    k, n = w.shape
    return np.ascontiguousarray(w.reshape(k // 256, 2, P, n).transpose(0, 2, 1, 3)).reshape(k // 256, P, -1)


def interleave(np, *ws):
    return np.stack(ws, 1).reshape(-1, *ws[0].shape[1:])


def col(np, v):
    return np.ascontiguousarray(np.moveaxis(v.reshape(*v.shape[:-1], v.shape[-1] // P, P), -1, 0))


def rows_of(np, x):
    return np.ascontiguousarray(x.reshape(-1, P, x.shape[-1]).transpose(1, 0, 2))


def shape_constants(np):
    s, t = np.arange(P)[:, None], np.arange(P)[None, :]
    strict, incl = s < t, s <= t
    lv = np.stack([(s >> (l + 1) == t >> (l + 1)) & (s >> l != t >> l) for l in range(7)], 1)
    f = lambda a: np.ascontiguousarray(a.astype(np.float32))
    pos = np.arange(T)
    angle = np.stack([pos // 64, pos % 64], 1)[:, :, None].astype(np.float32) * (
        np.float32(10000.0) ** (-np.arange(8, dtype=np.float32) / 8))
    rope = np.stack([np.cos(angle), np.sin(angle)], 1).reshape(TT, P, 2, 2, 8).transpose(1, 0, 2, 3, 4)
    q, c = np.arange(P)[:, None] % 64, np.arange(64)[None, :]
    start = np.clip(q - 8, 0, 48)
    return {"rope": f(rope), "window": f(np.where((c >= start) & (c < start + 16), 0.0, NEG)),
            "ml_tri": f(np.stack([s <= t, s >= t], 1)),
            "ml_mask": f(np.stack([np.where(t <= s, 0.0, NEG), np.where(t >= s, 0.0, NEG)], 1)),
            "head_block": f(s // 64 == t // 64), "head_pick": f(s // 64 == np.arange(2)[None, :]),
            "levels": f(lv), "earlier": f(np.broadcast_to(np.arange(NE)[None, :] < np.arange(NE)[:, None], (P, NE, NE))),
            "causal": f(np.where(np.arange(T)[None, None, :] <= (np.arange(TT)[None, :, None] * P + s[:, :, None]),
                                 0.0, NEG)), "tri": f(np.stack([strict, incl, strict, incl], 1))}


def lay_out(np, a):
    o = shape_constants(np)
    rkv = a["rwkv_w_rkv"][0]
    o["w_rkv_cols"] = np.concatenate([by_cols(np, rkv[0]), by_cols(np, rkv[1])])
    o["w_rkv_rows"] = by_rows(np, rkv[2])
    o["rwkv_w_out"] = by_rows(np, a["rwkv_w_out"][0])
    o["ffn_w_in"] = interleave(np, by_cols(np, a["ffn_w_gate"][0]), by_cols(np, a["ffn_w_up"][0]))
    o["ffn_w_down"] = by_rows(np, a["ffn_w_down"][0])
    x = a["x"][0]
    o["x_rows"] = rows_of(np, x)
    o["x_cols"] = np.ascontiguousarray(x.T.reshape(KT, P, T).transpose(1, 0, 2))
    o["mu_cols"] = col(np, a["rwkv_mu"][0])
    o["rwkv_cols"] = np.ascontiguousarray(np.stack([col(np, v) for v in (
        a["rwkv_decay_w0"][0], a["rwkv_iclr_a0"][0], a["rwkv_k_k"][0], a["rwkv_k_a"][0],
        a["rwkv_r_k"][0].reshape(-1))], 1))
    tiles = lambda w: np.ascontiguousarray(w.reshape(KT, P, -1).transpose(1, 0, 2))
    o["decay_w1"], o["iclr_a1"], o["gate_g1"] = (tiles(a[k][0]) for k in ("rwkv_decay_w1", "rwkv_iclr_a1", "rwkv_gate_g1"))
    o["decay_w2"], o["iclr_a2"], o["gate_g2"] = (a[k][0] for k in ("rwkv_decay_w2", "rwkv_iclr_a2", "rwkv_gate_g2"))
    o["gn_g"], o["gn_b"] = a["rwkv_gn_g"][0], a["rwkv_gn_b"][0]
    o["ln_g"], o["ln_b"] = a["ln_g"].reshape(4, D), a["ln_b"].reshape(4, D)
    o["moba_qk"] = np.concatenate([by_cols(np, a["moba_w_q"][0]), by_cols(np, a["moba_w_k"])])
    o["moba_v"], o["moba_o"] = by_rows(np, a["moba_w_v"]), by_rows(np, a["moba_w_o"][0])
    steps = FE // 2 // 256
    order = [("g", 0), ("u", 0)]
    for c in range(1, steps):
        order += [("g", c), ("u", c), ("d", c - 1)]
    order.append(("d", steps - 1))
    moe = np.empty((2 * NE * 3 * steps, P, CH), np.float32)
    n = 0
    for e in range(NE):
        side = {"g": by_cols(np, a["moe_w_gate"][0, e]), "u": by_cols(np, a["moe_w_up"][0, e]),
                "d": by_rows(np, a["moe_w_down"][0, e])}
        for half in range(2):
            for kind, c in order:
                moe[n] = side[kind][half * steps + c]
                n += 1
    o["moe_w"] = moe
    o["moe_router"] = tiles(a["moe_router"][0])

    b = {k[:-2]: v for k, v in a.items() if k.endswith("_2")}
    o["ctx_rows"] = rows_of(np, b["ctx"][0])
    o["c_cols"] = np.stack([col(np, b["c"][0]), col(np, b["c_ctx"])], 2)
    o["ada_w"] = np.concatenate([by_cols(np, b["ada_w"][l]) for l in range(2)])
    ab = b["ada_b"].reshape(2, 6, D)
    o["ada_b_cols"], o["ada_b_gates"] = col(np, ab[:, [0, 1, 3, 4]]), ab[:, [2, 5]].reshape(4, D)
    o["norm_g_cols"], o["norm_g_gates"] = col(np, b["norm_g"]), b["norm_g"][:, [1, 3]].reshape(4, D)
    o["ffn_up"] = np.concatenate([interleave(np, by_cols(np, b["ffn_w_up"][l][:, FC:]), by_cols(np, b["ffn_w_up"][l][:, :FC]))
                                  for l in range(2)])
    o["ffn_down"] = np.concatenate([by_rows(np, b["ffn_w_down"][l]) for l in range(2)])
    o["ffn_conv_w"] = np.moveaxis(col(np, b["ffn_conv_w"]), (0, 1, 2, 3), (1, 0, 3, 2))
    o["ffn_conv_b"] = np.moveaxis(col(np, b["ffn_conv_b"]), 0, 1)
    w = b["ev_w_in"][0]
    rows512 = lambda m: m.reshape(2, 4, P, 512).transpose(0, 2, 1, 3).reshape(2, P, CH)
    o["ev_cols"] = np.concatenate([by_cols(np, w[:, 0:1024]), by_cols(np, w[:, 1536:2560])])
    o["ev_rows"] = np.concatenate([rows512(w[:, n:n + 512]) for n in (1024, 2560, 3072)])
    o["ev_w_gates"], o["ev_gate_b"] = tiles(w[:, 3584:3600]), b["ev_gate_b"][0]
    o["ev_w_out"] = by_rows(np, b["ev_w_out"][0])
    o["ev_conv_w"] = col(np, b["ev_conv_w"][0]).transpose(0, 2, 1)
    o["ev_conv_b"], o["ev_ml_norm_g"] = col(np, b["ev_conv_b"][0]), b["ev_ml_norm_g"][0]
    c = np.arange(64)
    o["rpb"] = b["ev_rpb"][0][:, :, np.clip(c[None, :] - c[:, None], -15, 15) + 15]
    o["od_w_dq"], o["od_w_dkv"] = tiles(b["od_w_dq"][0]), tiles(b["od_w_dkv"][0])
    o["od_norm_g"] = np.concatenate([col(np, b["od_q_norm_g"][0]), col(np, b["od_kv_norm_g"][0])], 1)
    o["od_w_uq"] = b["od_w_uq"][0].reshape(2, P, -1).transpose(1, 0, 2)
    ukv = b["od_w_ukv"][0].reshape(P, 16, 2, 64)
    o["od_w_uk"], o["od_w_uv"] = ukv[:, :, 0].reshape(P, D), ukv[:, :, 1].reshape(P, D)
    o["od_w_o"] = by_rows(np, b["od_w_o"][0])
    return o


def kernel(**inputs):
    import numpy as np
    import concourse.bacc as bacc
    from concourse.bass_utils import run_bass_kernel_spmd as run

    nc = bacc.Bacc("TRN2", target_bir_lowering=False, num_devices=1)
    arrays = {k: np.ascontiguousarray(v) for k, v in lay_out(np, {k: np.asarray(v) for k, v in inputs.items()}).items()}
    aps = {k: nc.dram_tensor(k, v.shape, mybir.dt.from_np(v.dtype), kind="ExternalInput").ap() for k, v in arrays.items()}
    out = nc.dram_tensor("result", (1, T, D), F32, kind="ExternalOutput").ap()
    build(nc, aps, out)
    return run(nc, [arrays], core_ids=[0]).results[0]["result"]
```

```python
import math
from contextlib import ExitStack

import concourse.bass as bass
from concourse import mybir

F32 = mybir.dt.float32
U32 = mybir.dt.uint32
F32R = mybir.dt.float32r
ALU = mybir.AluOpType
ACT = mybir.ActivationFunctionType
AX = mybir.AxisListType.X

P = 128
D = 1024
KT = D // P
T = 256
TT = T // P
CH = 2048
R = 7
FF = 2816
FE = 3584
NE = 8
ALPHA = 4.0 ** 0.25
NEG = -1e30


class Sig:

    def __init__(self, handle):
        self.h, self.n, self.base = handle, 0, 0

    def up(self, by=1):
        self.n += by
        return self.h, by

    def at(self, k):
        return self.h, self.base + k

    def now(self):
        return self.h, self.n


class Kern:

    def __init__(self, nc, ctx, ins, out):
        self.nc, self.ctx, self.i, self.out = nc, ctx, ins, out
        sem = lambda n: ctx.enter_context(nc.semaphore(n))
        sb = lambda n, s, dt=F32: ctx.enter_context(nc.sbuf_tensor(n, s, dt))
        self.ring = sb("weight_ring", [P, R, CH])
        self.landed = [sem(f"weights_landed{s}") for s in range(R)]
        self.used = Sig(sem("weights_used"))
        self.dve, self.act, self.pool = Sig(sem("dve_chain")), Sig(sem("act_chain")), Sig(sem("pool_chain"))
        self.free_sigs = [Sig(sem(f"signal{n}")) for n in range(14)]
        self.load = Sig(sem("small_loads"))
        self.moe_gated, self.moe_hid, self.moe_read = (Sig(sem(f"dense_{n}")) for n in ("gated", "hidden", "read"))
        self.moe_sigs = [Sig(sem(f"routed_{n}")) for n in (
            "picked", "gathered", "tokens", "picks", "gated", "hidden", "output", "scattered", "free")]
        self.moe_free = self.moe_sigs[-1]
        self.ps = [ctx.enter_context(nc.psum_tensor(f"bank{b}", [P, 512], F32)) for b in range(8)]
        self.plan, self.taken, self.issued = [], 0, 0
        self.ident = sb("ident", [P, P])
        self.ones = sb("ones", [P, P])
        self.junk = sb("junk", [P, 1])
        self.nphase, self.uniq = 0, 0

    def sig(self, n):
        out = self.free_sigs[:n]
        for s in out:
            s.base = s.n
        return out

    def begin(self):
        self.nphase += 1
        for s in (self.used, self.dve, self.act, self.pool, self.load):
            s.base = s.n
        self.used.base = self.taken
        return self.nc.Block(f"phase{self.nphase}", no_gpsimd_drain=True)

    def chunk(self, pe):
        n = self.taken
        self.taken += 1
        pe.wait_ge(self.landed[n % R], 16 * (n // R + 1))
        return self.ring[:, n % R, :]

    def stream(self, sp):
        while self.issued < min(self.taken + R, len(self.plan)):
            n = self.issued
            if n >= R:
                sp.wait_ge(self.used.h, n - R + 1)
            sp.dma_start(self.ring[:, n % R, :], self.plan[n]).then_inc(self.landed[n % R], 16)
            self.issued += 1

    def v(self, eng, ins, sig=None):
        s = sig or self.dve
        ins.then_inc(*s.up())
        eng.wait_ge(*s.now())

    def a(self, eng, ins, sig=None):
        s = sig or self.act
        ins.then_inc(*s.up())
        eng.wait_ge(*s.now())

    def g(self, eng, ins, sig=None):
        s = sig or self.pool
        ins.then_inc(*s.up())
        eng.wait_ge(*s.now())


def scratch(K, st, *shapes):
    K.uniq += 1
    return [st.enter_context(K.nc.sbuf_tensor(f"s{K.uniq}_{n}", list(s), F32)) for n, s in enumerate(shapes)]


def load(K, eng, dst, src):
    eng.dma_start(dst, src).then_inc(*K.load.up(16))


def bc(ap, shape):
    return ap.broadcast_to(list(shape))


def constants(K):
    nc = K.nc
    with K.begin() as block:
        @block.gpsimd
        def _(pool):
            K.g(pool, nc.gpsimd.memset(K.ident[:, :], 0.0))
            K.g(pool, nc.gpsimd.memset(K.ones[:, :], 1.0))
            K.g(pool, nc.gpsimd.affine_select(out=K.ident[:, :], in_=K.ident[:, :], compare_op=ALU.not_equal,
                                              fill=1.0, base=0, pattern=[[-1, P]], channel_multiplier=1))

        @block.sync
        def _(sp):
            K.stream(sp)


def load_phase(K, pairs):
    with K.begin() as block:
        @block.scalar
        def _(act):
            for dst, src in pairs:
                load(K, act, dst, src)
            act.wait_ge(*K.load.now())


class Split:

    def __init__(self, K, st, chunks, depth, rows=None):
        self.K, self.first, self.rows = K, K.taken, rows
        self.chunks, self.depth, self.nact, self.ndve = chunks, depth, 0, 0
        K.uniq += 1
        new = lambda name, *shape: st.enter_context(K.nc.sbuf_tensor(f"s{K.uniq}_{name}", [P, *shape], F32R))
        self.hi, self.lo = new("w_high", 2 * depth, CH // 2), new("w_low", 2 * depth, CH // 2)
        if rows:
            tok = rows[0].shape[2]
            self.xhi, self.xlo = new("x_high", 2 * depth, tok), new("x_low", 2 * depth, tok)
        self.half, self.high, self.low = K.free_sigs[11:14]
        for g in (self.half, self.high, self.low):
            g.base = g.n

    def source(self, c, i):
        return self.K.ring[:, (self.first + c) % R, i * CH // 2:(i + 1) * CH // 2]

    def at(self, c, i):
        return c % self.depth * 2 + i

    def act(self, act, done):
        K = self.K
        while self.nact < min(done + self.depth + 1, self.chunks):
            c = self.nact
            n = self.first + c
            act.wait_ge(K.landed[n % R], 16 * (n // R + 1))
            for i in range(2):
                b = self.at(c, i)
                if c >= self.depth:
                    act.wait_ge(*(K.used if i else self.half).at(c - self.depth + 1))
                if self.rows:
                    x, kts = self.rows
                    K.nc.scalar.activation(self.xhi[:, b, :], x[:, kts[2 * c + i], :], ACT.Copy)
                K.nc.scalar.activation(self.hi[:, b, :], self.source(c, i), ACT.Copy).then_inc(*self.high.up())
            self.nact += 1

    def dve(self, dve, done):
        K = self.K
        while self.ndve < min(done + self.depth + 1, self.chunks):
            c = self.ndve
            for i in range(2):
                b = self.at(c, i)
                dve.wait_ge(*self.high.at(2 * c + i + 1))
                if self.rows:
                    x, kts = self.rows
                    K.nc.vector.tensor_tensor(self.xlo[:, b, :], x[:, kts[2 * c + i], :], self.xhi[:, b, :],
                                              ALU.subtract)
                K.nc.vector.tensor_tensor(self.lo[:, b, :], self.source(c, i), self.hi[:, b, :], ALU.subtract)\
                    .then_inc(*self.low.up())
            self.ndve += 1


def linear_cols(K, jobs):
    nc = K.nc
    evac, = K.sig(1)
    with K.begin() as block:
        @block.tensor
        def _(pe):
            n = 0
            for x, chunks, _ in jobs:
                tok = x.shape[2]
                nb = tok // 256
                for c in range(chunks):
                    w = K.chunk(pe).rearrange("p (k n) -> p k n", k=KT)
                    if n >= 3:
                        pe.wait_ge(*evac.at(n - 2))
                    for h in range(2):
                        for k in range(KT):
                            o = K.ps[n % 3 * 2 + (h if nb == 2 else 0)][:, (0 if nb == 2 else h * tok):][:, 0:tok]
                            last = nc.tensor.matmul(o, w[:, k, h * P:(h + 1) * P], x[:, k, :],
                                                    start=(k == 0), stop=(k == KT - 1))
                    last.then_inc(*K.used.up())
                    n += 1

        @block.scalar
        def _(act):
            n = 0
            for x, chunks, fn in jobs:
                tok = x.shape[2]
                nb = tok // 256
                for c in range(chunks):
                    act.wait_ge(*K.used.at(n + 1))
                    for h in range(2):
                        o = K.ps[n % 3 * 2 + (h if nb == 2 else 0)][:, (0 if nb == 2 else h * tok):][:, 0:tok]
                        last = fn(act, c, h, o)
                    K.a(act, last, evac)
                    n += 1

        @block.sync
        def _(sp):
            K.stream(sp)


def mm_rows(K, pe, x, kts, first=True, final=True, banks=(0, 1, 2, 3), tts=TT):
    nc = K.nc
    for i in range(0, len(kts), 2):
        w = K.chunk(pe).rearrange("p (k n) -> p k n", k=2)
        for q in range(2):
            for tt in range(tts):
                for h in range(2):
                    last = nc.tensor.matmul(K.ps[banks[tt * 2 + h]][:, :], x[:, kts[i + q], tt * P:(tt + 1) * P],
                                            w[:, q, h * 512:(h + 1) * 512],
                                            start=(first and i == 0 and q == 0),
                                            stop=(final and i + q == len(kts) - 1))
        last.then_inc(*K.used.up())


def linear_rows(K, x, kts, evac, tts=TT, after=None, sqrts=None, root_bufs=(), depth=2):
    nc = K.nc
    chunks = len(kts) // 2
    with ExitStack() as st:
        parts = Split(K, st, chunks, depth, (x, kts)) if depth else None
        with K.begin() as block:
            @block.tensor
            def _(pe):
                if not depth:
                    mm_rows(K, pe, x, kts, banks=tuple(range(8)), tts=tts)
                    return
                for c in range(chunks):
                    for i in range(2):
                        pe.wait_ge(*parts.low.at(2 * c + i + 1))
                        b = parts.at(c, i)
                        for tt in range(tts):
                            t = slice(tt * P, (tt + 1) * P)
                            for h in range(2):
                                n = slice(h * 512, (h + 1) * 512)
                                for p, (xs, ws) in enumerate(((parts.xlo, parts.hi), (parts.xhi, parts.lo), (parts.xhi, parts.hi))):
                                    last = nc.tensor.matmul(K.ps[tt * 2 + h][:, :], xs[:, b, t], ws[:, b, n],
                                                            start=(c == 0 and i == 0 and p == 0),
                                                            stop=(c == chunks - 1 and i == 1 and p == 2))
                        last.then_inc(*(K.used if i else parts.half).up())
                    K.taken += 1

            @block.vector
            def _(dve):
                if depth:
                    parts.dve(dve, chunks)
                dve.wait_ge(*K.used.at(chunks))
                for tt in range(tts):
                    for h in range(2):
                        K.v(dve, evac(dve, tt, h, K.ps[tt * 2 + h][:, :]))
                if after:
                    after(dve)

            @block.scalar
            def _(act):
                if depth:
                    parts.act(act, chunks)
                if sqrts:
                    roots(K, act, *sqrts, root_bufs)

            @block.sync
            def _(sp):
                K.stream(sp)


def to_cols(K, rows, cols, tiles, tts=TT, evac=None, width=P):
    nc = K.nc
    done, read = K.sig(2)
    jobs = [(tt, j) for tt in range(tts) for j in range(tiles)]
    with K.begin() as block:
        @block.tensor
        def _(pe):
            for n, (tt, j) in enumerate(jobs):
                if n % 4 == 0 and n >= 32:
                    pe.wait_ge(*read.at(n // 4 - 7))
                last = nc.tensor.transpose(K.ps[n // 4 % 8][0:width, n % 4 * P:n % 4 * P + P],
                                           rows(tt, j), K.ident[:, :])
                if n % 4 == 3 or n == len(jobs) - 1:
                    last.then_inc(*done.up())

        @block.scalar
        def _(act):
            for n, (tt, j) in enumerate(jobs):
                if n % 4 == 0:
                    act.wait_ge(*done.at(n // 4 + 1))
                src = K.ps[n // 4 % 8][0:width, n % 4 * P:n % 4 * P + P]
                last = evac(j, tt, src) if evac else nc.scalar.activation(cols(j, tt), src, ACT.Copy)
                if n % 4 == 3 or n == len(jobs) - 1:
                    last.then_inc(*read.up())
            act.wait_ge(*read.now())

        @block.sync
        def _(sp):
            K.stream(sp)


def roots(K, act, ask, given, bufs):
    for n, buf in enumerate(bufs):
        act.wait_ge(*ask.at(n + 1))
        K.nc.scalar.activation(buf, buf, ACT.Sqrt).then_inc(*given.up())


def rsqrt(K, dve, ins, buf, sqrts):
    ask, given = sqrts
    K.v(dve, ins, ask)
    dve.wait_ge(*given.at(ask.n - ask.base))
    K.v(dve, K.nc.vector.reciprocal(buf, buf))


def layer_norm(K, dve, z, out, small, g, b, width, groups, eps, sqrts):
    nc = K.nc
    st, mv, rs = small
    for n in range(groups):
        for q in range(0, width, 512):
            K.v(dve, nc.vector.bn_stats(st[:, (q // 512) * 6:(q // 512) * 6 + 6], z[:, n, q:q + min(512, width)]))
        K.v(dve, nc.vector.bn_aggr(mv[:, n, :], st[:, 0:6 * max(1, width // 512)]))
    rsqrt(K, dve, nc.vector.tensor_scalar(rs[:, 0:groups], mv[:, 0:groups, 1], eps, None, ALU.add),
          rs[:, 0:groups], sqrts)
    for n in range(groups):
        K.v(dve, nc.vector.tensor_scalar(out[:, n, :], z[:, n, :], mv[:, n, 0:1], rs[:, n:n + 1],
                                         ALU.subtract, ALU.mult))
    flat = out.rearrange("p n w -> p (n w)")
    K.v(dve, nc.vector.tensor_tensor(flat, flat, g, ALU.mult))
    if b is not None:
        K.v(dve, nc.vector.tensor_tensor(flat, flat, b, ALU.add))


def gated_hidden(K, st, x, hid, chunks, conv=None):
    nc = K.nc
    tok = x.shape[2]
    seqs = tok // T
    side = x.rearrange("p k t -> p (k t)").rearrange("p (b s h t) -> p b s h t", b=2, s=2, h=2)
    centre, tapped, gated, free, xsplit = K.sig(5)
    parts = Split(K, st, 2 * chunks, 1 if tok > T else 2)
    K.uniq += 1
    xhi, xlo = (st.enter_context(nc.sbuf_tensor(f"s{K.uniq}_x_{n}", [P, KT, tok], F32R)) for n in ("high", "low"))

    def bank(c, s, h):
        return K.ps[c % 2 * 4 + s * 2 + h][:, 0:tok]

    with K.begin() as block:
        @block.tensor
        def _(pe):
            for c in range(chunks):
                if c >= 2:
                    pe.wait_ge(*(tapped if conv else free).at(c - 1))
                for s in range(2):
                    for i in range(2):
                        pe.wait_ge(*parts.low.at(4 * c + 2 * s + i + 1))
                        b = parts.at(2 * c + s, i)
                        for h in range(2):
                            for k in range(KT // 2):
                                j = i * (KT // 2) + k
                                n = slice(k * 256 + h * P, k * 256 + h * P + P)
                                for p, (ws, xs) in enumerate(((parts.lo, xhi), (parts.hi, xlo), (parts.hi, xhi))):
                                    last = nc.tensor.matmul(bank(c, s, h), ws[:, b, n], xs[:, j, :],
                                                            start=(j == 0 and p == 0), stop=(j == KT - 1 and p == 2))
                        last.then_inc(*(K.used if i else parts.half).up())
                    K.taken += 1

        @block.scalar
        def _(act):
            def silu(c):
                act.wait_ge(*tapped.at(c + 1))
                for h in range(2):
                    last = nc.scalar.activation(side[:, c % 2, 0, h, :], side[:, c % 2, 0, h, :], ACT.Silu)
                last.then_inc(*gated.up())

            nc.scalar.activation(xhi[:, :, :], x, ACT.Copy).then_inc(*xsplit.up())
            for c in range(chunks):
                parts.act(act, 2 * c + 1 if conv else 2 * c)
                if conv is None:
                    act.wait_ge(*K.used.at(2 * c + 1))
                    if c >= 2:
                        act.wait_ge(*free.at(c - 1))
                    for h in range(2):
                        last = nc.scalar.activation(side[:, c % 2, 0, h, :], bank(c, 0, h), ACT.Silu)
                    last.then_inc(*gated.up())
                    continue
                act.wait_ge(*K.used.at(2 * c + 2))
                if c >= 2:
                    act.wait_ge(*free.at(c - 1))
                for s in range(2):
                    for h in range(2):
                        j = (chunks * 2 if s == 0 else 0) + 2 * c + h
                        last = nc.scalar.activation(side[:, c % 2, s, h, :], bank(c, s, h), ACT.Identity,
                                                    bias=conv[1][:, j:j + 1], scale=conv[0][:, j, 1:2])
                last.then_inc(*centre.up())
                if c >= 1:
                    silu(c - 1)
            if conv is not None:
                silu(chunks - 1)

        @block.vector
        def _(dve):
            def product(c):
                dve.wait_ge(*gated.at(c + 1))
                for h in range(2):
                    up = side[:, c % 2, 1, h, :] if conv else bank(c, 1, h)
                    last = nc.vector.tensor_tensor(hid[:, 2 * c + h, :], side[:, c % 2, 0, h, :], up, ALU.mult)
                last.then_inc(*free.up())

            dve.wait_ge(*xsplit.at(1))
            nc.vector.tensor_tensor(xlo[:, :, :], x, xhi[:, :, :], ALU.subtract)
            for c in range(chunks):
                parts.dve(dve, 2 * c + 1)
                if conv is None:
                    dve.wait_ge(*K.used.at(2 * c + 2))
                    product(c)
                    continue
                dve.wait_ge(*centre.at(c + 1))
                for tap, (dst, src) in enumerate(((slice(1, T), slice(0, T - 1)), (slice(0, T - 1), slice(1, T)))):
                    for s in range(2):
                        for h in range(2):
                            j = (chunks * 2 if s == 0 else 0) + 2 * c + h
                            o = side[:, c % 2, s, h, :].rearrange("p (q t) -> p q t", q=seqs)[:, :, dst]
                            i = bank(c, s, h).rearrange("p (q t) -> p q t", q=seqs)[:, :, src]
                            last = nc.vector.scalar_tensor_tensor(o, i, conv[0][:, j, 2 * tap:2 * tap + 1], o,
                                                                  ALU.mult, ALU.add)
                    K.v(dve, last, tapped if tap else None)
                if c >= 1:
                    product(c - 1)
            if conv is not None:
                product(chunks - 1)
            dve.wait_ge(*free.now())

        @block.sync
        def _(sp):
            K.stream(sp)


def rwkv(K, h1):
    nc, i = K.nc, K.i
    with ExitStack() as st:
        S = lambda *s: scratch(K, st, *s)
        units, = S([P, 14, CH])
        unit = lambda n, pat="p (j t) -> p j t", **kw: units[:, n, :].rearrange(pat, **kw)
        vr, gr = (unit(n, j=TT) for n in (0, 1))
        rT, kT, aT, dec = (unit(n, j=KT) for n in (2, 3, 4, 5))
        cols, = S([P, 5, KT])
        w0, a0, k_k, k_a, r_k = (cols[:, n, :] for n in range(5))
        with ExitStack() as st1:
            S1 = lambda *s: scratch(K, st1, *s)
            mixes = [unit(n, j=KT) for n in range(6, 12)]
            xT = unit(12, j=KT)
            mu, w2s, a2s, g1s, g2a, g2b = S1([P, 6, KT], [64, D], [64, D], [P, KT, 160], [P, D], [32, D])
            w1s = units[:, 13, 0:512].rearrange("p (k n) -> p k n", k=KT)
            a1s = units[:, 13, 512:1024].rearrange("p (k n) -> p k n", k=KT)
            hw, ha = units[0:64, 13, 1024:1280], units[0:64, 13, 1280:1536]
            hg, hg2 = units[:, 13, 1536:1792], units[0:32, 13, 1792:2048]
            load_phase(K, [(xT[:, :, :], i["x_cols"]), (mu[:, :, :], i["mu_cols"]), (cols[:, :, :], i["rwkv_cols"]),
                           (w1s[:, :, :], i["decay_w1"]), (w2s[:, :], i["decay_w2"]),
                           (a1s[:, :, :], i["iclr_a1"]), (a2s[:, :], i["iclr_a2"]), (g1s[:, :, :], i["gate_g1"]),
                           (g2a[:, :], i["gate_g2"][0:P, :]), (g2b[:, :], i["gate_g2"][P:160, :])])
            xx = mixes[5]

            with K.begin() as block:
                @block.vector
                def _(dve):
                    nc.vector.tensor_tensor(xx[:, :, 1:T], xT[:, :, 0:T - 1], xT[:, :, 1:T], ALU.subtract)
                    K.v(dve, nc.vector.tensor_scalar(xx[:, :, 0:1], xT[:, :, 0:1], -1.0, None, ALU.mult))
                    for m in range(6):
                        for k in range(KT):
                            last = nc.vector.scalar_tensor_tensor(mixes[m][:, k, :], xx[:, k, :], mu[:, m, k:k + 1],
                                                                  xT[:, k, :], ALU.mult, ALU.add)
                    K.v(dve, last)

                @block.sync
                def _(sp):
                    K.stream(sp)

            def keep(dst):
                return lambda act, c, h, o: nc.scalar.activation(dst[:, 2 * c + h, :], o, ACT.Copy)

            linear_cols(K, [(mixes[0], 4, keep(rT)), (mixes[1], 4, keep(kT))])
            linear_rows(K, mixes[2], range(KT), lambda dve, tt, h, o: nc.vector.tensor_copy(
                vr[:, tt, h * 512:(h + 1) * 512], o), depth=0)

            low, mid, hi, seen = K.sig(4)
            with K.begin() as block:
                @block.tensor
                def _(pe):
                    for b, (x, w, n0, n1) in enumerate(((mixes[3], w1s, 0, 64), (mixes[4], a1s, 0, 64),
                                                        (mixes[5], g1s, 0, P), (mixes[5], g1s, P, 160))):
                        for k in range(KT):
                            last = nc.tensor.matmul(K.ps[b][0:n1 - n0, 0:T], w[:, k, n0:n1], x[:, k, :],
                                                    start=(k == 0), stop=(k == KT - 1))
                        last.then_inc(*low.up())
                    pe.wait_ge(*mid.at(4))
                    for n in range(2 * KT):
                        w, x = (w2s, hw) if n < KT else (a2s, ha)
                        if n % 2 == 0 and n >= 8:
                            pe.wait_ge(*seen.at(n // 2 - 3))
                        last = nc.tensor.matmul(K.ps[4 + n // 2 % 4][:, n % 2 * T:n % 2 * T + T],
                                                w[:, n % KT * P:n % KT * P + P], x[:, :], start=True, stop=True)
                        if n % 2:
                            last.then_inc(*hi.up())
                    for tt in range(TT):
                        for h in range(2):
                            o = K.ps[2 * tt + h][:, :]
                            nc.tensor.matmul(o, hg[:, tt * P:(tt + 1) * P], g2a[:, h * 512:(h + 1) * 512],
                                             start=True, stop=False)
                            last = nc.tensor.matmul(o, hg2[:, tt * P:(tt + 1) * P], g2b[:, h * 512:(h + 1) * 512],
                                                    start=False, stop=True)
                    last.then_inc(*low.up())

                @block.scalar
                def _(act):
                    for b, (o, f) in enumerate(((hw, ACT.Tanh), (ha, ACT.Copy), (hg, ACT.Sigmoid),
                                                (hg2, ACT.Sigmoid))):
                        act.wait_ge(*low.at(b + 1))
                        nc.scalar.activation(o[:, :], K.ps[b][0:o.shape[0], 0:T], f).then_inc(*mid.up())
                    for n in range(2 * KT):
                        if n % 2 == 0:
                            act.wait_ge(*hi.at(n // 2 + 1))
                        dst, bias = (dec, w0) if n < KT else (aT, a0)
                        j = n % KT
                        last = nc.scalar.activation(dst[:, j, :], K.ps[4 + n // 2 % 4][:, n % 2 * T:n % 2 * T + T],
                                                    ACT.Sigmoid, bias=bias[:, j:j + 1])
                        if n % 2:
                            last.then_inc(*seen.up())
                    act.wait_ge(*seen.now())

                @block.vector
                def _(dve):
                    dve.wait_ge(*low.at(5))
                    for tt in range(TT):
                        for h in range(2):
                            last = nc.vector.tensor_copy(gr[:, tt, h * 512:(h + 1) * 512], K.ps[2 * tt + h][:, :])
                    K.v(dve, last)

                @block.sync
                def _(sp):
                    K.stream(sp)

        yr = h1
        with ExitStack() as st2:
            S2 = lambda *s: scratch(K, st2, *s)
            At, Rt, G, E, Bt, Kt = (unit(n, j=KT) for n in range(6, 12))
            AR = units[:, 12:14, :].rearrange("p u (j c a t) -> p (u j) c a t", j=KT // 2, c=TT, a=2)
            bones, hsel, bonus = S2([P, P], [P, 2], [P, TT, 16])
            level, dstate = S2([P, 7, P], [P, KT])
            tri, = S2([P, 4, P])
            Brow, Krow, Sbd = S2([P, D], [P, D], [P, KT, P])
            load_phase(K, [(bones[:, :], i["head_block"]), (hsel[:, :], i["head_pick"]), (level[:, :, :], i["levels"]),
                           (tri[:, :, :], i["tri"])])

            sq, nm, gs, ex, rk, ask, given = K.sig(7)
            b3 = lambda c: bc(c.unsqueeze(2), [P, KT, T])
            with K.begin() as block:
                @block.vector
                def _(dve):
                    V = nc.vector
                    K.v(dve, V.tensor_tensor(At[:, :, :], kT[:, :, :], b3(k_k), ALU.mult))
                    K.v(dve, V.tensor_tensor(E[:, :, :], At[:, :, :], At[:, :, :], ALU.mult), sq)
                    K.v(dve, V.tensor_scalar(dec[:, :, :], dec[:, :, :], -math.exp(-0.5), None, ALU.mult))
                    for j in range(KT):
                        for c in range(TT):
                            t = slice(c * P, c * P + P)
                            last = V.tensor_tensor_scan(G[:, j, t], K.ones[:, :], dec[:, j, t], 0.0, ALU.mult, ALU.add)
                    K.v(dve, last)
                    G4 = G[:, :, :].rearrange("p j (c t) -> p (j c) t", c=TT)
                    K.v(dve, V.tensor_copy(Sbd[:, 0, 0:2 * KT], G4[:, :, P - 1]))
                    K.v(dve, V.scalar_tensor_tensor(G4, bc(Sbd[:, 0, 0:2 * KT].unsqueeze(2), [P, 2 * KT, P]), -0.5, G4,
                                                    ALU.mult, ALU.add), gs)
                    dve.wait_ge(*nm.at(1))
                    K.v(dve, V.tensor_scalar(E[:, :, :], aT[:, :, :], -1.0, None, ALU.add))
                    K.v(dve, V.tensor_tensor(E[:, :, :], E[:, :, :], b3(k_a), ALU.mult))
                    K.v(dve, V.tensor_scalar(E[:, :, :], E[:, :, :], 1.0, None, ALU.add))
                    K.v(dve, V.tensor_tensor(kT[:, :, :], kT[:, :, :], E[:, :, :], ALU.mult))
                    K.v(dve, V.tensor_tensor(E[:, :, :], rT[:, :, :], kT[:, :, :], ALU.mult))
                    K.v(dve, V.tensor_tensor(E[:, :, :], E[:, :, :], b3(r_k), ALU.mult), rk)
                    for b in range(4):
                        rsqrt(K, dve, V.tensor_scalar(K.ps[b][:, :], K.ps[b][:, :], 1e-24, None, ALU.max),
                              K.ps[b][:, :], (ask, given))
                        pair = At[:, 2 * b:2 * b + 2, :].rearrange("p j t -> p (j t)")
                        K.v(dve, V.tensor_tensor(pair, pair, K.ps[b][:, :], ALU.mult))
                    K.v(dve, V.tensor_tensor(Bt[:, :, :], At[:, :, :], aT[:, :, :], ALU.mult))
                    dve.wait_ge(*nm.at(2))
                    K.v(dve, V.tensor_copy(bonus[:, :, :], K.ps[4][:, 0:32].rearrange("p (t h) -> p t h", t=TT)))
                    A4, R4 = (AR[:, :, :, n, :].rearrange("p j c t -> p (j c) t") for n in range(2))
                    flat = lambda x: x[:, :, :].rearrange("p j (c t) -> p (j c) t", c=TT)
                    dve.wait_ge(*ex.at(3))
                    K.v(dve, V.tensor_tensor(dstate[:, :], dstate[:, :], Sbd[:, 1, 0:KT], ALU.mult))
                    K.v(dve, V.tensor_tensor(R4, flat(rT), flat(Rt), ALU.mult))
                    K.v(dve, V.scalar_tensor_tensor(A4, flat(At), -1.0, flat(dec), ALU.mult, ALU.mult))
                    K.v(dve, V.tensor_tensor(Bt[:, :, :], Bt[:, :, :], Kt[:, :, :], ALU.mult))
                    K.v(dve, V.tensor_tensor(Kt[:, :, :], kT[:, :, :], Kt[:, :, :], ALU.mult))

                @block.tensor
                def _(pe):
                    pe.wait_ge(*sq.at(1))
                    for j in range(KT):
                        last = nc.tensor.matmul(K.ps[j // 2][:, j % 2 * T:j % 2 * T + T], bones[:, :], E[:, j, :],
                                                start=True, stop=True)
                    last.then_inc(*nm.up())
                    pe.wait_ge(*rk.at(1))
                    for tt in range(TT):
                        for j in range(KT):
                            last = nc.tensor.matmul(K.ps[4][:, tt * 16 + 2 * j:tt * 16 + 2 * j + 2],
                                                    E[:, j, tt * P:(tt + 1) * P], hsel[:, :], start=True, stop=True)
                    last.then_inc(*nm.up())

                @block.scalar
                def _(act):
                    act.wait_ge(*gs.at(1))
                    K.a(act, nc.scalar.activation(Rt[:, :, :], G[:, :, :], ACT.Exp), ex)
                    K.a(act, nc.scalar.activation(Kt[:, :, :], G[:, :, :], ACT.Exp, scale=-1.0), ex)
                    gend = G[:, :, :].rearrange("p j (c t) -> p j c t", c=TT)[:, :, :, P - 1]
                    K.a(act, nc.scalar.activation(dstate[:, :], gend[:, :, 0], ACT.Exp))
                    K.a(act, nc.scalar.activation(Sbd[:, 1, 0:KT], gend[:, :, 1], ACT.Exp))
                    act.wait_ge(*K.pool.at(1))
                    K.a(act, nc.scalar.activation(dec[:, :, :], dec[:, :, :], ACT.Exp), ex)
                    roots(K, act, ask, given, [K.ps[b][:, :] for b in range(4)])

                @block.gpsimd
                def _(pool):
                    pool.wait_ge(*gs.at(1))
                    K.g(pool, nc.gpsimd.tensor_tensor(dec[:, :, :], G[:, :, :], dec[:, :, :], ALU.subtract))

                @block.sync
                def _(sp):
                    K.stream(sp)

            to_cols(K, lambda tt, j: Bt[:, j, 0:P], lambda j, tt: Brow[:, j * P:(j + 1) * P], KT, tts=1)
            to_cols(K, lambda tt, j: Kt[:, j, 0:P], lambda j, tt: Krow[:, j * P:(j + 1) * P], KT, tts=1)
            gram = units[:, 2:6, :].rearrange("p u (h a t) -> p (u h) a t", h=4, a=4)
            Dm, DT, Wm, Lo = (unit(n, "p (h t) -> p h t", h=16) for n in (6, 7, 8, 9))
            X, SA = units[:, 9, 0:D], units[:, 8, 0:D]
            for c in range(TT):
                wkv_chunk(K, c, AR, Bt, Kt, vr, gram, Dm, DT, Wm, Lo, X, SA, tri, level, Brow, Krow, Sbd,
                          dstate, bones, yr)

            gg, gb = units[:, 10, 0:D], units[:, 10, D:2 * D]
            tmp = units[:, 11, 0:D].rearrange("p (n w) -> p n w", n=16)
            st_, mv, rs = S2([P, 12], [P, 16, 2], [P, 16])
            load_phase(K, [(gg[:, :], i["gn_g"].partition_broadcast(P)), (gb[:, :], i["gn_b"].partition_broadcast(P))])
            ask, given = K.sig(2)
            with K.begin() as block:
                @block.scalar
                def _(act):
                    roots(K, act, ask, given, [rs[:, :]] * TT)

                @block.vector
                def _(dve):
                    for tt in range(TT):
                        y = yr[:, tt, :].rearrange("p (n w) -> p n w", n=16)
                        layer_norm(K, dve, y, y, (st_, mv, rs), gg[:, :], gb[:, :], 64, 16, 64e-5, (ask, given))
                        v3 = vr[:, tt, :].rearrange("p (n w) -> p n w", n=16)
                        K.v(dve, nc.vector.tensor_tensor(tmp[:, :, :], v3, bc(bonus[:, tt, :].unsqueeze(2), [P, 16, 64]),
                                                         ALU.mult))
                        K.v(dve, nc.vector.tensor_tensor(y, y, tmp[:, :, :], ALU.add))
                        K.v(dve, nc.vector.tensor_tensor(yr[:, tt, :], yr[:, tt, :], gr[:, tt, :], ALU.mult))

                @block.sync
                def _(sp):
                    K.stream(sp)

        yT, xr = unit(2, j=KT), unit(3, j=TT)
        to_cols(K, lambda tt, j: yr[:, tt, j * P:(j + 1) * P], lambda j, tt: yT[:, j, tt * P:(tt + 1) * P], KT)
        load_phase(K, [(xr, i["x_rows"])])
        project_residual_norm(K, st, yT, KT, xr, h1, 0, depth=0)


def project_residual_norm(K, st, hT, kts, x, out, n, depth=2):
    nc, i = K.nc, K.i
    g, b, st_, mv, rs = scratch(K, st, [P, D], [P, D], [P, 12], [P, 1, 2], [P, 1])
    load_phase(K, [(g[:, :], i["ln_g"][n].partition_broadcast(P)), (b[:, :], i["ln_b"][n].partition_broadcast(P))])

    sqrts = K.sig(2)

    def evac(dve, tt, h, o):
        s = slice(h * 512, h * 512 + 512)
        return nc.vector.scalar_tensor_tensor(out[:, tt, s], x[:, tt, s], ALPHA, o, ALU.mult, ALU.add)

    def after(dve):
        for tt in range(TT):
            z = out[:, tt, :].unsqueeze(1)
            layer_norm(K, dve, z, z, (st_, mv, rs), g[:, :], b[:, :], D, 1, 1e-5, sqrts)

    linear_rows(K, hT, range(kts), evac, after=after, sqrts=sqrts, root_bufs=[rs[:, :]] * TT,
                depth=depth)


def wkv_chunk(K, c, AR, Bt, Kt, vr, gram, Dm, DT, Wm, Lo, X, SA, tri, level, Brow, Krow, Sbd, dstate, bones, yr):
    nc = K.nc
    V = nc.vector
    tok = slice(c * P, c * P + P)
    made, kept = K.sig(2)
    with K.begin() as block:
        @block.tensor
        def _(pe):
            for h in range(16):
                j, r = h // 2, slice(64 * (h % 2), 64 * (h % 2) + 64)
                if h >= 8:
                    pe.wait_ge(*kept.at(h - 7))
                rhs = AR[r, j, c, :, :].rearrange("p a t -> p (a t)")
                nc.tensor.matmul(K.ps[h % 8][:, 0:256], Bt[r, j, tok], rhs, start=True, stop=True)
                nc.tensor.matmul(K.ps[h % 8][:, 256:512], Kt[r, j, tok], rhs, start=True,
                                 stop=True).then_inc(*made.up())

        @block.vector
        def _(dve):
            K.v(dve, V.memset(gram[:, :, :, :], 0.0))
            for m in (Dm, DT):
                K.v(dve, V.tensor_copy(m[:, :, :], bc(K.ident[:, :].unsqueeze(1), [P, 16, P])))
            for h in range(16):
                dve.wait_ge(*made.at(h + 1))
                V.copy_predicated(gram[:, h, :, :].rearrange("p a t -> p (a t)"),
                                  tri[:, :, :].bitcast(U32).rearrange("p a t -> p (a t)"),
                                  K.ps[h % 8][:, :]).then_inc(*kept.up())
            dve.wait_ge(*kept.now())

        @block.sync
        def _(sp):
            K.stream(sp)

    lo, w, wc, dd, dn = K.sig(5)
    with K.begin() as block:
        @block.vector
        def _(dve):
            for l in range(7):
                for q in range(4):
                    if l:
                        dve.wait_ge(*w.at(4 * l))
                    K.v(dve, V.tensor_tensor(Lo[:, 4 * q:4 * q + 4, :], gram[:, 4 * q:4 * q + 4, 0, :],
                                             bc(level[:, l, :].unsqueeze(1), [P, 4, P]), ALU.mult), lo)
                for q in range(4):
                    dve.wait_ge(*dd.at(4 * l + q + 1))
                    o = q % 2 * 2
                    for m, b in ((Dm, 4 + o), (DT, 5 + o)):
                        f = m[:, 4 * q:4 * q + 4, :].rearrange("p a t -> p (a t)")
                        last = V.tensor_tensor(f, f, K.ps[b][:, :], ALU.add)
                    K.v(dve, last, dn)

        @block.tensor
        def _(pe):
            for l in range(7):
                for q in range(4):
                    pe.wait_ge(*lo.at(4 * l + q + 1))
                    if l:
                        pe.wait_ge(*dn.at(4 * (l - 1) + q + 1))
                        pe.wait_ge(*wc.at(4 * (l - 1) + q + 1))
                    for n in range(4):
                        h = 4 * q + n
                        last = nc.tensor.matmul(K.ps[q][:, n * P:(n + 1) * P], Lo[:, h, :], Dm[:, h, :],
                                                start=True, stop=True)
                    last.then_inc(*w.up())
                for q in range(4):
                    pe.wait_ge(*wc.at(4 * l + q + 1))
                    if 4 * l + q >= 2:
                        pe.wait_ge(*dn.at(4 * l + q - 1))
                    for n in range(4):
                        h = 4 * q + n
                        nc.tensor.matmul(K.ps[4 + q % 2 * 2][:, n * P:(n + 1) * P], DT[:, h, :], Wm[:, h, :],
                                         start=True, stop=True)
                        last = nc.tensor.matmul(K.ps[5 + q % 2 * 2][:, n * P:(n + 1) * P], Wm[:, h, :], DT[:, h, :],
                                                start=True, stop=True)
                    last.then_inc(*dd.up())

        @block.scalar
        def _(act):
            for l in range(7):
                for q in range(4):
                    act.wait_ge(*w.at(4 * l + q + 1))
                    if l:
                        act.wait_ge(*dd.at(4 * (l - 1) + q + 1))
                    nc.scalar.activation(Wm[:, 4 * q:4 * q + 4, :].rearrange("p a t -> p (a t)"), K.ps[q][:, :],
                                         ACT.Copy).then_inc(*wc.up())
            act.wait_ge(*wc.now())

        @block.sync
        def _(sp):
            K.stream(sp)

    vt = lambda h: vr[:, c, h * 64:(h + 1) * 64]
    p1, p2 = K.sig(2)
    with K.begin() as block:
        @block.tensor
        def _(pe):
            def accumulate(bank0, parts, state):
                for b in range(2):
                    first = True
                    for h in range(8 * b, 8 * b + 8):
                        o = K.ps[bank0 + b][:, h % 8 * 64:h % 8 * 64 + 64]
                        for lhsT, rhs in parts(h):
                            last = nc.tensor.matmul(o, lhsT, rhs, start=first, stop=(b == 1 and not state and h == 15),
                                                    skip_group_check=True)
                            first = False
                    if state is not None:
                        for j in range(4 * b, 4 * b + 4):
                            last = nc.tensor.matmul(K.ps[bank0 + b][:, j % 4 * P:j % 4 * P + P], AR[:, j, c, state, :],
                                                    Sbd[:, j, :], start=False, stop=True, skip_group_check=True)
                last.then_inc(*p1.up())

            accumulate(0, lambda h: [(gram[:, h, 2, :], vt(h))], 0 if c else None)
            pe.wait_ge(*p2.at(1))
            accumulate(2, lambda h: [(DT[:, h, :], X[:, h * 64:(h + 1) * 64])], None)
            pe.wait_ge(*p2.at(2))
            accumulate(4, lambda h: [(gram[:, h, 1, :], SA[:, h * 64:(h + 1) * 64]), (gram[:, h, 3, :], vt(h))],
                       1 if c else None)
            if c == 0:
                for b in range(2):
                    for j in range(4 * b, 4 * b + 4):
                        o = K.ps[6 + b][:, j % 4 * P:j % 4 * P + P]
                        nc.tensor.matmul(o, Brow[:, j * P:(j + 1) * P], SA[:, j * P:(j + 1) * P],
                                         start=True, stop=False)
                        last = nc.tensor.matmul(o, Krow[:, j * P:(j + 1) * P], vr[:, c, j * P:(j + 1) * P],
                                                start=False, stop=True)
                last.then_inc(*p1.up())

        @block.vector
        def _(dve):
            for n, dst in enumerate((X[:, :], SA[:, :], yr[:, c, :])):
                dve.wait_ge(*p1.at(n + 1))
                for b in range(2):
                    last = V.tensor_copy(dst[:, b * 512:(b + 1) * 512], K.ps[2 * n + b][:, :])
                K.v(dve, last, p2)
            if c == 0:
                dve.wait_ge(*p1.at(4))
                for j in range(KT):
                    K.v(dve, V.scalar_tensor_tensor(Sbd[:, j, :], K.ps[6 + j // 4][:, j % 4 * P:j % 4 * P + P],
                                                    dstate[:, j:j + 1], bones[:, :], ALU.mult, ALU.mult))

        @block.sync
        def _(sp):
            K.stream(sp)


def attention(K, st, units, outs):
    nc = K.nc
    V = nc.vector
    Pm, PT = scratch(K, st, [P, 3, 512], [P, 2, 512])
    mx, sm = scratch(K, st, [P, 3], [P, 3])
    scored, ready, expd, normed, turned, copied, applied, oread = K.sig(8)
    N = len(units)
    width = lambda u: units[u][1].shape[1]
    with K.begin() as block:
        @block.tensor
        def _(pe):
            def turn(u):
                pe.wait_ge(*normed.at(u + 1))
                if u >= 2:
                    pe.wait_ge(*copied.at(u - 1))
                for b in range(width(u) // P):
                    last = nc.tensor.transpose(K.ps[3 + u % 2][:, b * P:(b + 1) * P], Pm[:, u % 3, b * P:(b + 1) * P],
                                               K.ident[:, :])
                last.then_inc(*turned.up())

            def apply(u):
                pe.wait_ge(*copied.at(u + 1))
                g = u // 4
                if u % 4 == 0 and g >= 2:
                    pe.wait_ge(*oread.at(g - 1))
                vs = units[u][2]
                r, c = 64 * (u % 4 // 2), P * (u % 2)
                for b, v in enumerate(vs):
                    last = nc.tensor.matmul(K.ps[5 + g % 2][r:r + 64, c:c + P], v, PT[:, u % 2, b * P:(b + 1) * P],
                                            start=(b == 0), stop=(b == len(vs) - 1))
                last.then_inc(*applied.up())

            for u in range(N + 3):
                if u < N:
                    q, k, _, bias = units[u]
                    if u >= 3:
                        pe.wait_ge(*expd.at(u - 2))
                    last = nc.tensor.matmul(K.ps[u % 3][:, 0:width(u)], q, k, start=True, stop=bias is None)
                    if bias is not None:
                        last = nc.tensor.matmul(K.ps[u % 3][:, 0:bias.shape[1]], K.ident[:, :], bias,
                                                start=False, stop=True)
                    last.then_inc(*scored.up())
                if 2 <= u < N + 2:
                    turn(u - 2)
                if u >= 3:
                    apply(u - 3)

        @block.vector
        def _(dve):
            def norm(u):
                s = sm[:, u % 3:u % 3 + 1]
                dve.wait_ge(*expd.at(u + 1))
                K.v(dve, V.reciprocal(s, s))
                V.tensor_scalar(Pm[:, u % 3, 0:width(u)], Pm[:, u % 3, 0:width(u)], s, None, ALU.mult)\
                    .then_inc(*normed.up())

            for u in range(N + 4):
                if u < N:
                    dve.wait_ge(*scored.at(u + 1))
                    if u >= 3:
                        dve.wait_ge(*expd.at(u - 2))
                    V.reduce_max(mx[:, u % 3:u % 3 + 1], K.ps[u % 3][:, 0:width(u)], AX, negate=True)\
                        .then_inc(*ready.up())
                if 1 <= u <= N:
                    norm(u - 1)
                if u >= 4 and (u - 4) % 4 == 3:
                    g = (u - 4) // 4
                    dve.wait_ge(*applied.at(4 * g + 4))
                    V.tensor_copy(outs[g], K.ps[5 + g % 2][:, 0:256]).then_inc(*oread.up())
            dve.wait_ge(*oread.now())

        @block.scalar
        def _(act):
            def copy(u):
                act.wait_ge(*turned.at(u + 1))
                if u >= 2:
                    act.wait_ge(*applied.at(u - 1))
                nc.scalar.activation(PT[:, u % 2, 0:width(u)], K.ps[3 + u % 2][:, 0:width(u)], ACT.Copy)\
                    .then_inc(*copied.up())

            for u in range(N + 2):
                if u < N:
                    act.wait_ge(*ready.at(u + 1))
                    if u >= 3:
                        act.wait_ge(*turned.at(u - 2))
                    nc.scalar.activation(Pm[:, u % 3, 0:width(u)], K.ps[u % 3][:, 0:width(u)], ACT.Exp,
                                         bias=mx[:, u % 3:u % 3 + 1], accum_out=sm[:, u % 3:u % 3 + 1])\
                        .then_inc(*expd.up())
                if u >= 2:
                    copy(u - 2)

        @block.sync
        def _(sp):
            K.stream(sp)


def causal_attention(K, h2, h3):
    i = K.i
    with ExitStack() as st:
        hT, qT, kT, oT = scratch(K, st, *[[P, KT, T]] * 4)
        vr, mask = scratch(K, st, [P, TT, D], [P, TT, T])
        load_phase(K, [(mask[:, :, :], i["causal"])])
        to_cols(K, lambda tt, j: h2[:, tt, j * P:(j + 1) * P], lambda j, tt: hT[:, j, tt * P:(tt + 1) * P], KT)
        keep = lambda dst, f=1.0: lambda act, c, h, o: K.nc.scalar.activation(dst[:, 2 * c + h, :], o, ACT.Copy, scale=f)
        linear_cols(K, [(hT[:, :, :], 4, keep(qT, 64 ** -0.5)), (hT[:, :, :], 4, keep(kT))])
        linear_rows(K, hT, range(KT), lambda dve, tt, h, o: K.nc.vector.tensor_copy(
            vr[:, tt, h * 512:(h + 1) * 512], o))
        units = []
        for h in range(16):
            r, j = slice(64 * (h % 2), 64 * (h % 2) + 64), h // 2
            for qt in range(TT):
                nk = (qt + 1) * P
                units.append((qT[r, j, qt * P:(qt + 1) * P], kT[r, j, 0:nk],
                              [vr[:, b, h * 64:(h + 1) * 64] for b in range(qt + 1)], mask[:, qt, 0:nk]))
        with ExitStack() as st2:
            attention(K, st2, units, [oT[:, j, :] for j in range(KT)])
        project_residual_norm(K, st, oT, KT, h2, h3, 2)


CAP = 96
STEPS = FE // 256
PER = 3 * STEPS
GATE_AT = [1 if c == 0 else 3 * c for c in range(STEPS)]
UP_AT = [n + 1 for n in GATE_AT]
DOWN_AT = [min(3 * c + 5, PER) for c in range(STEPS)]


def moe(K, h3, h4):
    nc, i = K.nc, K.i
    V = nc.vector
    with ExitStack() as st:
        hT, acc = scratch(K, st, [P, KT, T], [P, TT, D])
        rt, lg, cmp_, eq, rank, gates, e8, m8, nm, low = scratch(
            K, st, [P, KT, NE], [P, TT, NE], [P, TT, NE, NE], [P, TT, NE, NE], [P, TT, NE], [P, TT, NE],
            [P, TT, NE], [P, TT, NE], [P, TT], [P, NE, NE])
        tri, slot, iota, most = scratch(K, st, [P, P], [P, TT, NE], [P, CAP], [P, 1])
        flag = st.enter_context(nc.sbuf_tensor("most_tokens", [P, 1], mybir.dt.int32))
        g, b, st_, mv, rs = scratch(K, st, [P, D], [P, D], [P, 12], [P, 1, 2], [P, 1])
        load_phase(K, [(rt[:, :, :], i["moe_router"]), (low[:, :, :], i["earlier"]), (tri[:, :], i["tri"][:, 1, :]),
                       (iota[:, :], i["slots"]),
                       (g[:, :], i["ln_g"][3].partition_broadcast(P)), (b[:, :], i["ln_b"][3].partition_broadcast(P))])
        to_cols(K, lambda tt, j: h3[:, tt, j * P:(j + 1) * P], lambda j, tt: hT[:, j, tt * P:(tt + 1) * P], KT)

        done, req, got, ranked, summed = K.sig(5)
        with K.begin() as block:
            @block.tensor
            def _(pe):
                for tt in range(TT):
                    for k in range(KT):
                        last = nc.tensor.matmul(K.ps[0][:, tt * NE:(tt + 1) * NE], hT[:, k, tt * P:(tt + 1) * P],
                                                rt[:, k, :], start=(k == 0), stop=(k == KT - 1))
                last.then_inc(*done.up())
                pe.wait_ge(*ranked.at(1))
                nc.tensor.matmul(K.ps[1][:, 0:NE], tri[:, :], rank[:, 0, :], start=True, stop=True)
                nc.tensor.matmul(K.ps[1][:, NE:2 * NE], K.ones[:, :], rank[:, 0, :], start=True, stop=False)
                nc.tensor.matmul(K.ps[1][:, NE:2 * NE], tri[:, :], rank[:, 1, :], start=False, stop=True)
                nc.tensor.matmul(K.ps[1][:, 2 * NE:3 * NE], K.ones[:, :], rank[:, 0, :], start=True, stop=False)
                nc.tensor.matmul(K.ps[1][:, 2 * NE:3 * NE], K.ones[:, :], rank[:, 1, :], start=False, stop=True)\
                    .then_inc(*summed.up())

            @block.vector
            def _(dve):
                dve.wait_ge(*done.at(1))
                K.v(dve, V.tensor_copy(lg[:, :, :], K.ps[0][:, 0:TT * NE].rearrange("p (t e) -> p t e", t=TT)))
                for tt in range(TT):
                    K.v(dve, V.max(m8[:, tt, :], lg[:, tt, :]))
                    K.v(dve, V.tensor_scalar(e8[:, tt, :], lg[:, tt, :], m8[:, tt, 0:1], None, ALU.subtract))
                    me = bc(lg[:, tt, :].unsqueeze(2), [P, NE, NE])
                    other = bc(lg[:, tt, :].unsqueeze(1), [P, NE, NE])
                    K.v(dve, V.tensor_tensor(cmp_[:, tt, :, :], other, me, ALU.is_gt))
                    K.v(dve, V.tensor_tensor(eq[:, tt, :, :], other, me, ALU.is_equal))
                    K.v(dve, V.tensor_tensor(eq[:, tt, :, :], eq[:, tt, :, :], low[:, :, :], ALU.mult))
                    K.v(dve, V.tensor_tensor(cmp_[:, tt, :, :], cmp_[:, tt, :, :], eq[:, tt, :, :], ALU.add))
                    K.v(dve, V.reduce_sum(rank[:, tt, :], cmp_[:, tt, :, :], AX))
                    K.v(dve, V.tensor_scalar(rank[:, tt, :], rank[:, tt, :], 1.5, None, ALU.is_lt))
                K.v(dve, V.memset(nm[:, :], 0.0), ranked)
                K.v(dve, V.memset(m8[:, :, :], 0.0), req)
                dve.wait_ge(*got.at(1))
                K.v(dve, V.tensor_tensor(e8[:, :, :], e8[:, :, :], rank[:, :, :], ALU.mult))
                K.v(dve, V.reduce_sum(nm[:, :], e8[:, :, :], AX))
                K.v(dve, V.reciprocal(nm[:, :], nm[:, :]))
                K.v(dve, V.tensor_tensor(gates[:, :, :], e8[:, :, :], bc(nm[:, :].unsqueeze(2), [P, TT, NE]), ALU.mult))
                dve.wait_ge(*summed.at(1))
                K.v(dve, V.tensor_tensor(slot[:, :, :], rank[:, :, :],
                                         K.ps[1][:, 0:2 * NE].rearrange("p (t e) -> p t e", t=TT), ALU.mult))
                K.v(dve, V.tensor_scalar(slot[:, :, :], slot[:, :, :], -1.0, None, ALU.add))
                K.v(dve, V.reduce_max(most[:, :], K.ps[1][:, 2 * NE:3 * NE], AX))
                K.v(dve, V.tensor_copy(flag[:, :], most[:, :]))
                K.v(dve, V.tensor_scalar(acc[:, :, :], h3[:, :, :], ALPHA, None, ALU.mult))
                for s in (K.moe_hid, K.moe_read, K.moe_free):
                    K.v(dve, V.memset(K.junk[:, :], 0.0), s)

            @block.scalar
            def _(act):
                act.wait_ge(*req.at(1))
                K.a(act, nc.scalar.activation(e8[:, :, :], e8[:, :, :], ACT.Exp), got)

            @block.sync
            def _(sp):
                K.stream(sp)

        assert K.issued == K.taken + R and PER % R == 0
        with K.begin() as block:
            dense = dense_experts(K, hT, acc, gates, st)
            routed = routed_experts(K, h3, acc, gates, slot, iota, st)

            @block.tensor
            def _(pe):
                n = pe.value_load(flag[0:1, 0:1], min_val=0, max_val=T)
                with pe.If(n > CAP):
                    dense[0](pe)
                with pe.Else():
                    routed[0](pe)

            @block.scalar
            def _(act):
                n = act.value_load(flag[0:1, 0:1], min_val=0, max_val=T)
                with act.If(n > CAP):
                    dense[1](act)
                with act.Else():
                    routed[1](act)

            @block.vector
            def _(dve):
                n = dve.value_load(flag[0:1, 0:1], min_val=0, max_val=T)
                with dve.If(n > CAP):
                    dense[2](dve)
                with dve.Else():
                    routed[2](dve)

            @block.sync
            def _(sp):
                first = K.taken

                def fill(e, n):
                    sp.wait_ge(K.used.h, e * PER + (first + n + 1))
                    sp.dma_start(K.ring[:, (first + n) % R, :], i["moe_w"][e * PER + (n + R)] if isinstance(e, int) else
                                 i["moe_w"][bass.ds(e * PER + (n + R), 1)].rearrange("o p c -> p (o c)"))\
                        .then_inc(K.landed[(first + n) % R], 16)

                with sp.Fori(0, NE - 1) as e:
                    for n in range(PER):
                        fill(e, n)
                for n in range(PER - R):
                    fill(NE - 1, n)
                K.taken += NE * PER
                K.issued = K.taken
                K.stream(sp)
            K.used.n += NE * PER

        sqrts = K.sig(2)
        with K.begin() as block:
            @block.vector
            def _(dve):
                for tt in range(TT):
                    layer_norm(K, dve, acc[:, tt, :].unsqueeze(1), h4[:, tt, :].unsqueeze(1), (st_, mv, rs),
                               g[:, :], b[:, :], D, 1, 1e-5, sqrts)

            @block.scalar
            def _(act):
                roots(K, act, *sqrts, [rs[:, :]] * TT)


def expert_chunks(K, pe, e):
    first, wave = K.taken, PER // R
    for n in range(PER):
        pe.wait_ge(K.landed[(first + n) % R], e * (16 * wave) + 16 * ((first + n) // R + 1))
        yield K.ring[:, (first + n) % R, :]


def dense_experts(K, hT, acc, gates, st):
    nc = K.nc
    V = nc.vector
    hid, sg = scratch(K, st, [P, 2, 2, T], [P, 2, 2, T])
    gated, hready, dread = K.moe_gated, K.moe_hid, K.moe_read
    u0 = K.taken

    def tensor(pe):
        with pe.Fori(0, NE) as e:
            chunks = expert_chunks(K, pe, e)

            def down(c):
                w = next(chunks).rearrange("p (k n) -> p k n", k=2)
                pe.wait_ge(hready.h, e * STEPS + (c + 2))
                if c == 0:
                    pe.wait_ge(dread.h, e + 1)
                for q in range(2):
                    for tt in range(TT):
                        for h in range(2):
                            last = nc.tensor.matmul(K.ps[tt * 2 + h][:, :], hid[:, c % 2, q, tt * P:(tt + 1) * P],
                                                    w[:, q, h * 512:(h + 1) * 512],
                                                    start=(c == 0 and q == 0), stop=(c == STEPS - 1 and q == 1))
                last.then_inc(K.used.h, 1)

            for c in range(STEPS):
                pe.wait_ge(hready.h, e * STEPS + max(c, 1))
                for s in range(2):
                    w = next(chunks).rearrange("p (k n) -> p k n", k=KT)
                    for h in range(2):
                        for k in range(KT):
                            last = nc.tensor.matmul(K.ps[4 + c % 2 * 2 + s][:, h * T:(h + 1) * T],
                                                    w[:, k, h * P:(h + 1) * P], hT[:, k, :],
                                                    start=(k == 0), stop=(k == KT - 1))
                    last.then_inc(K.used.h, 1)
                if c >= 1:
                    down(c - 1)
            down(STEPS - 1)

    def scalar(act):
        with act.Fori(0, NE) as e:
            for c in range(STEPS):
                act.wait_ge(K.used.h, e * PER + (u0 + GATE_AT[c]))
                act.wait_ge(hready.h, e * STEPS + max(c, 1))
                nc.scalar.activation(sg[:, c % 2, :, :].rearrange("p h t -> p (h t)"),
                                     K.ps[4 + c % 2 * 2][:, :], ACT.Silu).then_inc(gated.h, 1)

    def vector(dve):
        with dve.Fori(0, NE) as e:
            for c in range(STEPS):
                dve.wait_ge(K.used.h, e * PER + (u0 + UP_AT[c]))
                dve.wait_ge(gated.h, e * STEPS + (c + 1))
                if c >= 2:
                    dve.wait_ge(K.used.h, e * PER + (u0 + DOWN_AT[c - 2]))
                V.tensor_tensor(hid[:, c % 2, :, :].rearrange("p h t -> p (h t)"),
                                sg[:, c % 2, :, :].rearrange("p h t -> p (h t)"),
                                K.ps[5 + c % 2 * 2][:, :], ALU.mult).then_inc(hready.h, 1)
            dve.wait_ge(K.used.h, e * PER + (u0 + PER))
            for tt in range(TT):
                for h in range(2):
                    a = acc[:, tt, h * 512:(h + 1) * 512]
                    last = V.scalar_tensor_tensor(a, K.ps[tt * 2 + h][:, :], gates[:, tt, bass.ds(e, 1)], a,
                                                  ALU.mult, ALU.add)
            last.then_inc(dread.h, 1)
            dve.wait_ge(dread.h, e + 2)

    return tensor, scalar, vector


def routed_experts(K, h3, acc, gates, slot, iota, st):
    nc = K.nc
    V = nc.vector
    pick, pickT, xg, hid, sg, y = scratch(K, st, [P, TT, CAP], [CAP, T], [P, KT, CAP], [P, 2, 2, CAP],
                                          [P, 2, 2, CAP], [CAP, D])
    picked, gathered, xready, pready, gated, hready, yready, scattered, free = K.moe_sigs
    u0 = K.taken
    side = lambda c, s: K.ps[4 + c % 2 * 2 + s][:, 0:2 * CAP]
    NB = 5

    def tensor(pe):
        with pe.Fori(0, NE) as e:
            chunks = expert_chunks(K, pe, e)
            pe.wait_ge(picked.h, e + 1)
            pe.wait_ge(free.h, e + 1)
            for tt in range(TT):
                last = nc.tensor.transpose(K.ps[0][0:CAP, tt * P:(tt + 1) * P], pick[:, tt, :], K.ident[:, :])
            for j in range(KT):
                for tt in range(TT):
                    last = nc.tensor.matmul(K.ps[2 + j // NB][:, j % NB * CAP:j % NB * CAP + CAP],
                                            h3[:, tt, j * P:(j + 1) * P], pick[:, tt, :],
                                            start=(tt == 0), stop=(tt == TT - 1))
            last.then_inc(gathered.h, 1)

            def down(c):
                w = next(chunks).rearrange("p (k n) -> p k n", k=2)
                pe.wait_ge(hready.h, e * STEPS + (c + 1))
                if c == 0:
                    pe.wait_ge(pready.h, e + 1)
                for q in range(2):
                    for h in range(2):
                        last = nc.tensor.matmul(K.ps[h][0:CAP, :], hid[:, c % 2, q, :],
                                                w[:, q, h * 512:(h + 1) * 512],
                                                start=(c == 0 and q == 0), stop=(c == STEPS - 1 and q == 1))
                last.then_inc(K.used.h, 1)

            pe.wait_ge(xready.h, e + 1)
            for c in range(STEPS):
                if c >= 2:
                    pe.wait_ge(hready.h, e * STEPS + (c - 1))
                for s in range(2):
                    w = next(chunks).rearrange("p (k n) -> p k n", k=KT)
                    for h in range(2):
                        for k in range(KT):
                            last = nc.tensor.matmul(side(c, s)[:, h * CAP:(h + 1) * CAP], w[:, k, h * P:(h + 1) * P],
                                                    xg[:, k, :], start=(k == 0), stop=(k == KT - 1))
                    last.then_inc(K.used.h, 1)
                if c >= 1:
                    down(c - 1)
            down(STEPS - 1)
            pe.wait_ge(yready.h, e + 1)
            for tt in range(TT):
                for h in range(2):
                    last = nc.tensor.matmul(K.ps[2 + 2 * tt + h][:, :], pickT[:, tt * P:(tt + 1) * P],
                                            y[:, h * 512:(h + 1) * 512], start=True, stop=True)
            last.then_inc(scattered.h, 1)

    def scalar(act):
        with act.Fori(0, NE) as e:
            act.wait_ge(gathered.h, e + 1)
            nc.scalar.activation(pickT[:, :], K.ps[0][0:CAP, 0:T], ACT.Copy).then_inc(pready.h, 1)
            for c in range(STEPS):
                act.wait_ge(K.used.h, e * PER + (u0 + GATE_AT[c]))
                if c >= 2:
                    act.wait_ge(hready.h, e * STEPS + (c - 1))
                nc.scalar.activation(sg[:, c % 2, :, :].rearrange("p h t -> p (h t)"), side(c, 0), ACT.Silu)\
                    .then_inc(gated.h, 1)

    def vector(dve):
        with dve.Fori(0, NE) as e:
            for tt in range(TT):
                last = V.tensor_scalar(pick[:, tt, :], iota[:, :], slot[:, tt, bass.ds(e, 1)], None, ALU.is_equal)
            last.then_inc(picked.h, 1)
            dve.wait_ge(gathered.h, e + 1)
            V.tensor_copy(xg[:, 0:NB, :].rearrange("p j s -> p (j s)"), K.ps[2][:, 0:NB * CAP])
            V.tensor_copy(xg[:, NB:KT, :].rearrange("p j s -> p (j s)"), K.ps[3][:, 0:(KT - NB) * CAP])\
                .then_inc(xready.h, 1)
            for c in range(STEPS):
                dve.wait_ge(K.used.h, e * PER + (u0 + UP_AT[c]))
                dve.wait_ge(gated.h, e * STEPS + (c + 1))
                if c >= 2:
                    dve.wait_ge(K.used.h, e * PER + (u0 + DOWN_AT[c - 2]))
                V.tensor_tensor(hid[:, c % 2, :, :].rearrange("p h t -> p (h t)"),
                                sg[:, c % 2, :, :].rearrange("p h t -> p (h t)"), side(c, 1), ALU.mult)\
                    .then_inc(hready.h, 1)
            dve.wait_ge(K.used.h, e * PER + (u0 + PER))
            for h in range(2):
                last = V.tensor_copy(y[:, h * 512:(h + 1) * 512], K.ps[h][0:CAP, :])
            last.then_inc(yready.h, 1)
            dve.wait_ge(scattered.h, e + 1)
            for tt in range(TT):
                for h in range(2):
                    a = acc[:, tt, h * 512:(h + 1) * 512]
                    last = V.scalar_tensor_tensor(a, K.ps[2 + 2 * tt + h][:, :], gates[:, tt, bass.ds(e, 1)], a,
                                                  ALU.mult, ALU.add)
            last.then_inc(free.h, 1)
            dve.wait_ge(free.h, e + 2)

    return tensor, scalar, vector


FC = 2816
T2 = 2 * T
EPS = 1e-6


def adaln(K, coef, grow):
    nc, i = K.nc, K.i
    V = nc.vector
    with ExitStack() as st:
        cT, hot, mod, ab, ng = scratch(K, st, [P, KT, 2], [2, 2, P], [2, 4, 512], [P, 2, 4, KT], [P, 2, 4, KT])
        grb, gng = scratch(K, st, [P, 4, D], [P, 4, D])
        load_phase(K, [(cT[:, :, :], i["c_cols"]), (ab[:, :, :, :], i["ada_b_cols"]), (ng[:, :, :, :], i["norm_g_cols"])]
                   + [(grb[:, n, :], i["ada_b_gates"][n].partition_broadcast(P)) for n in range(4)]
                   + [(gng[:, n, :], i["norm_g_gates"][n].partition_broadcast(P)) for n in range(4)])
        hotted, sil, gread, copied, done = K.sig(5)
        with K.begin() as block:
            @block.scalar
            def _(act):
                nc.scalar.activation(cT[:, :, :], cT[:, :, :], ACT.Silu).then_inc(*sil.up())
                for b in range(24):
                    act.wait_ge(*K.used.at(2 * b + 2))
                    if b >= 4:
                        act.wait_ge(*done.at((b - 4) // 2 + 1))
                    nc.scalar.activation(mod[:, b % 4, :], K.ps[6 + b % 2][0:2, :], ACT.Copy).then_inc(*copied.up())

            @block.tensor
            def _(pe):
                def spread(n):
                    l, p = divmod(n, 6)
                    pe.wait_ge(*copied.at(2 * n + 2))
                    if p in (2, 5):
                        if n > 2:
                            pe.wait_ge(*gread.at(2 * l + (p == 5)))
                        for who in range(2 - l):
                            for h in range(2):
                                last = nc.tensor.matmul(K.ps[1 + who * 2 + h][:, :], hot[:, who, :],
                                                        mod[:, (2 * n + h) % 4, :], start=True, stop=True)
                    else:
                        for j in range(KT):
                            o = 2 * ((p if p < 2 else p - 1) * KT + j)
                            last = nc.tensor.transpose(K.ps[5 * l][:, o:o + 2],
                                                       mod[:, (2 * n + j // 4) % 4, j % 4 * P:j % 4 * P + P],
                                                       K.ident[0:2, 0:2])
                    last.then_inc(*done.up())

                pe.wait_ge(*sil.at(1))
                pe.wait_ge(*hotted.at(1))
                for b in range(26):
                    if b < 24:
                        if b >= 2:
                            pe.wait_ge(*copied.at(b - 1))
                        for c in range(2):
                            w = K.chunk(pe).rearrange("p (k n) -> p k n", k=KT)
                            for k in range(KT):
                                last = nc.tensor.matmul(K.ps[6 + b % 2][0:2, c * 256:c * 256 + 256], cT[:, k, :],
                                                        w[:, k, :], start=(k == 0), stop=(k == KT - 1))
                            last.then_inc(*K.used.up())
                    if b >= 3 and b % 2:
                        spread((b - 3) // 2)

            @block.vector
            def _(dve):
                for who in range(2):
                    last = V.tensor_copy(hot[:, who, :], bc(K.ident[0:2, who:who + 1], [2, P]))
                last.then_inc(*hotted.up())
                row = 0
                for l in range(2):
                    for g in range(2):
                        dve.wait_ge(*done.at(6 * l + 3 * g + 3))
                        for who in range(2 - l):
                            for b in range(2):
                                s = slice(b * 512, b * 512 + 512)
                                K.v(dve, V.tensor_tensor(grow[:, row, s], K.ps[1 + who * 2 + b][:, :],
                                                         grb[:, 2 * l + g, s], ALU.add))
                            if who == 1 - l:
                                K.v(dve, V.memset(K.junk[:, 0:1], 0.0), gread)
                            K.v(dve, V.tensor_tensor(grow[:, row, :], grow[:, row, :], gng[:, 2 * l + g, :], ALU.mult))
                            row += 1
                    m = K.ps[5 * l][:, 0:64].rearrange("p (q j w) -> p q j w", q=4, w=2)
                    for n in range(2):
                        for who in range(2):
                            K.v(dve, V.tensor_tensor(coef[:, l, n, who, 1, :], m[:, 2 * n, :, who], ab[:, l, 2 * n, :],
                                                     ALU.add))
                            s = coef[:, l, n, who, 0, :]
                            K.v(dve, V.tensor_tensor(s, m[:, 2 * n + 1, :, who], ab[:, l, 2 * n + 1, :], ALU.add))
                            K.v(dve, V.scalar_tensor_tensor(s, s, 1.0, ng[:, l, 2 * n, :], ALU.add, ALU.mult))

            @block.sync
            def _(sp):
                K.stream(sp)


def rms_phase(K, st, srcs, finish):
    nc = K.nc
    width = srcs[0].shape[1]
    junk, ss = scratch(K, st, [P, width], [P, len(srcs)])
    sqd, ask, given = K.sig(3)
    with K.begin() as block:
        @block.scalar
        def _(act):
            for n, src in enumerate(srcs):
                K.a(act, nc.scalar.activation(junk[:, :], src, ACT.Square, accum_out=ss[:, n:n + 1]), sqd)
            roots(K, act, ask, given, [ss[:, n:n + 1] for n in range(len(srcs))])

        @block.vector
        def _(dve):
            for n in range(len(srcs)):
                dve.wait_ge(*sqd.at(n + 1))
                r = ss[:, n:n + 1]
                rsqrt(K, dve, nc.vector.tensor_scalar(r, r, 1.0 / width, EPS, ALU.mult, ALU.add), r, (ask, given))
                finish(dve, n, r)

        @block.sync
        def _(sp):
            K.stream(sp)


def norm_to_cols(K, x, xn, hT, tts, coef):
    V, nc = K.nc.vector, K.nc
    with ExitStack() as st:
        rms_phase(K, st, [x[:, tt, :] for tt in range(tts)], lambda dve, n, r: K.v(dve, V.tensor_scalar(
            xn[:, n, :], x[:, n, :], r, None, ALU.mult)))
    to_cols(K, lambda tt, j: xn[:, tt, j * P:(j + 1) * P], None, KT, tts=tts,
            evac=lambda j, tt, src: nc.scalar.activation(
                hT[:, j, tt * P:(tt + 1) * P], src, ACT.Identity, bias=coef[:, tt // TT, 1, j:j + 1],
                scale=coef[:, tt // TT, 0, j:j + 1]))


def gated_residual(K, x, y, tts, gates):
    V = K.nc.vector
    with ExitStack() as st:
        def fin(dve, n, r):
            K.v(dve, V.scalar_tensor_tensor(y[:, n, :], y[:, n, :], r, gates[n // TT], ALU.mult, ALU.mult))
            K.v(dve, V.tensor_tensor(x[:, n, :], x[:, n, :], y[:, n, :], ALU.add))

        rms_phase(K, st, [y[:, tt, :] for tt in range(tts)], fin)


def keep_rows(K, y):
    return lambda dve, tt, h, o: K.nc.vector.tensor_copy(y[:, tt, h * 512:(h + 1) * 512], o)


def conv_ffn(K, x, l, tts, coef, gates):
    i = K.i
    with ExitStack() as st:
        hT, hid, cw, cb = scratch(K, st, [P, KT, tts * P], [P, FC // P, tts * P], [P, 2 * FC // P, 3], [P, 2 * FC // P])
        load_phase(K, [(cw[:, :, :], i["ffn_conv_w"][l]), (cb[:, :], i["ffn_conv_b"][l])])
        xn = hid[:, 0:KT, :].rearrange("p j t -> p (j t)").rearrange("p (t d) -> p t d", d=D)
        norm_to_cols(K, x, xn, hT, tts, coef)
        with ExitStack() as st2:
            gated_hidden(K, st2, hT[:, :, :], hid, FC // 256, conv=(cw, cb))
        y = hT[:, :, :].rearrange("p j t -> p (j t)").rearrange("p (t d) -> p t d", d=D)
        linear_rows(K, hid, range(FC // P), keep_rows(K, y), tts=tts)
        gated_residual(K, x, y, tts, gates)


def linear_rows512(K, x, outs):
    nc = K.nc
    read, = K.sig(1)
    with K.begin() as block:
        @block.tensor
        def _(pe):
            for m in range(len(outs)):
                if m >= 2:
                    pe.wait_ge(*read.at(m - 1))
                for c in range(2):
                    w = K.chunk(pe).rearrange("p (k n) -> p k n", k=4)
                    for k in range(4):
                        for tt in range(4):
                            last = nc.tensor.matmul(K.ps[m % 2 * 4 + tt][:, :],
                                                    x[:, 4 * c + k, tt * P:(tt + 1) * P], w[:, k, :],
                                                    start=(c == 0 and k == 0), stop=(c == 1 and k == 3))
                    last.then_inc(*K.used.up())

        @block.vector
        def _(dve):
            for m, o in enumerate(outs):
                dve.wait_ge(*K.used.at(2 * m + 2))
                for tt in range(4):
                    last = nc.vector.tensor_copy(o[:, tt, :], K.ps[m % 2 * 4 + tt][:, :])
                K.v(dve, last, read)

        @block.sync
        def _(sp):
            K.stream(sp)


def even_layer(K, x4, coef, grow):
    nc, i = K.nc, K.i
    V = nc.vector
    with ExitStack() as st:
        units, = scratch(K, st, [P, 11, CH])
        two = lambda n, pat="p u (j t) -> p (u j) t", **kw: units[:, n:n + 2, :].rearrange(pat, **(kw or {"t": T2}))
        one = lambda n, **kw: units[:, n, :].rearrange("p (j t) -> p j t", **(kw or {"t": T2}))
        yT, hT = two(0), two(2)
        naq, nak, nav = one(4), one(5), one(6)
        raw, mlv, mlo = two(7), one(9), one(10)
        cw, cb, gw, gb = scratch(K, st, [P, KT, 3], [P, KT], [P, KT, 16], [P, 16])
        load_phase(K, [(cw[:, :, :], i["ev_conv_w"]), (cb[:, :], i["ev_conv_b"]), (gw[:, :, :], i["ev_w_gates"]),
                       (gb[:, :], i["ev_gate_b"].partition_broadcast(P))])
        norm_to_cols(K, x4, two(4, "p u (a d) -> p (u a) d", d=D), hT, 4, coef[:, 0, 0])
        keep = lambda dst, f=1.0: lambda act, c, h, o: nc.scalar.activation(dst[:, 2 * c + h, :], o, ACT.Copy, scale=f)
        linear_cols(K, [(hT, 2, keep(naq, 64 ** -0.5)), (hT, 2, keep(nak)), (hT, 4, keep(raw))])
        linear_rows512(K, hT, [nav, mlv, mlo])
        G8, lf, tmp, bb, tot, u8 = scratch(K, st, [P, 4, 2, 2, 4], *[[P, 4, 2, 4]] * 5)
        tri, mask, window = scratch(K, st, [P, 2, P], [P, 2, P], [P, 64])
        load_phase(K, [(window[:, :], i["window"]), (tri[:, :, :], i["ml_tri"]), (mask[:, :, :], i["ml_mask"])])
        SEQ = ((2, 3, 0, 1), (3, 2, 1, 0))
        pg, ve, ae, pb = K.sig(4)
        with K.begin() as block:
            @block.tensor
            def _(pe):
                for tt in range(4):
                    for k in range(KT):
                        last = nc.tensor.matmul(K.ps[0][:, tt * 16:(tt + 1) * 16], hT[:, k, tt * P:(tt + 1) * P],
                                                gw[:, k, :], start=(k == 0), stop=(k == KT - 1))
                last.then_inc(*pg.up())
                pe.wait_ge(*ve.at(3))
                for d in range(2):
                    nc.tensor.matmul(K.ps[1][:, d * 16:(d + 1) * 16], tri[:, d, :], lf[:, :, d, :], start=True, stop=True)
                nc.tensor.matmul(K.ps[1][:, 32:64], K.ones[:, :], lf[:, :, :, :].rearrange("p s d h -> p (s d h)"),
                                 start=True, stop=True).then_inc(*pb.up())

            @block.vector
            def _(dve):
                dve.wait_ge(*pg.at(1))
                for d in range(2):
                    for s in range(4):
                        c = SEQ[d][s] * 16 + 8 * d
                        K.v(dve, V.tensor_tensor(G8[:, s, d, :, :].rearrange("p a h -> p (a h)"), K.ps[0][:, c:c + 8],
                                                 gb[:, 8 * d:8 * d + 8], ALU.add))
                f = G8[:, :, :, 1, :]
                K.v(dve, V.tensor_scalar(tmp[:, :, :, :], f, -1.0, None, ALU.mult))
                K.v(dve, V.tensor_tensor(tmp[:, :, :, :], tmp[:, :, :, :], f, ALU.min), ve)
                dve.wait_ge(*ae.at(1))
                K.v(dve, V.tensor_scalar(tmp[:, :, :, :], tmp[:, :, :, :], 1.0, None, ALU.add), ve)
                dve.wait_ge(*ae.at(2))
                K.v(dve, V.tensor_scalar(lf[:, :, :, :], f, 0.0, None, ALU.min))
                K.v(dve, V.tensor_tensor(lf[:, :, :, :], lf[:, :, :, :], tmp[:, :, :, :], ALU.subtract), ve)
                dve.wait_ge(*pb.at(1))
                for d in range(2):
                    K.v(dve, V.tensor_copy(bb[:, :, d, :], K.ps[1][:, d * 16:(d + 1) * 16].rearrange(
                        "p (s h) -> p s h", s=4)))
                K.v(dve, V.tensor_copy(tot[:, :, :, :].rearrange("p s d h -> p (s d h)"), K.ps[1][:, 32:64]))
                K.v(dve, V.tensor_tensor(u8[:, :, :, :], G8[:, :, :, 0, :], bb[:, :, :, :], ALU.subtract))

            @block.scalar
            def _(act):
                act.wait_ge(*ve.at(1))
                K.a(act, nc.scalar.activation(tmp[:, :, :, :], tmp[:, :, :, :], ACT.Exp), ae)
                act.wait_ge(*ve.at(2))
                K.a(act, nc.scalar.activation(tmp[:, :, :, :], tmp[:, :, :, :], ACT.Ln), ae)

            @block.sync
            def _(sp):
                K.stream(sp)

        neighbourhood(K, naq, nak, nav, units[:, 2:4, :].rearrange("p u (a k) -> p (u a) k", k=T), window[:, :],
                      yT)

        cqk = two(2)
        cv, = K.sig(1)
        with K.begin() as block:
            @block.vector
            def _(dve):
                for j in range(KT):
                    K.v(dve, V.tensor_scalar(cqk[:, j, :], raw[:, j, :], cw[:, j, 1:2], cb[:, j:j + 1], ALU.mult, ALU.add))
                    for tap, dst, src in ((0, slice(1, T), slice(0, T - 1)), (2, slice(0, T - 1), slice(1, T))):
                        o = cqk[:, j, :].rearrange("p (q t) -> p q t", q=2)[:, :, dst]
                        r = raw[:, j, :].rearrange("p (q t) -> p q t", q=2)[:, :, src]
                        K.v(dve, V.scalar_tensor_tensor(o, r, cw[:, j, tap:tap + 1], o, ALU.mult, ALU.add),
                            cv if tap else None)

            @block.scalar
            def _(act):
                for j in range(KT):
                    act.wait_ge(*cv.at(j + 1))
                    K.a(act, nc.scalar.activation(cqk[:, j, :], cqk[:, j, :], ACT.Silu))
                K.a(act, nc.scalar.activation(cqk[:, 0:4, :], cqk[:, 0:4, :], ACT.Copy, scale=P ** -0.5))
                K.a(act, nc.scalar.activation(mlo[:, :, :], mlo[:, :, :], ACT.Sigmoid))

            @block.sync
            def _(sp):
                K.stream(sp)
        krow, hf, hb = one(4), one(5), one(6)
        to_cols(K, lambda tt, j: cqk[:, 4 + j, tt * P:(tt + 1) * P], lambda j, tt: krow[:, tt, j * P:(j + 1) * P], 4, tts=4)
        mlstm(K, cqk, krow, mlv, (hf, hb), one(7, t=P), one(8, t=P), bb, tot, u8, mask, SEQ)

        mg, st_, mv, rs = scratch(K, st, [P, 512], [P, 12], [P, 4, 2], [P, 4])
        load_phase(K, [(mg[:, :], i["ev_ml_norm_g"].partition_broadcast(P))])
        sqrts = K.sig(2)
        with K.begin() as block:
            @block.vector
            def _(dve):
                K.v(dve, V.tensor_tensor(hf, hf, hb, ALU.add))
                K.v(dve, V.tensor_tensor(hf, hf, mlo, ALU.mult))
                for tt in range(4):
                    z = hf[:, tt, :].rearrange("p (n w) -> p n w", n=4)
                    layer_norm(K, dve, z, z, (st_, mv, rs), mg[:, :], None, P, 4, EPS, sqrts)

            @block.scalar
            def _(act):
                roots(K, act, *sqrts, [rs[:, :]] * 4)

            @block.sync
            def _(sp):
                K.stream(sp)
        to_cols(K, lambda tt, j: hf[:, tt, j * P:(j + 1) * P], lambda j, tt: yT[:, 4 + j, tt * P:(tt + 1) * P], 4, tts=4)
        y = two(2, "p u (a d) -> p (u a) d", d=D)
        linear_rows(K, yT, range(KT), keep_rows(K, y), tts=4, depth=0)
        gated_residual(K, x4, y, 4, [grow[:, 0, :], grow[:, 1, :]])


def neighbourhood(K, q, k, v, bias, window, yT):
    nc, i = K.nc, K.i
    b5 = bias.rearrange("p (h q) (r c) -> p h q r c", q=TT, c=64)
    with K.begin() as block:
        @block.scalar
        def _(act):
            for qr in range(4):
                for h in range(8):
                    act.dma_start(b5[64 * (qr % 2):64 * (qr % 2) + 64, h, qr // 2, :, :],
                                  i["rpb"][h, 7 - qr:11 - qr, :, :].rearrange("r q k -> q r k"))\
                        .then_inc(*K.load.up(16))
            act.wait_ge(*K.load.now())

        @block.vector
        def _(dve):
            dve.wait_ge(*K.load.now())
            K.v(dve, nc.vector.tensor_tensor(bias.rearrange("p u (r c) -> p (u r) c", c=64),
                                             bias.rearrange("p u (r c) -> p (u r) c", c=64),
                                             bc(window.unsqueeze(1), [P, 64, 64]), ALU.add))

        @block.sync
        def _(sp):
            K.stream(sp)
    units, outs = [], []
    for j in range(4):
        for ctx in range(2):
            for h in (2 * j, 2 * j + 1):
                r = slice(64 * (h % 2), 64 * (h % 2) + 64)
                for qt in range(TT):
                    c = (2 * ctx + qt) * P
                    keys = range(2 * ctx, 4)
                    units.append((q[r, j, c:c + P], k[r, j, keys[0] * P:T2], [v[:, b, h * 64:(h + 1) * 64] for b in keys],
                                  None if ctx else bias[:, 2 * h + qt, :]))
            outs.append(yT[:, j, ctx * T:(ctx + 1) * T])
    with ExitStack() as st:
        attention(K, st, units, outs)


def mlstm(K, cqk, krow, vrow, hout, ua, ub, bb, tot, u8, mask, SEQ):
    nc = K.nc
    V = nc.vector
    diag, W = ua[:, 0:8, :], ua[:, 8:16, :]
    qkw, qkT = ub[:, 0:8, :], ub[:, 8:16, :]
    with ExitStack() as st:
        Ct, Kw, args, sm = scratch(K, st, [P, 8, P], [P, 8, P], [P, 4, 8], [P, 8, 8])
        n_st, m_st, umax, mu, top, den, neg, rden = (sm[:, n, :] for n in range(8))
        sU, pU, sW, aW, pQ, vQ, pT, aT, pN, vK, pS, vS = K.sig(12)
        b3 = lambda a, n=8: bc(a.unsqueeze(2), [P, n, P])
        bank = lambda b: K.ps[b][:, :].rearrange("p (h s) -> p h s", h=4)
        with K.begin() as block:
            @block.tensor
            def _(pe):
                for k in range(4):
                    pe.wait_ge(*sU.at(k + 1))
                    for d in range(2):
                        last = nc.tensor.matmul(K.ps[d][:, :], K.ones[:, :],
                                                diag[:, 4 * d:4 * d + 4, :].rearrange("p h s -> p (h s)"),
                                                start=True, stop=True)
                    last.then_inc(*pU.up())
                    if k:
                        pe.wait_ge(*vS.at(k))
                    unit = [(u, u // 4, u % 4, slice(SEQ[u // 4][k] * P, SEQ[u // 4][k] * P + P), SEQ[u // 4][k])
                            for u in range(8)]
                    for u, d, h, t, _ in unit:
                        last = nc.tensor.matmul(K.ps[2 + d][:, h * P:(h + 1) * P], cqk[:, h, t], cqk[:, 4 + h, t],
                                                start=True, stop=True)
                    last.then_inc(*pQ.up())
                    pe.wait_ge(*vQ.at(k + 1))
                    for u, d, h, t, _ in unit:
                        last = nc.tensor.transpose(K.ps[d][:, h * P:(h + 1) * P], qkw[:, u, :], K.ident[:, :])
                    last.then_inc(*pT.up())
                    pe.wait_ge(*aT.at(k + 1))
                    for u, d, h, t, tt in unit:
                        nc.tensor.matmul(K.ps[4 + d][:, h * P:(h + 1) * P], qkT[:, u, :], vrow[:, tt, h * P:(h + 1) * P],
                                         start=True, stop=True)
                        nc.tensor.matmul(K.ps[6 + d][:, h * P:(h + 1) * P], cqk[:, h, t], Ct[:, u, :],
                                         start=True, stop=True)
                        last = nc.tensor.matmul(K.ps[2][:, u:u + 1], cqk[:, h, t], n_st[:, u:u + 1],
                                                start=True, stop=True)
                    last.then_inc(*pN.up())
                    pe.wait_ge(*vK.at(k + 1))
                    for u, d, h, t, tt in unit:
                        nc.tensor.matmul(K.ps[d][:, h * P:(h + 1) * P], Kw[:, u, :], vrow[:, tt, h * P:(h + 1) * P],
                                         start=True, stop=True)
                        last = nc.tensor.matmul(K.ps[3][:, u:u + 1], Kw[:, u, :], K.ones[:, 0:1], start=True, stop=True)
                    last.then_inc(*pS.up())

            @block.vector
            def _(dve):
                K.v(dve, V.memset(Ct[:, :, :], 0.0))
                K.v(dve, V.memset(sm[:, :, :], 0.0))
                for k in range(4):
                    flat = lambda a: a[:, k, :, :].rearrange("p d h -> p (d h)")
                    b8, t8, w8 = flat(bb), flat(tot), flat(u8)
                    K.v(dve, V.tensor_tensor(diag, bc(K.ident[:, :].unsqueeze(1), [P, 8, P]), b3(w8), ALU.mult), sU)
                    dve.wait_ge(*pU.at(k + 1))
                    for d in range(2):
                        K.v(dve, V.reduce_max(umax[:, 4 * d:4 * d + 4], bank(d), AX))
                        K.v(dve, V.tensor_tensor(W[:, 4 * d:4 * d + 4, :], bank(d),
                                                 bc(mask[:, d, :].unsqueeze(1), [P, 4, P]), ALU.add))
                    K.v(dve, V.reduce_max(mu, W, AX))
                    K.v(dve, V.tensor_tensor(mu, mu, m_st, ALU.max))
                    K.v(dve, V.tensor_tensor(top, umax, m_st, ALU.max))
                    K.v(dve, V.tensor_tensor(W, W, b3(mu), ALU.subtract))
                    K.v(dve, V.tensor_tensor(args[:, 0, :], m_st, mu, ALU.subtract))
                    K.v(dve, V.scalar_tensor_tensor(args[:, 1, :], b8, -1.0, mu, ALU.mult, ALU.subtract))
                    K.v(dve, V.tensor_tensor(args[:, 2, :], m_st, top, ALU.subtract))
                    K.v(dve, V.tensor_tensor(args[:, 3, :], w8, top, ALU.subtract), sW)
                    dve.wait_ge(*aW.at(k + 1))
                    dve.wait_ge(*pQ.at(k + 1))
                    for d in range(2):
                        last = V.tensor_tensor(qkw[:, 4 * d:4 * d + 4, :], bank(2 + d), W[:, 4 * d:4 * d + 4, :], ALU.mult)
                    K.v(dve, last, vQ)
                    for d in range(2):
                        last = V.tensor_tensor(Kw[:, 4 * d:4 * d + 4, :],
                                               krow[:, SEQ[d][k], :].rearrange("p (h e) -> p h e", h=4),
                                               b3(args[:, 3, 4 * d:4 * d + 4], 4), ALU.mult)
                    K.v(dve, last, vK)
                    K.v(dve, V.reduce_sum(den, qkw, AX))
                    dve.wait_ge(*pN.at(k + 1))
                    K.v(dve, V.tensor_tensor(neg, K.ps[2][:, 0:8], args[:, 0, :], ALU.mult))
                    K.v(dve, V.tensor_tensor(den, den, neg, ALU.add))
                    K.v(dve, V.tensor_scalar(neg, den, -1.0, None, ALU.mult))
                    K.v(dve, V.tensor_tensor(den, den, neg, ALU.max))
                    K.v(dve, V.tensor_tensor(den, den, args[:, 1, :], ALU.max))
                    K.v(dve, V.reciprocal(rden, den))
                    for d in range(2):
                        o = hout[d][:, SEQ[d][k], :].rearrange("p (h e) -> p h e", h=4)
                        s = slice(4 * d, 4 * d + 4)
                        K.v(dve, V.tensor_tensor(o, bank(6 + d), b3(args[:, 0, s], 4), ALU.mult))
                        K.v(dve, V.tensor_tensor(o, o, bank(4 + d), ALU.add))
                        K.v(dve, V.tensor_tensor(o, o, b3(rden[:, s], 4), ALU.mult))
                    K.v(dve, V.tensor_tensor(Ct[:, :, :], Ct[:, :, :], b3(args[:, 2, :]), ALU.mult))
                    K.v(dve, V.tensor_tensor(n_st, n_st, args[:, 2, :], ALU.mult))
                    K.v(dve, V.tensor_tensor(m_st, t8, top, ALU.add))
                    dve.wait_ge(*pS.at(k + 1))
                    for d in range(2):
                        K.v(dve, V.tensor_tensor(Ct[:, 4 * d:4 * d + 4, :], Ct[:, 4 * d:4 * d + 4, :], bank(d), ALU.add))
                    K.v(dve, V.tensor_tensor(n_st, n_st, K.ps[3][:, 0:8], ALU.add), vS)

            @block.scalar
            def _(act):
                for k in range(4):
                    act.wait_ge(*sW.at(k + 1))
                    K.a(act, nc.scalar.activation(W, W, ACT.Exp))
                    K.a(act, nc.scalar.activation(args[:, :, :], args[:, :, :], ACT.Exp), aW)
                    act.wait_ge(*pT.at(k + 1))
                    if k:
                        act.wait_ge(*pN.at(k))
                    for d in range(2):
                        last = nc.scalar.activation(qkT[:, 4 * d:4 * d + 4, :], bank(d), ACT.Copy)
                    K.a(act, last, aT)

            @block.sync
            def _(sp):
                K.stream(sp)


def odd_layer(K, x4, coef, grow):
    nc, i = K.nc, K.i
    V = nc.vector
    H, QK = 16, 96
    with ExitStack() as st:
        kT, qT, vr = scratch(K, st, [P, H, T2], [P, H, T], [P, 4, D])
        cqT, ckvT, oT, g = scratch(K, st, [P, 2, T], [P, T2], [P, KT, T], [P, 3])
        xn = kT[:, 0:8, :].rearrange("p j t -> p (j t)").rearrange("p (t d) -> p t d", d=D)
        hT = kT[:, 8:16, :]
        with ExitStack() as st1:
            wkv, wq = scratch(K, st1, [P, KT, 160], [P, KT, T])
            ckv, cq, rope, t4 = scratch(K, st1, [P, 4, 160], [P, TT, T], [P, TT, 2, 2, 8], [P, 4, 2, 8])
            load_phase(K, [(wkv[:, :, :], i["od_w_dkv"]), (wq[:, :, :], i["od_w_dq"]), (g[:, :], i["od_norm_g"]),
                           (rope[:, :, :, :, :], i["rope"])])
            norm_to_cols(K, x4, xn, hT, 4, coef[:, 1, 0])
            low, = K.sig(1)
            with K.begin() as block:
                @block.tensor
                def _(pe):
                    for tt in range(4):
                        for w, b, n in ((wkv, tt, 160), (wq, 4 + tt, T))[:2 if tt < TT else 1]:
                            for k in range(KT):
                                last = nc.tensor.matmul(K.ps[b][:, 0:n], hT[:, k, tt * P:(tt + 1) * P], w[:, k, :],
                                                        start=(k == 0), stop=(k == KT - 1))
                    last.then_inc(*low.up())

                @block.vector
                def _(dve):
                    dve.wait_ge(*low.at(1))
                    for tt in range(4):
                        K.v(dve, V.tensor_copy(ckv[:, tt, :], K.ps[tt][:, 0:160]))
                        if tt < TT:
                            K.v(dve, V.tensor_copy(cq[:, tt, :], K.ps[4 + tt][:, 0:T]))
                            rotate(K, dve, ckv[:, tt, 128:160].unsqueeze(1), rope[:, tt], t4)

                @block.sync
                def _(sp):
                    K.stream(sp)
            for t, n, w in ((ckv, 4, P), (cq, TT, T)):
                with ExitStack() as s2:
                    rms_phase(K, s2, [t[:, tt, 0:w] for tt in range(n)], lambda dve, m, r, t=t, w=w: K.v(
                        dve, V.tensor_scalar(t[:, m, 0:w], t[:, m, 0:w], r, None, ALU.mult)))
            to_cols(K, lambda tt, j: ckv[:, tt, 0:P], None, 1, tts=4, evac=lambda j, tt, src: nc.scalar.activation(
                ckvT[:, tt * P:(tt + 1) * P], src, ACT.Copy, scale=g[:, 2:3]))
            to_cols(K, lambda tt, j: cq[:, tt, j * P:(j + 1) * P], None, 2, evac=lambda j, tt, src: nc.scalar.activation(
                cqT[:, j, tt * P:(tt + 1) * P], src, ACT.Copy, scale=g[:, j:j + 1]))
            to_cols(K, lambda tt, j: ckv[:, tt, P:160], None, 1, tts=4, width=32,
                    evac=lambda j, tt, src: nc.scalar.activation(
                        kT[64:96, :, tt * P:(tt + 1) * P], bc(src.unsqueeze(1), [32, H, P]), ACT.Copy))
        with ExitStack() as st1:
            wuk, wuv, wuq, qr = scratch(K, st1, [P, D], [P, D], [P, 2, H * QK], [P, TT, H * QK])
            rope, t4 = scratch(K, st1, [P, TT, 2, 2, 8], [P, 4, H * 8])
            load_phase(K, [(wuk[:, :], i["od_w_uk"]), (wuv[:, :], i["od_w_uv"]), (wuq[:, :, :], i["od_w_uq"]),
                           (rope[:, :, :, :, :], i["rope"])])
            kd, kr, vd, qd = K.sig(4)
            with K.begin() as block:
                @block.tensor
                def _(pe):
                    for h in range(H):
                        if h >= 2:
                            pe.wait_ge(*kr.at(h - 1))
                        nc.tensor.matmul(K.ps[h % 2][0:64, :], wuk[:, h * 64:(h + 1) * 64], ckvT[:, :],
                                         start=True, stop=True).then_inc(*kd.up())
                    for tt in range(4):
                        for b in range(2):
                            n = 2 * tt + b
                            if n >= 3:
                                pe.wait_ge(*vd.at(n - 2))
                            nc.tensor.matmul(K.ps[2 + n % 3][:, :], ckvT[:, tt * P:(tt + 1) * P],
                                             wuv[:, b * 512:(b + 1) * 512], start=True, stop=True).then_inc(*qd.up())
                    for tt in range(TT):
                        for b in range(3):
                            n = 3 * tt + b
                            if n >= 3:
                                pe.wait_ge(*vd.at(8 + n - 2))
                            for k in range(2):
                                last = nc.tensor.matmul(K.ps[5 + b][:, :], cqT[:, k, tt * P:(tt + 1) * P],
                                                        wuq[:, k, b * 512:(b + 1) * 512], start=(k == 0), stop=(k == 1))
                            last.then_inc(*qd.up())

                @block.scalar
                def _(act):
                    for h in range(H):
                        act.wait_ge(*kd.at(h + 1))
                        nc.scalar.activation(kT[0:64, h, :], K.ps[h % 2][0:64, :], ACT.Copy).then_inc(*kr.up())
                    act.wait_ge(*kr.now())

                @block.vector
                def _(dve):
                    for n in range(14):
                        dve.wait_ge(*qd.at(n + 1))
                        dst, src = ((vr[:, n // 2, n % 2 * 512:n % 2 * 512 + 512], 2 + n % 3) if n < 8 else
                                    (qr[:, (n - 8) // 3, (n - 8) % 3 * 512:(n - 8) % 3 * 512 + 512], 5 + (n - 8) % 3))
                        K.v(dve, V.tensor_copy(dst, K.ps[src][:, :]), vd)
                    for tt in range(TT):
                        rotate(K, dve, qr[:, tt, :].rearrange("p (h e) -> p h e", h=H)[:, :, 64:96], rope[:, tt],
                               t4[:, :, :])

                @block.sync
                def _(sp):
                    K.stream(sp)
            to_cols(K, lambda tt, j: qr[:, tt, j * QK:(j + 1) * QK], None, H, width=QK,
                    evac=lambda j, tt, src: nc.scalar.activation(qT[0:QK, j, tt * P:(tt + 1) * P], src, ACT.Copy,
                                                                 scale=QK ** -0.5))
        units = [(qT[0:QK, h, qt * P:(qt + 1) * P], kT[0:QK, h, :], [vr[:, b, h * 64:(h + 1) * 64] for b in range(4)], None)
                 for h in range(H) for qt in range(TT)]
        with ExitStack() as st1:
            attention(K, st1, units, [oT[:, j, :] for j in range(KT)])
        y = qT[:, 0:8, :].rearrange("p j t -> p (j t)").rearrange("p (t d) -> p t d", d=D)
        linear_rows(K, oT, range(KT), keep_rows(K, y), depth=1)
        gated_residual(K, x4, y, TT, [grow[:, 4, :]])


def rotate(K, dve, x, table, tmp):
    V = K.nc.vector
    n = x.shape[1]
    for ax in range(2):
        lo, hi = x[:, :, 16 * ax:16 * ax + 8], x[:, :, 16 * ax + 8:16 * ax + 16]
        cos, sin = (bc(table[:, f, ax, :].unsqueeze(1), [P, n, 8]) for f in range(2))
        t = [tmp[:, m].rearrange("p a b -> p (a b)")[:, 0:8 * n] if len(tmp.shape) == 4 else tmp[:, m, 0:8 * n]
             for m in range(4)]
        t = [a.rearrange("p (n e) -> p n e", n=n) for a in t]
        for m, (a, b) in enumerate(((lo, cos), (hi, sin), (lo, sin), (hi, cos))):
            K.v(dve, V.tensor_tensor(t[m], a, b, ALU.mult))
        K.v(dve, V.tensor_tensor(lo, t[0], t[1], ALU.subtract))
        K.v(dve, V.tensor_tensor(hi, t[2], t[3], ALU.add))


def second_stack(K, x4):
    coef, grow = scratch(K, K.ctx, [P, 2, 2, 2, 2, KT], [P, 6, D])
    load_phase(K, [(x4[:, TT:2 * TT, :], K.i["ctx_rows"])])
    adaln(K, coef, grow)
    even_layer(K, x4, coef, grow)
    conv_ffn(K, x4, 0, 4, coef[:, 0, 1], [grow[:, 2, :], grow[:, 3, :]])
    odd_layer(K, x4, coef, grow)
    conv_ffn(K, x4, 1, TT, coef[:, 1, 1], [grow[:, 5, :]])


def store_rows(K, rows):
    with K.begin() as block:
        @block.sync
        def _(sp):
            sp.dma_start(K.out.rearrange("o (t p) d -> p (o t) d", p=P), rows[:, 0:TT, :]).then_inc(*K.load.up(16))
            sp.wait_ge(*K.load.now())


def build(nc, i, out):
    with ExitStack() as ctx:
        K = Kern(nc, ctx, i, out)
        plan = K.plan
        chunks = lambda name, *r: plan.extend(i[name][n] for n in range(*(r or (i[name].shape[0],))))
        chunks("w_rkv_cols")
        chunks("w_rkv_rows")
        chunks("rwkv_w_out")
        chunks("ffn_w_in")
        chunks("ffn_w_down")
        chunks("moba_qk")
        chunks("moba_v")
        chunks("moba_o")
        chunks("moe_w")
        chunks("ada_w")
        chunks("ev_cols")
        chunks("ev_rows")
        chunks("ev_w_out")
        chunks("ffn_up", 0, 22)
        chunks("ffn_down", 0, 11)
        chunks("od_w_o")
        chunks("ffn_up", 22, 44)
        chunks("ffn_down", 11, 22)
        x4 = ctx.enter_context(nc.sbuf_tensor("x4", [P, 2 * TT, D], F32))
        ha, hb = x4[:, 0:TT, :], x4[:, TT:2 * TT, :]
        constants(K)
        rwkv(K, hb)
        with ExitStack() as st:
            hT, hid = scratch(K, st, [P, KT, T], [P, FF // P, T])
            to_cols(K, lambda tt, j: hb[:, tt, j * P:(j + 1) * P], lambda j, tt: hT[:, j, tt * P:(tt + 1) * P], KT)
            gated_hidden(K, st, hT[:, :, :], hid, FF // 256)
            project_residual_norm(K, st, hid, FF // P, hb, ha, 1)
        causal_attention(K, ha, hb)
        moe(K, hb, ha)
        second_stack(K, x4)
        store_rows(K, x4)


def by_cols(np, w):
    k, n = w.shape
    return np.ascontiguousarray(w.reshape(k // P, P, n // 256, 256).transpose(2, 1, 0, 3)).reshape(n // 256, P, -1)


def by_rows(np, w):
    k, n = w.shape
    return np.ascontiguousarray(w.reshape(k // 256, 2, P, n).transpose(0, 2, 1, 3)).reshape(k // 256, P, -1)


def interleave(np, *ws):
    return np.stack(ws, 1).reshape(-1, *ws[0].shape[1:])


def col(np, v):
    return np.ascontiguousarray(np.moveaxis(v.reshape(*v.shape[:-1], v.shape[-1] // P, P), -1, 0))


def rows_of(np, x):
    return np.ascontiguousarray(x.reshape(-1, P, x.shape[-1]).transpose(1, 0, 2))


def shape_constants(np):
    s, t = np.arange(P)[:, None], np.arange(P)[None, :]
    strict, incl = s < t, s <= t
    lv = np.stack([(s >> (l + 1) == t >> (l + 1)) & (s >> l != t >> l) for l in range(7)], 1)
    f = lambda a: np.ascontiguousarray(a.astype(np.float32))
    pos = np.arange(T)
    angle = np.stack([pos // 64, pos % 64], 1)[:, :, None].astype(np.float32) * (
        np.float32(10000.0) ** (-np.arange(8, dtype=np.float32) / 8))
    rope = np.stack([np.cos(angle), np.sin(angle)], 1).reshape(TT, P, 2, 2, 8).transpose(1, 0, 2, 3, 4)
    q, c = np.arange(P)[:, None] % 64, np.arange(64)[None, :]
    start = np.clip(q - 8, 0, 48)
    return {"rope": f(rope), "window": f(np.where((c >= start) & (c < start + 16), 0.0, NEG)),
            "ml_tri": f(np.stack([s <= t, s >= t], 1)),
            "ml_mask": f(np.stack([np.where(t <= s, 0.0, NEG), np.where(t >= s, 0.0, NEG)], 1)),
            "slots": f(np.broadcast_to(np.arange(CAP)[None, :], (P, CAP))),
            "head_block": f(s // 64 == t // 64), "head_pick": f(s // 64 == np.arange(2)[None, :]),
            "levels": f(lv), "earlier": f(np.broadcast_to(np.arange(NE)[None, :] < np.arange(NE)[:, None], (P, NE, NE))),
            "causal": f(np.where(np.arange(T)[None, None, :] <= (np.arange(TT)[None, :, None] * P + s[:, :, None]),
                                 0.0, NEG)), "tri": f(np.stack([strict, incl, strict, incl], 1))}


def lay_out(np, a):
    o = shape_constants(np)
    rkv = a["rwkv_w_rkv"][0]
    o["w_rkv_cols"] = np.concatenate([by_cols(np, rkv[0]), by_cols(np, rkv[1])])
    o["w_rkv_rows"] = by_rows(np, rkv[2])
    o["rwkv_w_out"] = by_rows(np, a["rwkv_w_out"][0])
    o["ffn_w_in"] = interleave(np, by_cols(np, a["ffn_w_gate"][0]), by_cols(np, a["ffn_w_up"][0]))
    o["ffn_w_down"] = by_rows(np, a["ffn_w_down"][0])
    x = a["x"][0]
    o["x_rows"] = rows_of(np, x)
    o["x_cols"] = np.ascontiguousarray(x.T.reshape(KT, P, T).transpose(1, 0, 2))
    o["mu_cols"] = col(np, a["rwkv_mu"][0])
    o["rwkv_cols"] = np.ascontiguousarray(np.stack([col(np, v) for v in (
        a["rwkv_decay_w0"][0], a["rwkv_iclr_a0"][0], a["rwkv_k_k"][0], a["rwkv_k_a"][0],
        a["rwkv_r_k"][0].reshape(-1))], 1))
    tiles = lambda w: np.ascontiguousarray(w.reshape(KT, P, -1).transpose(1, 0, 2))
    o["decay_w1"], o["iclr_a1"], o["gate_g1"] = (tiles(a[k][0]) for k in ("rwkv_decay_w1", "rwkv_iclr_a1", "rwkv_gate_g1"))
    o["decay_w2"], o["iclr_a2"], o["gate_g2"] = (a[k][0] for k in ("rwkv_decay_w2", "rwkv_iclr_a2", "rwkv_gate_g2"))
    o["gn_g"], o["gn_b"] = a["rwkv_gn_g"][0], a["rwkv_gn_b"][0]
    o["ln_g"], o["ln_b"] = a["ln_g"].reshape(4, D), a["ln_b"].reshape(4, D)
    o["moba_qk"] = np.concatenate([by_cols(np, a["moba_w_q"][0]), by_cols(np, a["moba_w_k"])])
    o["moba_v"], o["moba_o"] = by_rows(np, a["moba_w_v"]), by_rows(np, a["moba_w_o"][0])
    order = [("g", 0), ("u", 0)]
    for c in range(1, STEPS):
        order += [("g", c), ("u", c), ("d", c - 1)]
    order.append(("d", STEPS - 1))
    moe = np.empty((NE, PER, P, CH), np.float32)
    for e in range(NE):
        side = {"g": by_cols(np, a["moe_w_gate"][0, e]), "u": by_cols(np, a["moe_w_up"][0, e]),
                "d": by_rows(np, a["moe_w_down"][0, e])}
        for n, (kind, c) in enumerate(order):
            moe[e, n] = side[kind][c]
    moe = moe.reshape(NE * PER, P, CH)
    o["moe_w"] = moe
    o["moe_router"] = tiles(a["moe_router"][0])

    b = {k[:-2]: v for k, v in a.items() if k.endswith("_2")}
    o["ctx_rows"] = rows_of(np, b["ctx"][0])
    o["c_cols"] = np.stack([col(np, b["c"][0]), col(np, b["c_ctx"])], 2)
    o["ada_w"] = np.concatenate([by_cols(np, b["ada_w"][l]) for l in range(2)])
    ab = b["ada_b"].reshape(2, 6, D)
    o["ada_b_cols"], o["ada_b_gates"] = col(np, ab[:, [0, 1, 3, 4]]), ab[:, [2, 5]].reshape(4, D)
    o["norm_g_cols"], o["norm_g_gates"] = col(np, b["norm_g"]), b["norm_g"][:, [1, 3]].reshape(4, D)
    o["ffn_up"] = np.concatenate([interleave(np, by_cols(np, b["ffn_w_up"][l][:, FC:]), by_cols(np, b["ffn_w_up"][l][:, :FC]))
                                  for l in range(2)])
    o["ffn_down"] = np.concatenate([by_rows(np, b["ffn_w_down"][l]) for l in range(2)])
    o["ffn_conv_w"] = np.moveaxis(col(np, b["ffn_conv_w"]), (0, 1, 2, 3), (1, 0, 3, 2))
    o["ffn_conv_b"] = np.moveaxis(col(np, b["ffn_conv_b"]), 0, 1)
    w = b["ev_w_in"][0]
    rows512 = lambda m: m.reshape(2, 4, P, 512).transpose(0, 2, 1, 3).reshape(2, P, CH)
    o["ev_cols"] = np.concatenate([by_cols(np, w[:, 0:1024]), by_cols(np, w[:, 1536:2560])])
    o["ev_rows"] = np.concatenate([rows512(w[:, n:n + 512]) for n in (1024, 2560, 3072)])
    o["ev_w_gates"], o["ev_gate_b"] = tiles(w[:, 3584:3600]), b["ev_gate_b"][0]
    o["ev_w_out"] = by_rows(np, b["ev_w_out"][0])
    o["ev_conv_w"] = col(np, b["ev_conv_w"][0]).transpose(0, 2, 1)
    o["ev_conv_b"], o["ev_ml_norm_g"] = col(np, b["ev_conv_b"][0]), b["ev_ml_norm_g"][0]
    c = np.arange(64)
    o["rpb"] = b["ev_rpb"][0][:, :, np.clip(c[None, :] - c[:, None], -15, 15) + 15]
    o["od_w_dq"], o["od_w_dkv"] = tiles(b["od_w_dq"][0]), tiles(b["od_w_dkv"][0])
    o["od_norm_g"] = np.concatenate([col(np, b["od_q_norm_g"][0]), col(np, b["od_kv_norm_g"][0])], 1)
    o["od_w_uq"] = b["od_w_uq"][0].reshape(2, P, -1).transpose(1, 0, 2)
    ukv = b["od_w_ukv"][0].reshape(P, 16, 2, 64)
    o["od_w_uk"], o["od_w_uv"] = ukv[:, :, 0].reshape(P, D), ukv[:, :, 1].reshape(P, D)
    o["od_w_o"] = by_rows(np, b["od_w_o"][0])
    return o


def kernel(**inputs):
    import numpy as np
    import concourse.bacc as bacc
    from concourse.bass_utils import run_bass_kernel_spmd as run

    nc = bacc.Bacc("TRN2", target_bir_lowering=False, num_devices=1)
    arrays = {k: np.ascontiguousarray(v) for k, v in lay_out(np, {k: np.asarray(v) for k, v in inputs.items()}).items()}
    aps = {k: nc.dram_tensor(k, v.shape, mybir.dt.from_np(v.dtype), kind="ExternalInput").ap() for k, v in arrays.items()}
    out = nc.dram_tensor("result", (1, T, D), F32, kind="ExternalOutput").ap()
    build(nc, aps, out)
    return run(nc, [arrays], core_ids=[0]).results[0]["result"]
```
